# Optimizing a Trainium2 kernel written in Bass

```python
import jax, jax.numpy as jnp
from jax import lax
import numpy as np
import math

D_MODEL = 1024
BATCH = 1
SEQ = 512
DEPTH = 1

CHUNK = 64
Q_BLOCK = 128
ROPE_THETA = 500000.0
EPS = 1e-6
NEG = -1e30

MLA_HEADS = 8
MLA_Q_LORA = 384
MLA_KV_LORA = 256
MLA_NOPE = 64
MLA_ROPE = 32
MLA_V = 64

DSA_HEADS = 8
DSA_HEAD_DIM = 64
DSA_ROT = DSA_HEAD_DIM // 4
IDX_HEADS = 8
IDX_DIM = 64
IDX_ROT = IDX_DIM // 4
DSA_TOPK_MAX = 256

N_GROUPS = 8
EXPERTS_PER_GROUP = 4
N_EXPERTS = N_GROUPS * EXPERTS_PER_GROUP
EXPERT_FF = 256
TOPK_IN_GROUP = 2

IN_SIZES = (
    MLA_Q_LORA,
    MLA_KV_LORA,
    MLA_ROPE,
    DSA_HEADS * DSA_HEAD_DIM,
    DSA_HEADS * DSA_HEAD_DIM,
    DSA_HEADS * DSA_HEAD_DIM,
    IDX_HEADS * IDX_DIM,
    IDX_DIM,
    IDX_HEADS,
    D_MODEL,
    D_MODEL,
)
IN_WIDTH = sum(IN_SIZES)


def rmsnorm(x, g):
    xf = x.astype(jnp.float32)
    y = xf * lax.rsqrt(jnp.mean(xf * xf, axis=-1, keepdims=True) + EPS)
    return (y * g.astype(jnp.float32)).astype(x.dtype)

def rope(x, pos, rot_dim):
    half = rot_dim // 2
    inv_freq = ROPE_THETA ** (-jnp.arange(half, dtype=jnp.float32) * 2.0 / rot_dim)
    ang = pos.astype(jnp.float32)[:, None] * inv_freq[None, :]
    cos = jnp.cos(ang)[:, None, :]
    sin = jnp.sin(ang)[:, None, :]
    xr = x[..., :rot_dim].astype(jnp.float32)
    x1, x2 = xr[..., :half], xr[..., half:]
    rot = jnp.concatenate([x1 * cos - x2 * sin, x2 * cos + x1 * sin], axis=-1).astype(x.dtype)
    return jnp.concatenate([rot, x[..., rot_dim:]], axis=-1)

def _to_blocks(a):
    b, s = a.shape[0], a.shape[1]
    return a.reshape(b, s // Q_BLOCK, Q_BLOCK, *a.shape[2:]).swapaxes(0, 1)

def _from_blocks(a):
    a = a.swapaxes(0, 1)
    return a.reshape(a.shape[0], a.shape[1] * a.shape[2], *a.shape[3:])

def chunk_causal_attention(q, k, v, scale):
    s_len = q.shape[1]
    nb = s_len // Q_BLOCK
    key_chunk = jnp.arange(s_len) // CHUNK

    def one_block(args):
        qi, bi = args
        q_chunk = (bi * Q_BLOCK + jnp.arange(Q_BLOCK)) // CHUNK
        mask = key_chunk[None, :] <= q_chunk[:, None]
        s = jnp.einsum('bqhd,bkhd->bhqk', qi, k).astype(jnp.float32) * scale
        s = jnp.where(mask[None, None], s, NEG)
        p = jax.nn.softmax(s, axis=-1).astype(v.dtype)
        return jnp.einsum('bhqk,bkhd->bqhd', p, v)

    out = lax.map(one_block, (_to_blocks(q), jnp.arange(nb)))
    return _from_blocks(out)

def indexed_sparse_attention(q, k, v, q_idx, k_idx, w_idx, top_k):
    s_len = q.shape[1]
    nb = s_len // Q_BLOCK
    key_chunk = jnp.arange(s_len) // CHUNK
    gather = jax.vmap(lambda a, i: a[i])

    def one_block(args):
        qi, qii, wi, bi = args
        q_chunk = (bi * Q_BLOCK + jnp.arange(Q_BLOCK)) // CHUNK
        adm = key_chunk[None, :] <= q_chunk[:, None]
        logits = jnp.einsum('bqhd,bkd->bqhk', qii, k_idx).astype(jnp.float32) * (IDX_DIM ** -0.5)
        score = jnp.einsum('bqh,bqhk->bqk', wi.astype(jnp.float32), jax.nn.relu(logits))
        score = jnp.where(adm[None], score, -jnp.inf)
        _, sel = lax.top_k(score, top_k)
        sel_ok = (sel // CHUNK) <= q_chunk[None, :, None]
        k_sel = gather(k, sel)
        v_sel = gather(v, sel)
        s = jnp.einsum('bqhd,bqkhd->bhqk', qi, k_sel).astype(jnp.float32) * (DSA_HEAD_DIM ** -0.5)
        s = jnp.where(sel_ok[:, None], s, NEG)
        p = jax.nn.softmax(s, axis=-1).astype(v.dtype)
        return jnp.einsum('bhqk,bqkhd->bqhd', p, v_sel)

    out = lax.map(one_block, (_to_blocks(q), _to_blocks(q_idx), _to_blocks(w_idx), jnp.arange(nb)))
    return _from_blocks(out)

def hierarchical_moe(h, w_router_group, b_router_group, w_router_expert, b_router_expert,
                     w_gate, w_up, w_down):
    t = h.shape[0]
    group_logits = jnp.matmul(h, w_router_group).astype(jnp.float32) + b_router_group.astype(jnp.float32)
    p_group = jax.nn.softmax(group_logits, axis=-1)
    g_sel = jnp.argmax(group_logits, axis=-1)
    w_grp = jnp.take_along_axis(p_group, g_sel[:, None], axis=-1)
    exp_logits = (jnp.matmul(h, w_router_expert).astype(jnp.float32)
                  + b_router_expert.astype(jnp.float32)).reshape(t, N_GROUPS, EXPERTS_PER_GROUP)
    in_group = jnp.take_along_axis(exp_logits, g_sel[:, None, None], axis=1)[:, 0]
    top_vals, top_idx = lax.top_k(in_group, TOPK_IN_GROUP)
    w_top = jax.nn.softmax(top_vals, axis=-1) * w_grp
    expert_id = g_sel[:, None] * EXPERTS_PER_GROUP + top_idx
    combine = jnp.sum(jax.nn.one_hot(expert_id, N_EXPERTS, dtype=jnp.float32) * w_top[..., None],
                      axis=1).astype(h.dtype)
    out = jnp.zeros_like(h)
    for e in range(N_EXPERTS):
        hid = jax.nn.silu(jnp.matmul(h, w_gate[e])) * jnp.matmul(h, w_up[e])
        out = out + jnp.matmul(hid, w_down[e]) * combine[:, e:e + 1]
    return out

def hybrid_layer(x, pos, norm_mix_g, w_in, mla_q_norm_g, w_uq, mla_kv_norm_g, w_uk, w_uv,
                 w_o_a, w_o_b, w_out, norm_ffn_g, w_router_group, b_router_group,
                 w_router_expert, b_router_expert, w_gate, w_up, w_down):
    b, s, d = x.shape
    h = rmsnorm(x, norm_mix_g)
    proj = jnp.einsum('bsd,de->bse', h, w_in)
    splits = np.cumsum(IN_SIZES)[:-1].tolist()
    (c_q, c_kv, k_r, q_b, k_b, v_b, q_i, k_i, w_i, g_a, g_b) = jnp.split(proj, splits, axis=-1)

    c_q = rmsnorm(c_q, mla_q_norm_g)
    q_a = jnp.einsum('bsr,re->bse', c_q, w_uq).reshape(b, s, MLA_HEADS, MLA_NOPE + MLA_ROPE)
    q_a = jnp.concatenate([q_a[..., :MLA_NOPE], rope(q_a[..., MLA_NOPE:], pos, MLA_ROPE)], axis=-1)
    c_kv = rmsnorm(c_kv, mla_kv_norm_g)
    k_nope = jnp.einsum('bsr,re->bse', c_kv, w_uk).reshape(b, s, MLA_HEADS, MLA_NOPE)
    v_a = jnp.einsum('bsr,re->bse', c_kv, w_uv).reshape(b, s, MLA_HEADS, MLA_V)
    k_pe = rope(k_r[:, :, None, :], pos, MLA_ROPE)
    k_a = jnp.concatenate([k_nope, jnp.broadcast_to(k_pe, (b, s, MLA_HEADS, MLA_ROPE))], axis=-1)
    o_a = chunk_causal_attention(q_a, k_a, v_a, (MLA_NOPE + MLA_ROPE) ** -0.5)
    y_a = jnp.einsum('bse,ed->bsd', o_a.reshape(b, s, MLA_HEADS * MLA_V), w_o_a)

    q_b = rope(q_b.reshape(b, s, DSA_HEADS, DSA_HEAD_DIM), pos, DSA_ROT)
    k_b = rope(k_b.reshape(b, s, DSA_HEADS, DSA_HEAD_DIM), pos, DSA_ROT)
    v_b = v_b.reshape(b, s, DSA_HEADS, DSA_HEAD_DIM)
    q_i = rope(q_i.reshape(b, s, IDX_HEADS, IDX_DIM), pos, IDX_ROT)
    k_i = rope(k_i[:, :, None, :], pos, IDX_ROT)[:, :, 0, :]
    top_k = min(DSA_TOPK_MAX, s // 4)
    o_b = indexed_sparse_attention(q_b, k_b, v_b, q_i, k_i, w_i * (IDX_HEADS ** -0.5), top_k)
    y_b = jnp.einsum('bse,ed->bsd', o_b.reshape(b, s, DSA_HEADS * DSA_HEAD_DIM), w_o_b)

    y = jax.nn.sigmoid(g_a) * y_a + jax.nn.sigmoid(g_b) * y_b
    x = x + jnp.einsum('bsd,de->bse', y, w_out)

    h2 = rmsnorm(x, norm_ffn_g).reshape(b * s, d)
    m = hierarchical_moe(h2, w_router_group, b_router_group, w_router_expert, b_router_expert,
                         w_gate, w_up, w_down)
    return x + m.reshape(b, s, d)

def first_inputs(seed: int = 0) -> dict:
    key = jax.random.key(seed)
    ks = jax.random.split(key, 20)
    f32 = jnp.float32
    L = DEPTH

    def dense(k, shape, fan_in):
        return jax.random.normal(k, shape, f32) * (fan_in ** -0.5)

    def gain(k, shape):
        return 1.0 + 0.05 * jax.random.normal(k, shape, f32)

    return {
        'x': jax.random.normal(ks[0], (BATCH, SEQ, D_MODEL), f32),
        'norm_mix_g': gain(ks[1], (L, D_MODEL)),
        'w_in': dense(ks[2], (L, D_MODEL, IN_WIDTH), D_MODEL),
        'mla_q_norm_g': gain(ks[3], (L, MLA_Q_LORA)),
        'w_uq': dense(ks[4], (L, MLA_Q_LORA, MLA_HEADS * (MLA_NOPE + MLA_ROPE)), MLA_Q_LORA),
        'mla_kv_norm_g': gain(ks[5], (L, MLA_KV_LORA)),
        'w_uk': dense(ks[6], (L, MLA_KV_LORA, MLA_HEADS * MLA_NOPE), MLA_KV_LORA),
        'w_uv': dense(ks[7], (L, MLA_KV_LORA, MLA_HEADS * MLA_V), MLA_KV_LORA),
        'w_o_a': dense(ks[8], (L, MLA_HEADS * MLA_V, D_MODEL), MLA_HEADS * MLA_V),
        'w_o_b': dense(ks[9], (L, DSA_HEADS * DSA_HEAD_DIM, D_MODEL), DSA_HEADS * DSA_HEAD_DIM),
        'w_out': dense(ks[10], (L, D_MODEL, D_MODEL), D_MODEL),
        'norm_ffn_g': gain(ks[11], (L, D_MODEL)),
        'w_router_group': dense(ks[12], (L, D_MODEL, N_GROUPS), D_MODEL),
        'b_router_group': 0.01 * jax.random.normal(ks[13], (L, N_GROUPS), f32),
        'w_router_expert': dense(ks[14], (L, D_MODEL, N_EXPERTS), D_MODEL),
        'b_router_expert': 0.01 * jax.random.normal(ks[15], (L, N_EXPERTS), f32),
        'w_gate': dense(ks[16], (L, N_EXPERTS, D_MODEL, EXPERT_FF), D_MODEL),
        'w_up': dense(ks[17], (L, N_EXPERTS, D_MODEL, EXPERT_FF), D_MODEL),
        'w_down': dense(ks[18], (L, N_EXPERTS, EXPERT_FF, D_MODEL), EXPERT_FF),
        'final_norm_g': gain(ks[19], (D_MODEL,)),
    }

def first_block(x, norm_mix_g, w_in, mla_q_norm_g, w_uq, mla_kv_norm_g, w_uk, w_uv, w_o_a, w_o_b,
              w_out, norm_ffn_g, w_router_group, b_router_group, w_router_expert, b_router_expert,
              w_gate, w_up, w_down, final_norm_g):
    pos = jnp.arange(x.shape[1], dtype=jnp.int32)
    for l in range(DEPTH):
        x = hybrid_layer(x, pos, norm_mix_g[l], w_in[l], mla_q_norm_g[l], w_uq[l], mla_kv_norm_g[l],
                         w_uk[l], w_uv[l], w_o_a[l], w_o_b[l], w_out[l], norm_ffn_g[l],
                         w_router_group[l], b_router_group[l], w_router_expert[l],
                         b_router_expert[l], w_gate[l], w_up[l], w_down[l])
    return rmsnorm(x, final_norm_g)


DEPTH_2 = 2

HEAD_DIM = 128
ROT_DIM = HEAD_DIM // 4
DIL_PAIRS = ((128, 1), (512, 4), (2048, 16))
N_GROUPS_2 = len(DIL_PAIRS)
A_HEADS = D_MODEL // HEAD_DIM
A_WIDTH = A_HEADS * HEAD_DIM
A_QKV = N_GROUPS_2 * A_WIDTH
B_HEADS = D_MODEL // HEAD_DIM
B_KEY = 128
B_VAL = 128
B_WIDTH = B_HEADS * B_VAL
MEM_LEN = 256
MEM_HEADS = 4
MEM_WIDTH = MEM_HEADS * HEAD_DIM
MIX_WIDTH = A_WIDTH + MEM_WIDTH
IN_A = 3 * A_QKV + MEM_WIDTH + MIX_WIDTH
IN_B = 3 * B_HEADS * B_KEY + MEM_WIDTH + MIX_WIDTH
N_A_LAYERS = (DEPTH_2 + 1) // 2
N_B_LAYERS = DEPTH_2 // 2
ATTN_SCALE = 1.0 / math.sqrt(HEAD_DIM)


def rms_norm(x, g):
    xf = x.astype(jnp.float32)
    y = xf * lax.rsqrt(jnp.mean(xf * xf, axis=-1, keepdims=True) + EPS)
    return (y * g.astype(jnp.float32)).astype(x.dtype)

def rotary_tables(positions):
    inv_freq = ROPE_THETA ** (-jnp.arange(0, ROT_DIM, 2, dtype=jnp.float32) / ROT_DIM)
    ang = positions.astype(jnp.float32)[..., None] * inv_freq
    return jnp.cos(ang), jnp.sin(ang)

def apply_partial_rotary(x, cos, sin):
    xf = x.astype(jnp.float32)
    half = ROT_DIM // 2
    x1, x2, rest = xf[..., :half], xf[..., half:ROT_DIM], xf[..., ROT_DIM:]
    out = jnp.concatenate([x1 * cos - x2 * sin, x2 * cos + x1 * sin, rest], axis=-1)
    return out.astype(x.dtype)

def dilated_window_attention(q, k, v, dilation, n_back):
    B, S, H, Dh = q.shape
    span = dilation * n_back
    Sp = -(-S // span) * span
    nb = Sp // span

    def to_blocks(t):
        t = jnp.pad(t, ((0, 0), (0, Sp - S), (0, 0), (0, 0)))
        return t.reshape(B, nb, n_back, dilation, H, Dh).transpose(0, 3, 1, 2, 4, 5)

    qb, kb, vb = to_blocks(q), to_blocks(k), to_blocks(v)
    shift = lambda t: jnp.pad(t, ((0, 0), (0, 0), (1, 0), (0, 0), (0, 0), (0, 0)))[:, :, :-1]
    kc = jnp.concatenate([shift(kb), kb], axis=3)
    vc = jnp.concatenate([shift(vb), vb], axis=3)
    s = jnp.einsum('brcqhd,brckhd->brchqk', qb, kc).astype(jnp.float32) * ATTN_SCALE
    i = jnp.arange(n_back)[:, None]
    j = jnp.arange(2 * n_back)[None, :]
    dist = n_back + i - j
    band = (dist >= 0) & (dist <= n_back)
    c = jnp.arange(nb)[:, None, None]
    valid = band[None] & ((c * n_back + j[None] - n_back) >= 0)
    valid = valid[None, None, :, None]
    s = jnp.where(valid, s, -jnp.inf)
    m = jnp.max(s, axis=-1, keepdims=True)
    p = jnp.exp(s - m)
    den = jnp.sum(p, axis=-1, keepdims=True)
    o = jnp.einsum('brchqk,brckhd->brcqhd', p.astype(v.dtype), vc).astype(jnp.float32)
    o = o / jnp.moveaxis(den, 3, 4)
    lse = (m + jnp.log(den))[..., 0]
    o = o.transpose(0, 2, 3, 1, 4, 5).reshape(B, Sp, H, Dh)[:, :S]
    lse = lse.transpose(0, 2, 4, 1, 3).reshape(B, Sp, H)[:, :S]
    return o, lse

def dilated_mixer(cols, cos, sin, q_gain, k_gain):
    B, S, _ = cols.shape
    qkv = cols.reshape(B, S, 3, N_GROUPS_2, A_HEADS, HEAD_DIM)
    q = rms_norm(qkv[:, :, 0], q_gain[:, None, :])
    k = rms_norm(qkv[:, :, 1], k_gain[:, None, :])
    v = qkv[:, :, 2]
    cos5, sin5 = cos[:, :, None, None, :], sin[:, :, None, None, :]
    q = apply_partial_rotary(q, cos5, sin5)
    k = apply_partial_rotary(k, cos5, sin5)
    outs, lses = [], []
    for g, (window, dil) in enumerate(DIL_PAIRS):
        o, lse = dilated_window_attention(q[:, :, g], k[:, :, g], v[:, :, g], dil, window // dil)
        outs.append(o)
        lses.append(lse)
    alpha = jax.nn.softmax(jnp.stack(lses, axis=0), axis=0)
    o = jnp.sum(alpha[..., None] * jnp.stack(outs, axis=0), axis=0)
    return o.reshape(B, S, A_WIDTH).astype(cols.dtype)

def gla_chunk_scan(q, k, v, log_f):
    B, S, H, dk = q.shape
    dv = v.shape[-1]
    nc = S // CHUNK
    to_c = lambda t: t.reshape(B, nc, CHUNK, H, t.shape[-1]).transpose(1, 0, 3, 2, 4)
    qc, kc, vc = to_c(q), to_c(k), to_c(v)
    G = jnp.cumsum(to_c(log_f), axis=3)
    causal = jnp.tril(jnp.ones((CHUNK, CHUNK), dtype=bool))[..., None]

    def step(state, inp):
        qt, kt, vt, Gt = inp
        o_inter = jnp.einsum('bhtk,bhkv->bhtv', qt * jnp.exp(Gt), state)
        diff = Gt[:, :, :, None, :] - Gt[:, :, None, :, :]
        decay = jnp.where(causal, jnp.exp(jnp.where(causal, diff, 0.0)), 0.0)
        attn = jnp.einsum('bhtk,bhsk,bhtsk->bhts', qt, kt, decay)
        o_intra = jnp.einsum('bhts,bhsv->bhtv', attn, vt)
        g_last = Gt[:, :, -1:, :]
        k_dec = kt * jnp.exp(g_last - Gt)
        new_state = jnp.exp(g_last[:, :, 0, :])[..., None] * state + jnp.einsum('bhsk,bhsv->bhkv', k_dec, vt)
        return new_state, o_inter + o_intra

    init = jnp.zeros((B, H, dk, dv), jnp.float32)
    _, o = lax.scan(step, init, (qc, kc, vc, G))
    return o.transpose(1, 0, 3, 2, 4).reshape(B, S, H, dv)

def hgrn2_mixer(cols, lb, o_gain):
    B, S, _ = cols.shape
    w = B_HEADS * B_KEY
    q = cols[..., :w].astype(jnp.float32)
    f = cols[..., w:2 * w].astype(jnp.float32)
    iv = cols[..., 2 * w:].astype(jnp.float32)
    log_f = jnp.logaddexp(jnp.log(lb), jnp.log1p(-lb) + jax.nn.log_sigmoid(f))
    k = (1.0 - lb) * jax.nn.sigmoid(-f)
    sh = lambda t, d: t.reshape(B, S, B_HEADS, d)
    o = gla_chunk_scan(sh(q, B_KEY), sh(k, B_KEY), sh(iv, B_VAL), sh(log_f, B_KEY))
    o = rms_norm(o, o_gain)
    return o.reshape(B, S, B_WIDTH).astype(cols.dtype)

def memory_cross_attention(q_cols, mem, mem_gain, w_kv, q_gain, k_gain):
    B, S, _ = q_cols.shape
    M = mem.shape[1]
    kv = rms_norm(mem, mem_gain) @ w_kv
    km = rms_norm(kv[..., :MEM_WIDTH].reshape(B, M, MEM_HEADS, HEAD_DIM), k_gain)
    vm = kv[..., MEM_WIDTH:].reshape(B, M, MEM_HEADS, HEAD_DIM)
    qm = rms_norm(q_cols.reshape(B, S, MEM_HEADS, HEAD_DIM), q_gain)
    s = jnp.einsum('bshd,bmhd->bhsm', qm, km).astype(jnp.float32) * ATTN_SCALE
    p = jax.nn.softmax(s, axis=-1)
    o = jnp.einsum('bhsm,bmhd->bshd', p.astype(vm.dtype), vm)
    return o.reshape(B, S, MEM_WIDTH)

def second_inputs(seed: int = 0) -> dict:
    key = jax.random.key(seed)
    ks = jax.random.split(key, 16)
    nrm = lambda k, shape, scale: jax.random.normal(k, shape, jnp.float32) * scale
    gain = lambda k, shape: 1.0 + 0.05 * jax.random.normal(k, shape, jnp.float32)
    x = nrm(ks[0], (BATCH, SEQ, D_MODEL), 1.0)
    mem = nrm(ks[1], (BATCH, MEM_LEN, D_MODEL), 1.0)
    offsets = jax.random.randint(ks[2], (BATCH, 1), 0, 4096, dtype=jnp.int32)
    positions = offsets + jnp.arange(SEQ, dtype=jnp.int32)[None, :]
    return {
        "x": x,
        "mem": mem,
        "positions": positions,
        "norm_gain": gain(ks[3], (DEPTH_2, D_MODEL)),
        "w_in_a": nrm(ks[4], (N_A_LAYERS, D_MODEL, IN_A), D_MODEL ** -0.5),
        "q_gain_a": gain(ks[5], (N_A_LAYERS, N_GROUPS_2, HEAD_DIM)),
        "k_gain_a": gain(ks[6], (N_A_LAYERS, N_GROUPS_2, HEAD_DIM)),
        "w_out_a": nrm(ks[7], (N_A_LAYERS, MIX_WIDTH, D_MODEL), MIX_WIDTH ** -0.5),
        "w_in_b": nrm(ks[8], (N_B_LAYERS, D_MODEL, IN_B), D_MODEL ** -0.5),
        "lb_logits": nrm(ks[9], (DEPTH_2, B_HEADS * B_KEY), 0.5),
        "o_gain_b": gain(ks[10], (N_B_LAYERS, B_VAL)),
        "w_out_b": nrm(ks[11], (N_B_LAYERS, MIX_WIDTH, D_MODEL), MIX_WIDTH ** -0.5),
        "mem_norm_gain": gain(ks[12], (DEPTH_2, D_MODEL)),
        "w_mem_kv": nrm(ks[13], (DEPTH_2, D_MODEL, 2 * MEM_WIDTH), D_MODEL ** -0.5),
        "mem_q_gain": gain(ks[14], (DEPTH_2, HEAD_DIM)),
        "mem_k_gain": gain(ks[15], (DEPTH_2, HEAD_DIM)),
    }

def second_block(x, mem, positions, norm_gain, w_in_a, q_gain_a, k_gain_a, w_out_a,
              w_in_b, lb_logits, o_gain_b, w_out_b, mem_norm_gain, w_mem_kv,
              mem_q_gain, mem_k_gain):
    cos, sin = rotary_tables(positions)
    sm = jax.nn.softmax(lb_logits.astype(jnp.float32), axis=0)
    lower_bounds = jnp.cumsum(sm, axis=0) - sm[0:1]
    for l in range(DEPTH_2):
        j = l // 2
        h = rms_norm(x, norm_gain[l])
        if l % 2 == 0:
            cols = h @ w_in_a[j]
            mix = dilated_mixer(cols[..., :3 * A_QKV], cos, sin, q_gain_a[j], k_gain_a[j])
            q_mem = cols[..., 3 * A_QKV:3 * A_QKV + MEM_WIDTH]
            gate = cols[..., 3 * A_QKV + MEM_WIDTH:]
            w_out = w_out_a[j]
        else:
            cols = h @ w_in_b[j]
            wb = 3 * B_HEADS * B_KEY
            mix = hgrn2_mixer(cols[..., :wb], lower_bounds[l], o_gain_b[j])
            q_mem = cols[..., wb:wb + MEM_WIDTH]
            gate = cols[..., wb + MEM_WIDTH:]
            w_out = w_out_b[j]
        mem_out = memory_cross_attention(q_mem, mem, mem_norm_gain[l], w_mem_kv[l],
                                         mem_q_gain[l], mem_k_gain[l])
        y = jnp.concatenate([mix, mem_out], axis=-1) * jax.nn.silu(gate)
        x = x + y @ w_out
    return x


def setup_inputs(seed=0):
    out = dict(first_inputs(seed))
    for name, value in second_inputs(seed + 1).items():
        if name != "x":
            out[name + "_2"] = value
    return out


def reference(
    x, norm_mix_g, w_in, mla_q_norm_g, w_uq, mla_kv_norm_g, w_uk, w_uv, w_o_a, w_o_b, w_out,
    norm_ffn_g, w_router_group, b_router_group, w_router_expert, b_router_expert, w_gate, w_up,
    w_down, final_norm_g, mem_2, positions_2, norm_gain_2, w_in_a_2, q_gain_a_2, k_gain_a_2,
    w_out_a_2, w_in_b_2, lb_logits_2, o_gain_b_2, w_out_b_2, mem_norm_gain_2, w_mem_kv_2,
    mem_q_gain_2, mem_k_gain_2,
):
    x = first_block(
        x, norm_mix_g, w_in, mla_q_norm_g, w_uq, mla_kv_norm_g, w_uk, w_uv, w_o_a, w_o_b, w_out,
        norm_ffn_g, w_router_group, b_router_group, w_router_expert, b_router_expert, w_gate,
        w_up, w_down, final_norm_g,
    )
    return second_block(
        x, mem_2, positions_2, norm_gain_2, w_in_a_2, q_gain_a_2, k_gain_a_2, w_out_a_2,
        w_in_b_2, lb_logits_2, o_gain_b_2, w_out_b_2, mem_norm_gain_2, w_mem_kv_2, mem_q_gain_2,
        mem_k_gain_2,
    )


_drawn_inputs = setup_inputs


def setup_inputs(seed=0):
    import zlib

    import numpy as np

    out = dict(_drawn_inputs(seed))
    spreads = {}
    factors = {'mla_q_norm_g': 3.529,
     'mla_kv_norm_g': 2.89,
     'b_router_group': 4.009,
     'b_router_expert': 4.466,
     'q_gain_a_2': 8.0,
     'k_gain_a_2': 8.0,
     'mem_norm_gain_2': 8.0,
     'mem_q_gain_2': 8.0,
     'mem_k_gain_2': 8.0,
     'o_gain_b_2': 8.0}
    for name, (base, spread) in spreads.items():
        noise = np.random.default_rng([zlib.crc32(name.encode()), seed]).standard_normal(out[name].shape)
        drawn = base * np.exp(spread * noise) if base else spread * noise
        out[name] = __import__('jax').numpy.asarray(drawn.astype(out[name].dtype))
    for name, factor in factors.items():
        out[name] = (out[name] * factor).astype(out[name].dtype)
    return out
```

```python
from contextlib import ExitStack

import numpy as np

import concourse.bass as bass
from concourse import mybir

F32 = mybir.dt.float32
F32R = mybir.dt.float32r
I32 = mybir.dt.int32
ALU = mybir.AluOpType
ACT = mybir.ActivationFunctionType
AX = mybir.AxisListType

P = 128
T, D = 512, 1024
NT, KD = T // P, D // P
EPS = 1e-6
NEG = -1e30
LOW = -3e38
GONE = -3.4e38
THETA = 500000.0
RAW, SPL = 3, 2
PIECE = 2048
H8 = 8
TOPK = min(256, T // 4)
NGRP, EPG, FF = 8, 4, 256
CAP = 128
DIL = ((128, 1), (512, 4), (2048, 16))
MEM = 256
MH = 4
HD = 128

C_CQ, C_CKV, C_KR, C_QB, C_KB, C_VB, C_QI, C_KI, C_WI, C_GA, C_GB = np.cumsum(
    [0, 384, 256, 32, 512, 512, 512, 512, 64, 8, 1024]).tolist()


def shape_constants():
    parts, at, n = [], {}, 0

    def add(name, a):
        nonlocal n
        a = np.ascontiguousarray(a, np.float32).reshape(P, -1)
        at[name] = (n, a.shape[1])
        parts.append(a)
        n += a.shape[1]

    p = np.arange(P)
    add("ident", np.eye(P))
    chunk_mask = np.where((p[None, :] // 64) <= (p[:, None] // 64), 0.0, NEG)
    add("cmask", np.concatenate([np.zeros((P, 384)), chunk_mask], 1))
    pos = (np.arange(NT)[None, :] * P + p[:, None]).astype(np.float32)
    for name, rot in (("A", 32), ("B", 16)):
        half = rot // 2
        inv = np.float32(THETA) ** (-np.arange(half, dtype=np.float32) * np.float32(2.0) / np.float32(rot))
        ang = pos[:, :, None] * inv.astype(np.float32)[None, None, :]
        add("cos" + name, np.cos(ang))
        add("sin" + name, np.sin(ang))
    add("ones", np.ones((P, P)))
    base_end = n
    add("before", (p[:, None] < p[None, :]).astype(np.float32))
    add("iota_g", np.broadcast_to(np.arange(8), (P, 8)))
    add("iota_s", np.broadcast_to(np.arange(P), (P, P)))
    add("iota_p", p[:, None])
    moe_end = n
    dp = 4 * (p[:, None] - p[None, :])
    add("wmask", np.stack([np.where((dp + d >= 0) & (dp + d <= 128), 0.0, NEG)
                           for d in (3, 2, 1, 0, -1, -2, -3)], 1))
    add("dmask", np.stack([np.where(p[None, :] <= p[:, None], 0.0, NEG),
                           np.where((p[None, :] <= p[:, None]) & ((p[:, None] - p[None, :]) % 4 == 0), 0.0, NEG)], 1))
    inv2 = np.float32(THETA) ** (-np.arange(0, 32, 2, dtype=np.float32) / np.float32(32))
    add("inv2", np.broadcast_to(inv2, (P, 16)))
    dil_end = n
    s, t = p[:, None], p[None, :]
    levels = []
    for half in (1, 2, 4, 8, 16, 32, 64):
        levels.append((s // (2 * half) == t // (2 * half)) & (s // half % 2 == 0) & (t // half % 2 == 1))
    levels.append(s == t)
    add("lmask", np.stack(levels, 1))
    sg = np.ones(T)
    sg[::64] = 0.0
    add("seg", np.broadcast_to(sg, (P, T)))
    return np.concatenate(parts, 1), at, (base_end, moe_end, dil_end, n)


CONST, CAT, (C_BASE, C_MOE, C_DIL, C_ALL) = shape_constants()


def build(nc, A, out):
    ctx = ExitStack()
    with ctx:
        def sb(name, shape, dt=F32):
            return ctx.enter_context(nc.sbuf_tensor(name, shape, dt))

        sems = {}

        def S(name):
            if name not in sems:
                sems[name] = ctx.enter_context(nc.semaphore(name))
            return sems[name]

        wraw = sb("wraw", [P, RAW, PIECE])
        whi = sb("whi", [P, SPL, PIECE], F32R)
        wlo = sb("wlo", [P, SPL, PIECE], F32R)
        AT_hi = sb("AT_hi", [P, 12, T], F32R)
        AT_lo = sb("AT_lo", [P, 12, T], F32R)
        y_hi = sb("y_hi", [P, 1024], F32R)
        y_lo = sb("y_lo", [P, 1024], F32R)
        comb_s = sb("comb_s", [P, NT, 8], F32R)
        small = sb("small", [P, 720])
        flag = sb("flag", [1, 2], I32)
        posi = sb("posi", [P, NT], I32)
        n_arena = 23700
        arena = sb("arena", [P, n_arena])
        pb = ctx.enter_context(nc.psum_tensor("pb", [P, 8, 512], F32))
        ACC = [pb[:, i, :] for i in range(4)]
        TP = [pb[:, 4 + i, :] for i in range(2)]
        SC = [pb[:, 6 + i, :] for i in range(2)]

        x_mid = nc.dram_tensor("x_mid", (T, D), F32, kind="Internal").ap()
        x_mid2 = nc.dram_tensor("x_mid2", (T, D), F32, kind="Internal").ap()

        top = [0]
        marks = {}

        def take(n, *shape, **kw):
            a = top[0]
            top[0] += n
            assert top[0] <= n_arena, (top[0], n_arena)
            return view(a, n, *shape)

        def view(a, n, *shape):
            v = arena[:, a:a + n]
            if len(shape) <= 1:
                return v
            names = "abcd"[:len(shape)]
            return v.rearrange("p (" + " ".join(names) + ") -> p " + " ".join(names),
                               **{k: m for k, m in zip(names, shape)})

        stat_at = [0]

        def stat(n):
            a = stat_at[0]
            stat_at[0] += n
            assert stat_at[0] <= 720
            return small[:, a:a + n]

        base0 = take(C_BASE)

        def const(name, where, first):
            a, n = CAT[name]
            return where[:, a - first:a - first + n]

        ident = const("ident", base0, 0)
        cmask = const("cmask", base0, 0)
        ones = const("ones", base0, 0)
        ropeA = [const(k + "A", base0, 0).rearrange("p (t c) -> p t c", t=NT) for k in ("cos", "sin")]
        ropeB = [const(k + "B", base0, 0).rearrange("p (t c) -> p t c", t=NT) for k in ("cos", "sin")]
        gains = take(64)
        g_mix, g_cq, g_ckv, g_ffn = gains[:, 0:8], gains[:, 8:11], gains[:, 11:13], gains[:, 13:21]
        g_n2 = [gains[:, 21:29], gains[:, 29:37]]
        g_mem = [gains[:, 37:45], gains[:, 45:53]]
        AT_mem_hi, AT_mem_lo = (a[:, 8:12, :].rearrange("p a b -> p (a b)").rearrange("p (k m) -> p k m", k=KD)
                                for a in (AT_hi, AT_lo))
        phase0 = top[0]

        pieces = []
        chunks = []
        CH = {}

        def chunk(name, srcs, n, at, k, per, nt=NT, mem=False):
            first = len(pieces)
            for k0 in range(0, k, per):
                loads, c0 = [], 0
                for s in srcs:
                    w = s.shape[2]
                    loads.append((c0, w, s[:, k0:k0 + per, :]))
                    c0 += w
                assert c0 == n and per * n <= PIECE
                pieces.append((loads, per, n))
            CH[name] = len(chunks)
            chunks.append(dict(first=first, count=k // per, n=n, at=at, per=per, nt=nt, mem=mem))

        def tiled(w):
            return w.rearrange("(k p) n -> p k n", p=P)

        w_in = tiled(A["w_in"][0])
        for i in range(2):
            chunk(f"cqkv{i}", [w_in[:, :, 336 * i:336 * i + 336]], 336, 0, 8, 4)
        w_uq = tiled(A["w_uq"][0])
        for i in range(2):
            chunk(f"uq{i}", [w_uq[:, :, 384 * i:384 * i + 384]], 384, 8, 3, 3)
        chunk("uk", [tiled(A["w_uk"][0])], 512, 8, 2, 2)
        chunk("uv", [tiled(A["w_uv"][0])], 512, 8, 2, 2)
        for i in range(2):
            chunk(f"idx{i}", [w_in[:, :, C_QI + 292 * i:C_QI + 292 * i + 292]], 292, 0, 8, 4)
        for i in range(3):
            chunk(f"qkvb{i}", [w_in[:, :, C_QB + 512 * i:C_QB + 512 * i + 512]], 512, 0, 8, 4)
        for ab, c0, w in (("a", C_GA, "w_o_a"), ("b", C_GB, "w_o_b")):
            for i in range(2):
                chunk(f"g{ab}{i}", [w_in[:, :, c0 + 512 * i:c0 + 512 * i + 512]], 512, 0, 8, 4)
            for i in range(2):
                chunk(f"o{ab}{i}", [tiled(A[w][0])[:, :, 512 * i:512 * i + 512]], 512, 8, 4, 4)
        for i in range(2):
            chunk(f"out{i}", [tiled(A["w_out"][0])[:, :, 512 * i:512 * i + 512]], 512, 0, 8, 4)
        P_MOE = len(pieces)
        EXPERT_ORDER = [("gu", 0), ("gu", 0), ("gu", 1), ("gu", 1), ("dn", 0), ("gu", 2), ("gu", 2),
                        ("dn", 1), ("gu", 3), ("gu", 3), ("dn", 2), ("dn", 3)]
        PPG = len(EXPERT_ORDER)
        for _ in range(NGRP * PPG):
            pieces.append(None)

        def memory_chunks(l):
            w = tiled(A["w_mem_kv_2"][l])
            for i in range(2):
                chunk(f"mkv{l}{i}", [w[:, :, 512 * i:512 * i + 512]], 512, 8, 8, 4, nt=2, mem=True)

        def gate_chunks(l, w, c0, w_out):
            for i in range(3):
                chunk(f"gate{l}{i}", [w[:, :, c0 + 512 * i:c0 + 512 * i + 512]], 512, 0, 8, 4)
            for i in range(2):
                chunk(f"fin{l}{i}", [tiled(w_out)[:, :, 512 * i:512 * i + 512]], 512, 0, 12, 4)

        AQ = 3 * 1024
        w_a = tiled(A["w_in_a_2"][0])
        memory_chunks(0)
        chunk("qm0", [w_a[:, :, 3 * AQ:3 * AQ + 512]], 512, 0, 8, 4)
        for hp in range(4):
            for g in range(3):
                c = 1024 * g + 256 * hp
                chunk(f"qk{hp}{g}", [w_a[:, :, c:c + 256], w_a[:, :, AQ + c:AQ + c + 256]], 512, 0, 8, 4)
            for h in range(2):
                c = 2 * AQ + 256 * hp + 128 * h
                chunk(f"v{hp}{h}", [w_a[:, :, c + 1024 * g:c + 1024 * g + 128] for g in range(3)], 384, 0, 8, 4)
        gate_chunks(0, w_a, 3 * AQ + 512, A["w_out_a_2"][0])
        w_b = tiled(A["w_in_b_2"][0])
        memory_chunks(1)
        chunk("qm1", [w_b[:, :, 3072:3584]], 512, 0, 8, 4)
        for hh in range(2):
            for i, nm in enumerate("qfv"):
                c = 1024 * i + 512 * hh
                chunk(f"{nm}l{hh}", [w_b[:, :, c:c + 512]], 512, 0, 8, 4)
        gate_chunks(1, w_b, 3584, A["w_out_b_2"][0])
        NP = len(pieces)
        bank_uses = [[sum(c["nt"] > t for c in chunks[:j]) for t in range(NT)] for j in range(len(chunks) + 1)]
        readies = [sum(c["nt"] - 1 for c in chunks[:j]) for j in range(len(chunks) + 1)]

        def slot_cols(p):
            return PIECE if pieces[p] is None else pieces[p][1] * pieces[p][2]

        TPU, ntp = {}, [0]

        def tpu(name, n):
            TPU[name] = ntp[0]
            ntp[0] += n

        for name, n in (("n1", 8), ("cq", 3), ("qa", 8), ("ckv", 2), ("ka", 8), ("mla", 32), ("oa", 4),
                        ("qkb", 8), ("qi", 4), ("ki", 1), ("dsa", 32), ("ob", 4), ("y", 8), ("h2", 8)):
            tpu(name, n)
        ntp[0] += ntp[0] % 2
        assert ntp[0] == TPU["h2"] + 8, "an even start keeps the loop's bank parity"
        tpu("moe", 6 * NGRP)
        tpu("n2", 8)

        def mem_units(l):
            for name, n in ((f"mem{l}", 8), (f"km{l}", 4), (f"qm{l}", 4), (f"mat{l}", 16)):
                tpu(name, n)
        mem_units(0)
        for hp in range(4):
            tpu(f"qk{hp}", 12)
            tpu(f"dil{hp}", 16)
        tpu("y0", 12)
        tpu("n3", 8)
        mem_units(1)
        for hh in range(2):
            tpu(f"ql{hh}", 4)
            tpu(f"fl{hh}", 4)
        tpu("y1", 12)
        AU, nau = {}, 0
        for name, n in (("mla", 32), ("dsa", 32), ("mat0", 16), ("dil0", 8), ("dil1", 8), ("dil2", 8),
                        ("dil3", 8), ("mat1", 16)):
            AU[name] = nau
            nau += n

        raw_in = [S(f"raw_in{i}") for i in range(RAW)]
        hi_done, lo_done = S("hi_done"), S("lo_done")
        piece_used = S("piece_used")
        acc_ready = S("acc_ready")
        acc_free = [S(f"acc_free{t}") for t in range(NT)]
        tp_ready = S("tp_ready")
        tp_free = [S(f"tp_free{i}") for i in range(2)]
        act_hi = S("act_hi")
        att_s, att_m, att_p = S("att_s"), S("att_m"), S("att_p")
        att_t, att_r, att_o, att_done = S("att_t"), S("att_r"), S("att_o"), S("att_done")
        phase = S("phase")

        xr = take(4096, NT, D)
        cqkv = view(phase0, 2688, NT, 672)
        top[0] = phase0 + 4096
        qk_tok = take(3072, NT, H8, 96)
        qaT = take(4096, H8, T)
        kaT = take(4096, H8, T)
        v_a = take(2048, NT, 512)
        work = take(3072)
        att_s_sb = [work[:, 0:512], work[:, 512:1024]]
        att_pt = [work[:, 1024:1536], work[:, 1536:2048]]
        o_tok = qk_tok.rearrange("p a b c -> p (a b c)")[:, 0:2048].rearrange("p (t c) -> p t c", t=NT)
        ropetmp = work[:, 0:2048]
        a0 = phase0
        qkvb = view(a0, 6144, NT, 1536)
        idx = view(a0 + 6144, 2336, NT, 584)
        score = view(a0 + 6144, 1536, 3, 512)
        qkbT = view(a0 + 8480, 4096, 8, T)
        qiT = view(a0 + 12576, 2048, 4, T)
        kiT = view(a0 + 14624, 512)
        o_tokb = qkvb[:, :, 0:512]
        y_pos = a0 + 8480 + 4096 + 2048 + 512
        y1 = view(y_pos, 4096, NT, D)
        gb = view(a0 + 8480, 4096, NT, D)
        x1 = view(a0, 4096, NT, D)
        work2 = view(y_pos + 4096, 3072)
        assert y_pos + 4096 + 3072 <= n_arena
        s_sb2 = [work2[:, 0:512], work2[:, 512:1024]]
        pt2 = [work2[:, 1024:1536], work2[:, 1536:2048]]
        rel = [work2[:, 0:512], work2[:, 512:1024]]
        tk = work2[:, 1024:1536]
        kidup = work2[:, 2048:2560].rearrange("p (t c) -> p t c", t=NT)
        ropetmp2 = work2[:, 0:3072]
        wi_s = stat(32).rearrange("p (t h) -> p t h", t=NT)
        max8 = stat(8)

        def norm_cols(n):
            return dict(ss=stat(n), ms=stat(n), rt=stat(n), rs=stat(n))

        ns = {name: norm_cols(4) for name in ("n1", "cq", "ckv", "ffn", "final", "n2", "n3")}
        for l in range(2):
            ns[f"mem{l}"] = norm_cols(2)
            ns[f"km{l}"] = norm_cols(8)
            ns[f"qm{l}"] = norm_cols(16)
        qk_n = norm_cols(16)
        qk_rs = stat(3 * NT * 4).rearrange("p (g t c) -> p g t c", g=3, t=NT)
        gl_n = norm_cols(32)
        att_mx, att_nm, att_l, att_rl = stat(12), stat(4), stat(4), stat(4)

        w_slot = lambda buf, p, i: buf[:, i, 0:slot_cols(p)]

        def mla_unit(i):
            h, qt = i // NT, i % NT
            kw = P * (qt + 1)
            return dict(s=[(0, qaT[0:96, h, qt * P:qt * P + P], kaT[0:96, h, 0:kw], cmask[:, 512 - kw:512], 96 ** -0.5)],
                        kw=kw, v=[v_a[:, b, 64 * h:64 * h + 64] for b in range(qt + 1)],
                        dv=64, o=o_tok[:, qt, 64 * h:64 * h + 64], sb=att_s_sb, pt=att_pt)

        def dsa_unit(i):
            h, qt = i // NT, i % NT
            kw = P * (qt + 1)
            r0 = 64 * (h % 2)
            mask = cmask[:, 384:512] if qt == 0 else score[:, qt - 1, 0:kw]
            return dict(s=[(0, qkbT[r0:r0 + 64, h // 2, qt * P:qt * P + P], qkbT[r0:r0 + 64, 4 + h // 2, 0:kw], mask, 0.125)],
                        kw=kw, v=[qkvb[:, b, 1024 + 64 * h:1088 + 64 * h] for b in range(qt + 1)],
                        dv=64, o=o_tokb[:, qt, 64 * h:64 * h + 64], sb=s_sb2, pt=pt2)

        top[0] = a0 + 4096
        c_moe = take(C_MOE - C_BASE)
        before, iota_g, iota_s, iota_p = (const(k, c_moe, C_BASE) for k in ("before", "iota_g", "iota_s", "iota_p"))
        h2T = take(4096, KD, T)
        w_rt = take(KD * 40, KD, 40)
        b_rt = take(40)
        lg = take(NT * 40, NT, 40)
        rt = take(1200)
        key = take(NT)
        keyb = take(NT * P, NT, P)
        keyrow = take(T)
        comb4 = take(NT * EPG, NT, EPG)
        comb32 = take(NT * 32, NT, 32)
        wslot = take(EPG)
        sg_sb = [take(FF) for _ in range(2)]
        hid_sb = [take(FF) for _ in range(2)]
        fin_g = take(D)
        big = take(4096)
        bigt = big.rearrange("p (t d) -> p t d", t=NT)
        rt_at = [0]

        def route(*shape):
            n = int(np.prod(shape))
            a = rt[:, rt_at[0]:rt_at[0] + n]
            rt_at[0] += n
            assert rt_at[0] <= 1200
            names = "abc"[:len(shape)]
            return a if len(shape) == 1 else a.rearrange("p (" + " ".join(names) + ") -> p " + " ".join(names),
                                                         **dict(zip(names, shape)))

        r_gmax, r_gi, r_m1, r_m2, r_min4, r_d2, r_e2, r_sum, r_w1, r_w2, r_rank, r_over = (route(NT) for _ in range(12))
        r_d, r_e, r_eq, r_cand, oneh = (route(NT, 8) for _ in range(5))
        r_in4, r_in4b, r_eq4, r_cand4, r_oh1, r_oh2 = (route(NT, EPG) for _ in range(6))
        r_el = route(NT, 8, EPG)
        gen_gu = big.rearrange("p (w k f) -> p w k f", w=2, k=KD)
        gen_d = take(2048, 2, D)
        gen_sil = take(1024, 2, T)
        gen_hid = take(1024, 2, T)
        xs_hi = AT_hi[:, 0:8, :].rearrange("p a b -> p (a b)").rearrange("p (t d) -> p t d", t=NT)
        xs_lo = AT_lo[:, 0:8, :].rearrange("p a b -> p (a b)").rearrange("p (t d) -> p t d", t=NT)
        spare_hi = AT_hi[:, 8:12, :].rearrange("p a b -> p (a b)")
        spare_lo = AT_lo[:, 8:12, :].rearrange("p a b -> p (a b)")
        xg_hi = spare_hi[:, 0:1024].rearrange("p (k s) -> p k s", k=KD)
        xg_lo = spare_lo[:, 0:1024].rearrange("p (k s) -> p k s", k=KD)
        hd_hi = [spare_hi[:, 1024 + 256 * i:1280 + 256 * i] for i in range(2)]
        hd_lo = [spare_lo[:, 1024 + 256 * i:1280 + 256 * i] for i in range(2)]
        pick = spare_hi[:, 1536:2048].rearrange("p (t s) -> p t s", t=NT)
        put = spare_lo[:, 1536:2048]
        w_g_e = A["w_gate"][0].rearrange("e (k p) f -> e p k f", p=P)
        w_u_e = A["w_up"][0].rearrange("e (k p) f -> e p k f", p=P)
        w_d_e = A["w_down"][0].rearrange("e (k p) d -> e p k d", p=P)

        top[0] = phase0
        mix = take(6144, NT, 1536)
        l2_0 = top[0]
        memx = take(2048, 2, D)
        km_tok = take(1024, 2, 512)
        vm = take(1024, 2, 512)
        kmT = take(1024, MH, MEM)
        qm_tok = take(2048, NT, 512)
        qmT = take(2048, MH, T)
        mg = take(256)
        mwork = take(2048)
        ms_sb = [mwork[:, 0:256], mwork[:, 256:512]]
        mpt = [mwork[:, 512:768], mwork[:, 768:1024]]
        msq = mwork[:, 1024:1536]
        xn = take(4096, NT, D)
        junkD = km_tok.rearrange("p a b -> p (a b)")
        mjunk = mwork[:, 0:1024]
        top[0] = l2_0
        c_dil = take(C_DIL - C_MOE)
        wmask, dmask, inv2 = (const(k, c_dil, C_MOE) for k in ("wmask", "dmask", "inv2"))
        qkg = take(768, 3, 2, P)
        cos2 = take(64, NT, 16)
        sin2 = take(64, NT, 16)
        qT = take(3072, 3, 2, T)
        kT = take(3072, 3, 2, T)
        v2 = take(3072, NT, 2, 3 * P)
        qk_t = take(2048, NT, 512)
        d_s = [take(768) for _ in range(2)]
        d_pt = [take(768)]
        rtmp = take(768)
        sqb = d_s[0][:, 0:512]
        rot_r, rot_c, rot_a, rot_k = (rtmp[:, 64 * i:64 * i + 64].rearrange("p (t c) -> p t c", t=NT) for i in range(4))
        rot_p = rtmp[:, 256:256 + NT]
        junkE = qk_t.rearrange("p a b -> p (a b)")[:, 0:1024]
        n3x = view(phase0, 4096, NT, D)
        res2 = view(l2_0 + (C_DIL - C_MOE) + 896, 4096, NT, D)
        silu_sb = [d_s[0][:, 0:512], d_s[1][:, 0:512]]
        dil_end = top[0]
        top[0] = l2_0
        c_gla = take(C_ALL - C_DIL)
        lmask, seg = (const(k, c_gla, C_DIL) for k in ("lmask", "seg"))
        lmask = lmask.rearrange("p (l c) -> p l c", c=P)
        og = take(P)
        lbl = take(16, 2, 8)
        lb = take(8)
        lb1 = take(8)
        at_ltok = top[0]
        l_tok = take(2048, NT, 512)
        lA = l_tok.rearrange("p a b -> p (a b)").rearrange("p (s t) -> p s t", s=NT)
        at_lq = top[0]
        lq = take(2048, 4, T)
        lk = take(2048, 4, T)
        lf = take(2048, 4, T)
        lv = take(2048, NT, 512)
        G64 = take(T)
        G512 = take(T)
        lexp = [take(T) for _ in range(2)]
        qe = [take(T) for _ in range(2)]
        ke = [take(T) for _ in range(2)]
        res3 = view(at_lq + 2048, 4096, NT, D)
        lsq = view(at_lq, 2048, 2, D)
        silu3 = [lsq[:, i, 0:512] for i in range(2)]

        def AT_perm(a, k):
            return a[:, k, :].rearrange("p (r t q) -> p t q r", r=4, t=NT)

        def mem_unit(i):
            h, qt = i // NT, i % NT
            return dict(s=[(0, qmT[:, h, qt * P:qt * P + P], kmT[:, h, :], None, HD ** -0.5)], kw=MEM,
                        v=[vm[:, b, P * h:P * h + P] for b in range(2)], dv=P,
                        o=mix[:, qt, 1024 + P * h:1152 + P * h], sb=ms_sb, pt=mpt)

        def dil_unit(hp, i):
            h, r = i // NT, i % NT
            q = lambda g: qT[:, g, h, r * P:r * P + P]
            sc = lambda g: qk_rs[:, g, r, h:h + 1]
            return dict(s=[(0, q(0), kT[:, 0, h, :], wmask[:, (3 - r) * P:(7 - r) * P], sc(0)),
                           (512, q(1), kT[:, 1, h, r * P:r * P + P], dmask[:, 0:P], sc(1)),
                           (640, q(2), kT[:, 2, h, r * P:r * P + P], dmask[:, P:2 * P], sc(2))],
                        kw=768, v=[v2[:, b, h, 0:P] for b in range(4)] + [v2[:, r, h, P:2 * P], v2[:, r, h, 2 * P:3 * P]],
                        dv=P, o=mix[:, r, P * (2 * hp + h):P * (2 * hp + h) + P], sb=d_s, pt=d_pt)


        def scores_out(u, off, n):
            return SC[u % 2][:, off:off + n] if off < 512 else ACC[u % 2][:, off - 512:off - 512 + n]

        block = ctx.enter_context(nc.Block())

        @block.sync
        def _(sp):
            for t in range(NT):
                sp.dma_start(xr[:, t, :], A["x"][0, t * P:t * P + P, :]).then_inc(S(f"x_in{t}"), 16)

            def load(p):
                loads, per, n = pieces[p]
                if p >= RAW:
                    sp.wait_ge(lo_done, p - RAW + 1)
                dst = wraw[:, p % RAW, 0:per * n].rearrange("p (k n) -> p k n", k=per)
                share = 96 // len(loads)
                for c0, w, src in loads:
                    sp.dma_start(dst[:, :, c0:c0 + w], src).then_inc(raw_in[p % RAW], share)

            for p in range(P_MOE):
                load(p)
            with sp.Fori(0, NGRP) as g:
                for j, (kind, e) in enumerate(EXPERT_ORDER):
                    p = P_MOE + j
                    half = EXPERT_ORDER[:j].count((kind, e))
                    ex = sp.snap(g * EPG + e)
                    sp.wait_ge(lo_done, g * PPG + (p - RAW + 1))
                    if kind == "gu":
                        dst = wraw[:, p % RAW, :].rearrange("p (k n) -> p k n", k=4)
                        for i, w in enumerate((w_g_e, w_u_e)):
                            sp.dma_start(dst[:, :, FF * i:FF * i + FF],
                                         w[bass.ds(ex, 1), :, 4 * half:4 * half + 4, :].rearrange("e p k f -> p (e k) f")
                                         ).then_inc(raw_in[p % RAW], 48)
                    else:
                        sp.dma_start(wraw[:, p % RAW, :].rearrange("p (k n) -> p k n", k=2),
                                     w_d_e[bass.ds(ex, 1), :, :, :].rearrange("e p k f -> p (e k) f")
                                     ).then_inc(raw_in[p % RAW], 96)
            for p in range(P_MOE + NGRP * PPG, NP):
                load(p)

        NORMS = (("n1", 4, 4, 0), ("cq", 4, 4, 0), ("ckv", 4, 4, 0), ("ffn", 4, 4, 0), ("final", 4, 0, 0), ("n2", 4, 4, 0),
                 ("mem0", 2, 2, 0), ("km0", 0, 8, 2), ("qm0", 0, 16, 4), ("n3", 4, 4, 0), ("mem1", 2, 2, 0), ("km1", 0, 8, 2),
                 ("qm1", 0, 16, 4))
        ORDER = [n[0] for n in NORMS]
        norm_ss, norm_ms, norm_rt, norm_xs = S("norm_ss"), S("norm_ms"), S("norm_rt"), S("norm_xs")
        head_sq, head_red = S("head_sq"), S("head_red")

        def so_far(name, what, n):
            return sum(row[what] for row in NORMS[:ORDER.index(name)]) + n

        def wait_acc(eng, j, t):
            c = chunks[j]
            if t == c["nt"] - 1:
                eng.wait_ge(piece_used, c["first"] + c["count"])
            else:
                eng.wait_ge(acc_ready, readies[j] + t + 1)

        def wait_tp_read(eng, name, n):
            for par in range(2):
                last = max(u for u in range(TPU[name], TPU[name] + n) if u % 2 == par) if n > 1 or TPU[name] % 2 == par else None
                if last is not None:
                    eng.wait_ge(tp_free[par], last // 2 + 1)

        def wait_read(eng, name, t):
            eng.wait_ge(acc_free[t], bank_uses[CH[name]][t] + 1)

        phases = {"PE": 0, "ACT": 0, "DVE": 0, "POOL": 0}

        def end_phase(eng, who):
            phases[who] += 1
            eng.drain().then_inc(phase, 1)
            eng.wait_ge(phase, 4 * phases[who])

        @block.gpsimd
        def _(pool):
            chain = [0]

            def link(ins):
                chain[0] += 1
                ins.then_inc(S("pool_step"), 1)
                pool.wait_ge(S("pool_step"), chain[0])

            def rope(x1, x2, cos, sin, tmp, shape):
                n = int(np.prod(shape))
                v = [tmp[:, i * n:i * n + n].rearrange("p (t h c) -> p t h c", t=shape[0], h=shape[1]) for i in range(4)]
                bc = lambda a: a.unsqueeze(2).broadcast_to([P] + list(shape))
                c, s = bc(cos), bc(sin)
                pool.tensor_tensor(v[0], x1, c, ALU.mult)
                pool.tensor_tensor(v[1], x2, s, ALU.mult)
                pool.tensor_tensor(v[2], x2, c, ALU.mult)
                link(pool.tensor_tensor(v[3], x1, s, ALU.mult))
                pool.tensor_tensor(x1, v[0], v[1], ALU.subtract)
                return pool.tensor_tensor(x2, v[2], v[3], ALU.add)

            pool.wait_ge(S("consts"), 16)

            def load_memory(l):
                pool.dma_start(memx, A["mem_2"][0].rearrange("(t p) d -> p t d", p=P)).then_inc(S(f"memx{l}"), 16)
                for i, w in enumerate(("mem_q_gain_2", "mem_k_gain_2")):
                    pool.dma_start(mg[:, P * i:P * i + P], A[w][l:l + 1, :].broadcast_to([P, P])).then_inc(S(f"memx{l}"), 16)

            for i in range(2):
                for t in range(NT):
                    wait_read(pool, f"uq{i}", t)
                q = qk_tok[:, :, 4 * i:4 * i + 4, :]
                for t in range(NT):
                    r = rope(q[:, t:t + 1, :, 64:80], q[:, t:t + 1, :, 80:96], ropeA[0][:, t:t + 1], ropeA[1][:, t:t + 1],
                             ropetmp[:, 256 * t:256 * t + 256], (1, 4, 16))
                r.then_inc(S("qa_rot"), 1)
            kr = cqkv[:, :, 640:672].unsqueeze(2)
            link(rope(kr[:, :, :, 0:16], kr[:, :, :, 16:32], ropeA[0], ropeA[1], ropetmp[:, 1024:1280], (NT, 1, 16)))
            wait_tp_read(pool, "qa", 8)
            for t in range(NT):
                pool.tensor_copy(qk_tok[:, t, :, 64:96],
                                 kr[:, t, :, :].broadcast_to([P, H8, 32])).then_inc(S("ka_rot"), 1)
            end_phase(pool, "POOL")

            for tok, n, last in ((idx, 9, "idx1"), (qkvb, 16, "qkvb2")):
                for t in range(NT):
                    wait_read(pool, last, t)
                x = tok[:, :, 0:64 * n].rearrange("p t (h c) -> p t h c", h=n)
                for t in range(NT):
                    r = rope(x[:, t:t + 1, :, 0:8], x[:, t:t + 1, :, 8:16], ropeB[0][:, t:t + 1], ropeB[1][:, t:t + 1],
                             ropetmp2[:, 512 * t:512 * t + 512], (1, n, 8))
                link(r)
                if tok is idx:
                    for half in range(2):
                        pool.tensor_copy(kidup[:, :, 64 * half:64 * half + 64], idx[:, :, 512:576])
                    r = pool.tensor_scalar(wi_s, idx[:, :, 576:584], H8 ** -0.5, None, ALU.mult)
                else:
                    r = pool.nop()
                r.then_inc(S("b_rot"), 1)
            wait_tp_read(pool, "ob", 4)
            pool.dma_start(x1, A["x"][0].rearrange("(t p) d -> p t d", p=P)).then_inc(S("res1"), 16)
            pool.wait_ge(S("res1"), 16)
            end_phase(pool, "POOL")

            pool.dma_start(c_moe, A["const"][:, C_BASE:C_MOE]).then_inc(S("moe_in"), 16)
            pool.dma_start(w_rt[:, :, 0:8], tiled(A["w_router_group"][0])).then_inc(S("moe_in"), 16)
            pool.dma_start(w_rt[:, :, 8:40], tiled(A["w_router_expert"][0])).then_inc(S("moe_in"), 16)
            pool.dma_start(b_rt[:, 0:8], A["b_router_group"][0:1, :].broadcast_to([P, 8])).then_inc(S("moe_in"), 16)
            pool.dma_start(b_rt[:, 8:40], A["b_router_expert"][0:1, :].broadcast_to([P, 32])).then_inc(S("moe_in"), 16)
            pool.dma_start(fin_g, A["final_norm_g"].unsqueeze(0).broadcast_to([P, D])).then_inc(S("moe_in"), 16)
            pool.wait_ge(S("moe_in"), 96)
            pool.wait_ge(S("flag_in"), 1)
            pool.wait_ge(S("moe_end"), 1)
            with pool.If(pool.value_load(flag[0:1, 0:1], min_val=0, max_val=T) > 0):
                with pool.Fori(0, NGRP * EPG) as e:
                    one = bass.ds(e, 1)
                    pool.wait_ge(S("gen_y"), e * 8 + 8)
                    pool.dma_start(gen_gu[:, 0, :, :], w_g_e[one].rearrange("e p k f -> p (e k) f")).then_inc(S("gen_in"), 16)
                    pool.dma_start(gen_gu[:, 1, :, :], w_u_e[one].rearrange("e p k f -> p (e k) f")).then_inc(S("gen_in"), 16)
                    pool.dma_start(gen_d, w_d_e[one].rearrange("e p k f -> p (e k) f")).then_inc(S("gen_in"), 16)
            end_phase(pool, "POOL")

            load_memory(0)
            for t in range(NT):
                pool.wait_ge(S("fin_x"), t + 1)
                pool.dma_start(x_mid[t * P:t * P + P, :], xn[:, t, :]).then_inc(S("mid_out"), 16)
            pool.wait_ge(S("mid_out"), 16 * NT)
            end_phase(pool, "POOL")

            pool.dma_start(c_dil, A["const"][:, C_MOE:C_DIL]).then_inc(S("dil_in"), 16)
            for i, w in enumerate(("q_gain_a_2", "k_gain_a_2")):
                pool.dma_start(qkg[:, :, i, :], A[w][0:1].broadcast_to([P, 3, P])).then_inc(S("dil_in"), 16)
            pool.dma_start(posi[:, :], A["positions_2"].rearrange("o (p r) -> (o p) r", r=4)).then_inc(S("dil_in"), 16)
            pool.wait_ge(S("rot2"), 1)
            for n in range(12):
                pool.wait_ge(S("qk_rs"), n + 1)
                for t in range(NT):
                    k = qk_t[:, t, 256:512].rearrange("p (h c) -> p h c", h=2)
                    r = pool.tensor_tensor(k, k, qk_rs[:, n % 3, t, 2:4].unsqueeze(2).broadcast_to([P, 2, P]), ALU.mult)
                link(r)
                for t in range(NT):
                    x = qk_t[:, t:t + 1, :].rearrange("p t (h c) -> p t h c", h=4)
                    r = rope(x[:, :, :, 0:16], x[:, :, :, 16:32], cos2[:, t:t + 1], sin2[:, t:t + 1],
                             rtmp[:, 256 * (t % 3):256 * (t % 3) + 256], (1, 4, 16))
                r.then_inc(S("qk_rot"), 1)
            end_phase(pool, "POOL")
            for r in range(NT):
                pool.dma_start(res2[:, r, :], x_mid.rearrange("(p r) d -> r p d", r=4)[r]).then_inc(S("res2"), 16)
            for r in range(NT):
                wait_read(pool, "fin01", r)
                pool.dma_start(x_mid2.rearrange("(p r) d -> r p d", r=4)[r], res2[:, r, :]).then_inc(S("mid_out2"), 16)
            pool.wait_ge(S("mid_out2"), 16 * NT)
            end_phase(pool, "POOL")

            load_memory(1)
            end_phase(pool, "POOL")

            pool.dma_start(c_gla, A["const"][:, C_DIL:C_ALL]).then_inc(S("gla_in"), 16)
            pool.dma_start(og, A["o_gain_b_2"][0:1, :].broadcast_to([P, P])).then_inc(S("gla_in"), 16)
            with nc.allow_non_contiguous_dma(reason="a column of lower bounds for each head"):
                for i in range(2):
                    pool.dma_start(lbl[:, i, :], A["lb_logits_2"][i].rearrange("(h c) -> c h", c=P)).then_inc(S("gla_in"), 16)
            for b in qe + ke:
                r = pool.memset(b, 0.0)
            r.then_inc(S("gla_zero"), 1)
            for hh in range(2):
                wait_tp_read(pool, f"fl{hh}", 4)
                pool.memset(lA, 0.0).then_inc(S("lA_zero"), 1)
            end_phase(pool, "POOL")
            pool.dma_start(res3, x_mid2.rearrange("(t p) d -> p t d", p=P)).then_inc(S("res3"), 16)
            for t in range(NT):
                wait_read(pool, "fin11", t)
                pool.dma_start(out[0, t * P:t * P + P, :], res3[:, t, :]).then_inc(S("out_done"), 16)
            pool.wait_ge(S("out_done"), 16 * NT)

        @block.scalar
        def _(act):
            his = [0]

            def feed(p):
                if p >= NP:
                    return
                act.wait_ge(raw_in[p % RAW], 96 * (p // RAW + 1))
                if p >= SPL:
                    act.wait_ge(piece_used, p - SPL + 1)
                act.activation(w_slot(whi, p, p % SPL), w_slot(wraw, p, p % RAW), ACT.Copy).then_inc(hi_done, 1)

            def during(j):
                for i in range(chunks[j]["count"] - 1):
                    feed(chunks[j]["first"] + i + SPL)

            def after(j):
                feed(chunks[j]["first"] + chunks[j]["count"] - 1 + SPL)

            def evac(name, dst, func=ACT.Copy, scale=1.0):
                j = CH[name]
                during(j)
                for t in range(chunks[j]["nt"]):
                    wait_acc(act, j, t)
                    src = ACC[t][:, 0:chunks[j]["n"]]
                    d = dst(t)
                    if len(d.shape) == 3:
                        src = src.rearrange("p (h c) -> p h c", h=d.shape[1])
                    act.activation(d, src, func, scale=scale).then_inc(acc_free[t], 1)
                after(j)

            def hi(name, i, dst, src, gain=None):
                act.wait_ge(tp_ready, TPU[name] + i + 1)
                act.activation(dst, src, ACT.Copy, scale=1.0 if gain is None else gain).then_inc(act_hi, 1)

            def tcopy(name, i, dst, src, scale=1.0):
                u = TPU[name] + i
                act.wait_ge(tp_ready, u + 1)
                act.activation(dst, src, ACT.Copy, scale=scale).then_inc(tp_free[u % 2], 1)

            def tb(name, i):
                return TP[(TPU[name] + i) % 2]

            def sumsq(src, junk, ss, name, t):
                if t:
                    act.wait_ge(norm_ss, so_far(name, 1, t))
                act.activation(junk, src, ACT.Square, accum_out=ss).then_inc(norm_ss, 1)

            def root(name, c):
                act.wait_ge(norm_ms, ORDER.index(name) + 1)
                act.activation(c["rt"], c["ms"], ACT.Sqrt).then_inc(norm_rt, 1)

            def attention(name, unit, n):
                U0 = AU[name]

                def out_of_psum(i):
                    u = unit(i)
                    U = U0 + i
                    act.wait_ge(att_o, U + 1)
                    act.wait_ge(att_r, U + 1)
                    act.activation(u["o"], SC[U % 2][:, 0:u["dv"]], ACT.Copy, scale=att_rl[:, U % 4:U % 4 + 1]
                                   ).then_inc(att_done, 1)

                for i in range(n):
                    u = unit(i)
                    U = U0 + i
                    act.wait_ge(att_m, U + 1)
                    masked = u["s"][0][3] is not None
                    src = u["sb"][U % 2][:, 0:u["kw"]] if masked else SC[U % 2][:, 0:u["kw"]]
                    act.activation(u["sb"][U % 2][:, 0:u["kw"]], src, ACT.Exp, bias=att_nm[:, U % 4:U % 4 + 1],
                                   scale=1.0 if masked else u["s"][0][4],
                                   accum_out=att_l[:, U % 4:U % 4 + 1]).then_inc(att_p, 1)
                    if i:
                        out_of_psum(i - 1)
                out_of_psum(n - 1)

            def head_norm(name, chunk, tok, nt, dst, sq):
                for t in range(nt):
                    if t:
                        act.wait_ge(head_red, so_far(name, 3, t))
                    wait_read(act, chunk, t)
                    act.activation(sq, tok[:, t, :], ACT.Square).then_inc(head_sq, 1)
                root(name, dst)

            def memory_stage(l):
                act.wait_ge(S(f"memx{l}"), 48)
                for t in range(2):
                    sumsq(memx[:, t, :], mjunk, ns[f"mem{l}"]["ss"][:, t:t + 1], f"mem{l}", t)
                root(f"mem{l}", ns[f"mem{l}"])
                for k in range(KD):
                    hi(f"mem{l}", k, AT_mem_hi[:, k, :], tb(f"mem{l}", k)[:, 0:MEM], g_mem[l][:, k:k + 1])
                evac(f"mkv{l}0", lambda t: km_tok[:, t, :])
                head_norm(f"km{l}", f"mkv{l}0", km_tok, 2, ns[f"km{l}"], msq)
                evac(f"mkv{l}1", lambda t: vm[:, t, :])
                for h in range(MH):
                    tcopy(f"km{l}", h, kmT[:, h, :], tb(f"km{l}", h)[:, 0:MEM])
                evac(f"qm{l}", lambda t: qm_tok[:, t, :])
                head_norm(f"qm{l}", f"qm{l}", qm_tok, NT, ns[f"qm{l}"], msq)
                for h in range(MH):
                    tcopy(f"qm{l}", h, qmT[:, h, :], tb(f"qm{l}", h))
                attention(f"mat{l}", mem_unit, 16)

            def gates(l, tmp):
                for i in range(3):
                    j = CH[f"gate{l}{i}"]
                    during(j)
                    for t in range(NT):
                        n = NT * i + t
                        wait_acc(act, j, t)
                        if n >= 2:
                            act.wait_ge(S(f"gated{l}"), n - 1)
                        act.activation(tmp[n % 2], ACC[t][:, :], ACT.Silu).then_inc(acc_free[t], 1)
                    after(j)
                act.wait_ge(piece_used, chunks[CH[f"gate{l}2"]]["first"] + 2)
                for k in range(12):
                    hi(f"y{l}", k, AT_hi[:, k, :], tb(f"y{l}", k))
                for i in range(2):
                    j = CH[f"fin{l}{i}"]
                    during(j)
                    after(j)

            act.dma_start(base0, A["const"][:, 0:C_BASE]).then_inc(S("consts"), 16)
            with nc.allow_non_contiguous_dma(reason="gains as columns"):
                for dst, src in ((g_mix, A["norm_mix_g"][0]), (g_cq, A["mla_q_norm_g"][0]), (g_ckv, A["mla_kv_norm_g"][0]),
                                 (g_ffn, A["norm_ffn_g"][0]), (g_n2[0], A["norm_gain_2"][0]), (g_n2[1], A["norm_gain_2"][1]),
                                 (g_mem[0], A["mem_norm_gain_2"][0]), (g_mem[1], A["mem_norm_gain_2"][1])):
                    act.dma_start(dst, src.rearrange("(k p) -> p k", p=P)).then_inc(S("gains_in"), 16)
            feed(0)
            feed(1)
            for t in range(NT):
                act.wait_ge(S(f"x_in{t}"), 16)
                sumsq(xr[:, t, :], work[:, 0:1024], ns["n1"]["ss"][:, t:t + 1], "n1", t)
            root("n1", ns["n1"])
            act.wait_ge(S("gains_in"), 128)
            for k in range(KD):
                hi("n1", k, AT_hi[:, k, :], tb("n1", k), g_mix[:, k:k + 1])
            for i in range(2):
                evac(f"cqkv{i}", lambda t: cqkv[:, t, 336 * i:336 * i + 336])
            for name, c0, w in (("cq", 0, 384), ("ckv", 384, 256)):
                for t in range(NT):
                    act.wait_ge(acc_free[t], 2)
                    sumsq(cqkv[:, t, c0:c0 + w], work[:, 0:w], ns[name]["ss"][:, t:t + 1], name, t)
                root(name, ns[name])
            for k in range(3):
                hi("cq", k, AT_hi[:, 8 + k, :], tb("cq", k), g_cq[:, k:k + 1])
            for i in range(2):
                evac(f"uq{i}", lambda t: qk_tok[:, t, 4 * i:4 * i + 4, :])
            for h in range(H8):
                tcopy("qa", h, qaT[0:96, h, :], tb("qa", h)[0:96, :])
            act.wait_ge(piece_used, chunks[CH["uq1"]]["first"] + 1)
            for k in range(2):
                hi("ckv", k, AT_hi[:, 8 + k, :], tb("ckv", k), g_ckv[:, k:k + 1])
            evac("uk", lambda t: qk_tok[:, t, :, 0:64])
            evac("uv", lambda t: v_a[:, t, :])
            for h in range(H8):
                tcopy("ka", h, kaT[0:96, h, :], tb("ka", h)[0:96, :])
            attention("mla", mla_unit, 32)
            for k in range(4):
                hi("oa", k, AT_hi[:, 8 + k, :], tb("oa", k))
            end_phase(act, "ACT")

            for name, tok, c0 in (("idx0", idx, 0), ("idx1", idx, 292), ("qkvb0", qkvb, 0), ("qkvb1", qkvb, 512),
                                  ("qkvb2", qkvb, 1024)):
                evac(name, lambda t: tok[:, t, c0:c0 + chunks[CH[name]]["n"]])
            for i in range(2):
                evac(f"ga{i}", lambda t: y1[:, t, 512 * i:512 * i + 512], ACT.Sigmoid)
            for i in range(2):
                during(CH[f"oa{i}"])
                after(CH[f"oa{i}"])
            for i in range(8):
                tcopy("qkb", i, qkbT[:, i, :], tb("qkb", i))
            for i in range(4):
                tcopy("qi", i, qiT[:, i, :], tb("qi", i))
            tcopy("ki", 0, kiT, tb("ki", 0))
            for n in range(24):
                kw = P * (n // 8 + 2)
                act.wait_ge(S("idx_mm"), n + 1)
                if n >= 2:
                    act.wait_ge(S("idx_add"), n - 1)
                act.activation(rel[n % 2][:, 0:kw], SC[n % 2][:, 0:kw], ACT.Relu, scale=0.125).then_inc(S("idx_relu"), 1)
            attention("dsa", dsa_unit, 32)
            for i in range(2):
                evac(f"gb{i}", lambda t: gb[:, t, 512 * i:512 * i + 512], ACT.Sigmoid)
            act.wait_ge(piece_used, chunks[CH["oa1"]]["first"] + 1)
            for k in range(4):
                hi("ob", k, AT_hi[:, 8 + k, :], tb("ob", k))
            for i in range(2):
                during(CH[f"ob{i}"])
                after(CH[f"ob{i}"])
            act.wait_ge(piece_used, chunks[CH["gb1"]]["first"] + 2)
            for k in range(KD):
                hi("y", k, AT_hi[:, k, :], tb("y", k))
            for i in range(2):
                during(CH[f"out{i}"])
                after(CH[f"out{i}"])
            end_phase(act, "ACT")

            for t in range(NT):
                sumsq(x1[:, t, :], big[:, 0:1024], ns["ffn"]["ss"][:, t:t + 1], "ffn", t)
            root("ffn", ns["ffn"])
            for t in range(NT):
                act.wait_ge(norm_xs, so_far("ffn", 2, t + 1))
                act.activation(xs_hi[:, t, :], bigt[:, t, :], ACT.Copy).then_inc(S("xs_hi"), 1)
            for k in range(KD):
                tcopy("h2", k, h2T[:, k, :], tb("h2", k), g_ffn[:, k:k + 1])
            act.wait_ge(S("rt_exp"), 1)
            act.activation(r_e, r_d, ACT.Exp).then_inc(S("rt_exp_done"), 1)
            act.wait_ge(S("rt_exp"), 2)
            act.activation(r_e2, r_d2, ACT.Exp).then_inc(S("rt_exp_done"), 1)
            act.wait_ge(S("rt_comb"), 1)
            act.activation(comb_s[:, :, 0:4], comb4, ACT.Copy).then_inc(S("comb_hi"), 1)
            act.wait_ge(S("key_mm"), 1)
            act.activation(keyrow, ACC[2], ACT.Copy).then_inc(S("key_row"), 1)
            with act.Fori(0, NGRP) as g:
                def feed_in(j):
                    p = P_MOE + j + SPL
                    act.wait_ge(raw_in[p % RAW], g * (96 * PPG // RAW) + 96 * (p // RAW + 1))
                    act.wait_ge(piece_used, g * PPG + (P_MOE + j + 1))
                    act.activation(whi[:, p % SPL, :], wraw[:, p % RAW, :], ACT.Copy).then_inc(hi_done, 1)

                def hi_in(i, pairs):
                    u = TPU["moe"] + i
                    act.wait_ge(tp_ready, g * 6 + (u + 1))
                    for n, (dst, src, gain) in enumerate(pairs):
                        r = act.activation(dst, src, ACT.Copy, scale=gain)
                    r.then_inc(act_hi, 1)

                def silu(e):
                    last = max(j for j, pe_ in enumerate(EXPERT_ORDER) if pe_ == ("gu", e))
                    act.wait_ge(piece_used, g * PPG + (P_MOE + last + 1))
                    act.wait_ge(S("hid_done"), g * EPG + (e + 1))
                    act.activation(sg_sb[e % 2], ACC[e % 2][:, 0:FF], ACT.Silu).then_inc(S("silu"), 1)
                    hi_in(2 + e, [(hd_hi[e % 2], TP[e % 2][:, 0:2 * P], 1.0)])

                for i in range(2):
                    hi_in(i, [(xg_hi[:, 4 * i + k, :], TP[i][:, k * P:k * P + P], g_ffn[:, 4 * i + k:4 * i + k + 1])
                              for k in range(4)])
                feed_in(0)
                feed_in(1)
                silu(0)
                feed_in(2)
                feed_in(3)
                silu(1)
                for j in (4, 5, 6):
                    feed_in(j)
                silu(2)
                for j in (7, 8, 9):
                    feed_in(j)
                silu(3)
                feed_in(10)
                feed_in(11)
                act.wait_ge(S("sc_ready"), g * 8 + 1)
                for n in range(2):
                    act.activation(y_hi[:, 512 * n:512 * n + 512], ACC[2 + n], ACT.Copy).then_inc(S("y_hi"), 1)
            act.wait_ge(S("flag_in"), 1)
            with act.If(act.value_load(flag[0:1, 0:1], min_val=0, max_val=T) > 0):
                with act.Fori(0, NGRP * EPG) as e:
                    act.wait_ge(S("gen_gu"), e + 1)
                    act.wait_ge(S("gen_hid"), e + 1)
                    act.activation(gen_sil[:, 0, :], ACC[0], ACT.Silu)
                    act.activation(gen_sil[:, 1, :], ACC[1], ACT.Silu).then_inc(S("gen_silu"), 1)
            end_phase(act, "ACT")

            for t in range(NT):
                sumsq(x1[:, t, :], junkD, ns["final"]["ss"][:, t:t + 1], "final", t)
            root("final", ns["final"])
            for t in range(NT):
                act.wait_ge(S("fin_x"), t + 1)
                sumsq(xn[:, t, :], junkD, ns["n2"]["ss"][:, t:t + 1], "n2", t)
            root("n2", ns["n2"])
            for k in range(KD):
                hi("n2", k, AT_perm(AT_hi, k), tb("n2", k).rearrange("p (t q r) -> p t q r", t=NT, r=4), g_n2[0][:, k:k + 1])
            memory_stage(0)
            end_phase(act, "ACT")

            act.wait_ge(S("rot_ang"), 1)
            act.activation(sin2, rot_r, ACT.Sin)
            act.activation(cos2, rot_c, ACT.Sin).then_inc(S("rot2"), 1)
            for hp in range(4):
                for g in range(3):
                    n = 3 * hp + g
                    j = CH[f"qk{hp}{g}"]
                    during(j)
                    for t in range(NT):
                        wait_acc(act, j, t)
                        if t or n:
                            act.wait_ge(S("qk_red"), NT * n + t)
                        act.activation(sqb, ACC[t][:, :], ACT.Square).then_inc(S("qk_sq"), 1)
                    after(j)
                    act.wait_ge(S("qk_ms"), n + 1)
                    act.activation(qk_n["rt"], qk_n["ms"], ACT.Sqrt).then_inc(S("qk_rt"), 1)
                    for i in range(4):
                        tcopy(f"qk{hp}", 4 * g + i, (qT if i < 2 else kT)[:, g, i % 2, :], tb(f"qk{hp}", 4 * g + i))
                for h in range(2):
                    evac(f"v{hp}{h}", lambda t: v2[:, t, h, :])
                attention(f"dil{hp}", lambda i: dil_unit(hp, i), 8)
            end_phase(act, "ACT")
            gates(0, silu_sb)
            for t in range(NT):
                wait_read(act, "fin01", t)
                sumsq(res2[:, t, :], junkE, ns["n3"]["ss"][:, t:t + 1], "n3", t)
            root("n3", ns["n3"])
            act.wait_ge(piece_used, chunks[CH["fin01"]]["first"] + 3)
            for k in range(KD):
                hi("n3", k, AT_hi[:, k, :].rearrange("p (q r) -> p r q", r=4),
                   tb("n3", k).rearrange("p (r q) -> p r q", r=4), g_n2[1][:, k:k + 1])
            end_phase(act, "ACT")
            memory_stage(1)
            end_phase(act, "ACT")

            act.wait_ge(S("lb_in"), 1)
            act.activation(lb, lbl[:, 1, :], ACT.Sigmoid)
            act.activation(lb1, lbl[:, 1, :], ACT.Sigmoid, scale=-1.0).then_inc(S("lb_ready"), 1)
            for hh in range(2):
                if hh:
                    act.wait_ge(S("gl_o"), 4)
                evac(f"ql{hh}", lambda t: l_tok[:, t, :])
                for i in range(4):
                    tcopy(f"ql{hh}", i, lq[:, i, :], tb(f"ql{hh}", i))
                evac(f"fl{hh}", lambda t: l_tok[:, t, :])
                for i in range(4):
                    u = TPU[f"fl{hh}"] + i
                    act.wait_ge(tp_ready, u + 1)
                    act.activation(lf[:, i, :], TP[u % 2], ACT.Sigmoid)
                    act.activation(lk[:, i, :], TP[u % 2], ACT.Sigmoid, scale=-1.0).then_inc(tp_free[u % 2], 1)
                evac(f"vl{hh}", lambda t: lv[:, t, :])
                act.wait_ge(S("lf_in"), hh + 1)
                act.activation(lf, lf, ACT.Ln).then_inc(S("lf_done"), 1)
                for h in range(4):
                    H = 4 * hh + h
                    for i in range(9):
                        n = 9 * H + i
                        act.wait_ge(S("gl_e"), n + 1)
                        act.activation(lexp[n % 2], lexp[n % 2], ACT.Exp).then_inc(S("gl_x"), 1)
                    act.wait_ge(S("gl_o"), H + 1)
                    act.activation(mix[:, :, P * H:P * H + P], ACC[H % 2].rearrange("p (t c) -> p t c", t=NT),
                                   ACT.Copy).then_inc(S("gl_od"), 1)
            end_phase(act, "ACT")
            for t in range(NT):
                if t >= 2:
                    act.wait_ge(S("gla_red"), t - 1)
                act.activation(lsq[:, t % 2, :], mix[:, t, 0:1024], ACT.Square).then_inc(S("gla_sq"), 1)
            act.wait_ge(S("gla_ms"), 1)
            act.activation(gl_n["rt"], gl_n["ms"], ACT.Sqrt).then_inc(S("gla_rt"), 1)
            act.wait_ge(S("gla_red"), NT)
            gates(1, silu3)


        @block.vector
        def _(dve):
            chain, los = [0], [0]

            def link(ins):
                chain[0] += 1
                ins.then_inc(S("dve_step"), 1)
                dve.wait_ge(S("dve_step"), chain[0])

            def feed(p):
                if p >= NP:
                    return
                dve.wait_ge(hi_done, p + 1)
                dve.tensor_tensor(w_slot(wlo, p, p % SPL), w_slot(wraw, p, p % RAW), w_slot(whi, p, p % SPL).bitcast(F32),
                                  ALU.subtract).then_inc(lo_done, 1)

            def during(j):
                for i in range(chunks[j]["count"] - 1):
                    feed(chunks[j]["first"] + i + SPL)

            def after(j):
                feed(chunks[j]["first"] + chunks[j]["count"] - 1 + SPL)

            def flow(name):
                during(CH[name])
                after(CH[name])

            def lo(name, i, dst, src, hi, gain=None):
                u = TPU[name] + i
                los[0] += 1
                dve.wait_ge(act_hi, los[0])
                if gain is None:
                    r = dve.tensor_tensor(dst, src, hi.bitcast(F32), ALU.subtract)
                else:
                    r = dve.scalar_tensor_tensor(dst, src, gain, hi.bitcast(F32), ALU.mult, ALU.subtract)
                r.then_inc(tp_free[u % 2], 1)

            def tb(name, i):
                return TP[(TPU[name] + i) % 2]

            def mean(name, c, width):
                dve.tensor_scalar(c["ms"], c["ss"], 1.0 / width, EPS, ALU.mult, ALU.add).then_inc(norm_ms, 1)
                dve.wait_ge(norm_rt, ORDER.index(name) + 1)
                link(dve.reciprocal(c["rs"], c["rt"]))

            def row_norm(name, nt, width, rows, dst=None):
                dve.wait_ge(norm_ss, so_far(name, 1, nt))
                mean(name, ns[name], width)
                for t in range(nt):
                    dve.tensor_scalar((dst or rows)(t), rows(t), ns[name]["rs"][:, t:t + 1], None, ALU.mult
                                      ).then_inc(norm_xs, 1)

            def head_norm(name, tok, nt, gain, sq):
                c = ns[name]
                for t in range(nt):
                    dve.wait_ge(head_sq, so_far(name, 3, t + 1))
                    dve.tensor_reduce(c["ss"][:, MH * t:MH * t + MH], sq.rearrange("p (h c) -> p h c", h=MH),
                                      AX.X, ALU.add).then_inc(head_red, 1)
                dve.wait_ge(head_red, so_far(name, 3, nt))
                mean(name, c, HD)
                for t in range(nt):
                    for h in range(MH):
                        x = tok[:, t, P * h:P * h + P]
                        dve.scalar_tensor_tensor(x, x, c["rs"][:, MH * t + h:MH * t + h + 1], gain, ALU.mult, ALU.mult
                                                 ).then_inc(norm_xs, 1)

            def attention(name, unit, n):
                U0 = AU[name]

                def maxima(i):
                    u, U = unit(i), U0 + i
                    r = U % 4
                    nm = att_nm[:, r:r + 1]
                    mx = att_mx[:, 3 * r:3 * r + len(u["s"])]
                    dve.wait_ge(att_s, U + 1)
                    if u["s"][0][3] is None:
                        link(dve.tensor_reduce(mx, SC[U % 2][:, 0:u["kw"]], AX.X, ALU.max))
                        dve.tensor_scalar(nm, mx, -u["s"][0][4], None, ALU.mult).then_inc(att_m, 1)
                        return
                    for k, (off, _, keys, mask, scale) in enumerate(u["s"]):
                        w = keys.shape[1]
                        ins = dve.tensor_tensor_reduce(u["sb"][U % 2][:, off:off + w], scores_out(U, off, w), mask, scale, LOW,
                                                       ALU.add, ALU.max, mx[:, k:k + 1])
                    link(ins)
                    if len(u["s"]) > 1:
                        link(dve.tensor_reduce(nm, mx, AX.X, ALU.max))
                        mx = nm
                    dve.tensor_scalar(nm, mx, -1.0, None, ALU.mult).then_inc(att_m, 1)

                maxima(0)
                for i in range(n):
                    u, U = unit(i), U0 + i
                    if i + 1 < n:
                        maxima(i + 1)
                    nb = u["kw"] // P
                    per = -(-nb // 4)
                    pt = u["pt"][i % len(u["pt"])]
                    if i >= len(u["pt"]):
                        dve.wait_ge(att_o, U - len(u["pt"]) + 1)
                    for k in range(per):
                        tu = TPU[name] + per * i + k
                        w = P * min(4, nb - 4 * k)
                        dve.wait_ge(tp_ready, tu + 1)
                        dve.tensor_copy(pt[:, 512 * k:512 * k + w], TP[tu % 2][:, 0:w]).then_inc(tp_free[tu % 2], 1)
                    dve.wait_ge(att_p, U + 1)
                    dve.reciprocal(att_rl[:, U % 4:U % 4 + 1], att_l[:, U % 4:U % 4 + 1]).then_inc(att_r, 1)

            def accumulate(name, dst):
                j = CH[name]
                during(j)
                for t in range(NT):
                    wait_acc(dve, j, t)
                    d = dst(t)
                    dve.tensor_tensor(d, ACC[t][:, :], d, ALU.add).then_inc(acc_free[t], 1)
                after(j)

            def memory_stage(l):
                row_norm(f"mem{l}", 2, D, lambda t: memx[:, t, :])
                for k in range(KD):
                    lo(f"mem{l}", k, AT_mem_lo[:, k, :], tb(f"mem{l}", k)[:, 0:MEM], AT_mem_hi[:, k, :], g_mem[l][:, k:k + 1])
                flow(f"mkv{l}0")
                head_norm(f"km{l}", km_tok, 2, mg[:, P:2 * P], msq)
                flow(f"mkv{l}1")
                flow(f"qm{l}")
                head_norm(f"qm{l}", qm_tok, NT, mg[:, 0:P], msq)
                attention(f"mat{l}", mem_unit, 16)

            def gates(l, tmp, res, res_in):
                for i in range(3):
                    j = CH[f"gate{l}{i}"]
                    during(j)
                    for t in range(NT):
                        wait_read(dve, f"gate{l}{i}", t)
                        m = mix[:, t, 512 * i:512 * i + 512]
                        dve.tensor_tensor(m, m, tmp[(NT * i + t) % 2], ALU.mult).then_inc(S(f"gated{l}"), 1)
                    after(j)
                for k in range(12):
                    lo(f"y{l}", k, AT_lo[:, k, :], tb(f"y{l}", k), AT_hi[:, k, :])
                dve.wait_ge(S(f"res{l + 2}"), res_in)
                for i in range(2):
                    accumulate(f"fin{l}{i}", lambda t: res[:, t, 512 * i:512 * i + 512])

            dve.sem_inc(S("hid_done"), 2)
            dve.sem_inc(S("y_done"), 2)
            dve.sem_inc(S("sc_ready"), 1)
            dve.sem_inc(S("sc_free"), 2)
            dve.sem_inc(S("gen_y"), 8)
            dve.sem_inc(S("gen_hid"), 1)
            dve.sem_inc(S("gen_add"), 2)
            feed(0)
            feed(1)
            row_norm("n1", NT, D, lambda t: xr[:, t, :])
            dve.wait_ge(S("gains_in"), 128)
            dve.wait_ge(S("consts"), 16)
            for k in range(KD):
                lo("n1", k, AT_lo[:, k, :], tb("n1", k), AT_hi[:, k, :], g_mix[:, k:k + 1])
            flow("cqkv0")
            flow("cqkv1")
            row_norm("cq", NT, 384, lambda t: cqkv[:, t, 0:384])
            row_norm("ckv", NT, 256, lambda t: cqkv[:, t, 384:640])
            for k in range(3):
                lo("cq", k, AT_lo[:, 8 + k, :], tb("cq", k), AT_hi[:, 8 + k, :], g_cq[:, k:k + 1])
            flow("uq0")
            flow("uq1")
            for k in range(2):
                lo("ckv", k, AT_lo[:, 8 + k, :], tb("ckv", k), AT_hi[:, 8 + k, :], g_ckv[:, k:k + 1])
            flow("uk")
            flow("uv")
            attention("mla", mla_unit, 32)
            for k in range(4):
                lo("oa", k, AT_lo[:, 8 + k, :], tb("oa", k), AT_hi[:, 8 + k, :])
            end_phase(dve, "DVE")

            for name in ("idx0", "idx1", "qkvb0", "qkvb1", "qkvb2", "ga0", "ga1"):
                flow(name)
            for i in range(2):
                j = CH[f"oa{i}"]
                during(j)
                for t in range(NT):
                    wait_acc(dve, j, t)
                    wait_read(dve, f"ga{i}", t)
                    y = y1[:, t, 512 * i:512 * i + 512]
                    dve.tensor_tensor(y, ACC[t][:, :], y, ALU.mult).then_inc(acc_free[t], 1)
                after(j)
            dve.wait_ge(S("b_rot"), 2)
            dve.wait_ge(tp_ready, TPU["ki"] + 1)
            for n in range(24):
                qt, h = 1 + n // 8, n % 8
                kw = P * (qt + 1)
                sc, w = score[:, qt - 1, 0:kw], wi_s[:, qt, h:h + 1]
                dve.wait_ge(S("idx_relu"), n + 1)
                if h == 0:
                    dve.tensor_scalar(sc, rel[n % 2][:, 0:kw], w, None, ALU.mult).then_inc(S("idx_add"), 1)
                else:
                    dve.wait_ge(S("idx_add"), n)
                    dve.scalar_tensor_tensor(sc, rel[n % 2][:, 0:kw], w, sc, ALU.mult, ALU.add).then_inc(S("idx_add"), 1)
                if h == 7:
                    dve.wait_ge(S("idx_add"), n + 1)
                    link(dve.tensor_tensor(sc[:, kw - P:kw], sc[:, kw - P:kw], cmask[:, 384:512], ALU.add))
            for qt in range(1, NT):
                kw = P * (qt + 1)
                sc, left = score[:, qt - 1, 0:kw], tk[:, 0:kw]
                for r in range(TOPK // 8):
                    src = left if r else sc
                    link(dve.max(max8, src))
                    link(dve.match_replace(left, max8, src, GONE))
                link(dve.tensor_tensor(sc, left, sc, ALU.is_equal))
                link(dve.tensor_scalar(sc, sc, NEG, None, ALU.mult))
            attention("dsa", dsa_unit, 32)
            flow("gb0")
            flow("gb1")
            for k in range(4):
                lo("ob", k, AT_lo[:, 8 + k, :], tb("ob", k), AT_hi[:, 8 + k, :])
            for i in range(2):
                j = CH[f"ob{i}"]
                during(j)
                for t in range(NT):
                    wait_acc(dve, j, t)
                    wait_read(dve, f"gb{i}", t)
                    b = gb[:, t, 512 * i:512 * i + 512]
                    dve.tensor_tensor(b, ACC[t][:, :], b, ALU.mult).then_inc(acc_free[t], 1)
                for t in range(NT):
                    y = y1[:, t, 512 * i:512 * i + 512]
                    wait_read(dve, f"ob{i}", t)
                    dve.tensor_tensor(y, y, gb[:, t, 512 * i:512 * i + 512], ALU.add).then_inc(S("y_sum"), 1)
                after(j)
            for k in range(KD):
                lo("y", k, AT_lo[:, k, :], tb("y", k), AT_hi[:, k, :])
            dve.wait_ge(S("res1"), 16)
            for i in range(2):
                accumulate(f"out{i}", lambda t: x1[:, t, 512 * i:512 * i + 512])
            end_phase(dve, "DVE")

            row_norm("ffn", NT, D, lambda t: x1[:, t, :], dst=lambda t: bigt[:, t, :])
            for t in range(NT):
                dve.wait_ge(S("xs_hi"), t + 1)
                dve.tensor_tensor(xs_lo[:, t, :], bigt[:, t, :], xs_hi[:, t, :].bitcast(F32), ALU.subtract
                                  ).then_inc(S("xs_lo"), 1)
            spread = lambda a, n: a.unsqueeze(2).broadcast_to([P, NT, n])
            rows = lambda a, n: a.unsqueeze(1).broadcast_to([P, NT, n])
            dve.wait_ge(S("moe_in"), 96)
            dve.wait_ge(S("rt_mm"), 1)
            link(dve.tensor_tensor(lg, ACC[0][:, 0:NT * 40].rearrange("p (t c) -> p t c", t=NT), rows(b_rt, 40), ALU.add))
            glg = lg[:, :, 0:8]
            link(dve.tensor_reduce(r_gmax, glg, AX.X, ALU.max))
            dve.tensor_tensor(r_d, glg, spread(r_gmax, 8), ALU.subtract).then_inc(S("rt_exp"), 1)
            link(dve.tensor_tensor(r_eq, glg, spread(r_gmax, 8), ALU.is_equal))
            link(dve.scalar_tensor_tensor(r_cand, r_eq, -8.0, rows(iota_g, 8), ALU.mult, ALU.add))
            link(dve.tensor_reduce(r_gi, r_cand, AX.X, ALU.min))
            dve.tensor_tensor(oneh, r_cand, spread(r_gi, 8), ALU.is_equal).then_inc(S("rt_oneh"), 1)
            dve.wait_ge(S("rt_oneh"), 1)
            link(dve.tensor_tensor(r_el, lg[:, :, 8:40].rearrange("p t (g e) -> p t g e", g=8),
                                   oneh.unsqueeze(3).broadcast_to([P, NT, 8, EPG]), ALU.mult))
            link(dve.tensor_reduce(r_in4, r_el.rearrange("p t g e -> p t e g"), AX.X, ALU.add))
            src = r_in4
            for m, oh in ((r_m1, r_oh1), (r_m2, r_oh2)):
                link(dve.tensor_reduce(m, src, AX.X, ALU.max))
                link(dve.tensor_tensor(r_eq4, src, spread(m, EPG), ALU.is_equal))
                link(dve.scalar_tensor_tensor(r_cand4, r_eq4, -8.0, rows(iota_g[:, 0:EPG], EPG), ALU.mult, ALU.add))
                link(dve.tensor_reduce(r_min4, r_cand4, AX.X, ALU.min))
                link(dve.tensor_tensor(oh, r_cand4, spread(r_min4, EPG), ALU.is_equal))
                if m is r_m1:
                    link(dve.scalar_tensor_tensor(r_in4b, r_oh1, LOW, r_in4, ALU.mult, ALU.add))
                    src = r_in4b
            dve.tensor_tensor(r_d2, r_m2, r_m1, ALU.subtract).then_inc(S("rt_exp"), 1)
            dve.wait_ge(S("rt_exp_done"), 2)
            link(dve.tensor_reduce(r_sum, r_e, AX.X, ALU.add))
            link(dve.tensor_scalar(r_w1, r_e2, 1.0, None, ALU.add))
            link(dve.tensor_tensor(r_w1, r_w1, r_sum, ALU.mult))
            link(dve.reciprocal(r_w1, r_w1))
            link(dve.tensor_tensor(r_w2, r_w1, r_e2, ALU.mult))
            dve.tensor_tensor(r_oh1, r_oh1, spread(r_w1, EPG), ALU.mult)
            link(dve.tensor_tensor(r_oh2, r_oh2, spread(r_w2, EPG), ALU.mult))
            dve.tensor_tensor(comb4, r_oh1, r_oh2, ALU.add).then_inc(S("rt_comb"), 1)
            dve.wait_ge(S("comb_hi"), 1)
            dve.tensor_tensor(comb_s[:, :, 4:8], comb4, comb_s[:, :, 0:4].bitcast(F32), ALU.subtract).then_inc(S("comb_lo"), 1)
            dve.wait_ge(S("rank_mm"), 1)
            link(dve.tensor_tensor(r_eq, ACC[1][:, 0:NT * 8].rearrange("p (t c) -> p t c", t=NT), oneh, ALU.mult))
            link(dve.tensor_reduce(r_rank, r_eq, AX.X, ALU.add))
            dve.tensor_scalar(r_over, r_rank, float(CAP), None, ALU.is_ge).then_inc(S("rt_over"), 1)
            link(dve.scalar_tensor_tensor(key, r_gi, float(P), r_rank, ALU.mult, ALU.add))
            link(dve.tensor_scalar(key, key, float(8 * P), None, ALU.add))
            link(dve.scalar_tensor_tensor(key, r_over, 1e6, key, ALU.mult, ALU.add))
            dve.tensor_copy(keyb, spread(key, P)).then_inc(S("key_b"), 1)
            dve.wait_ge(S("rt_over"), 1)
            link(dve.tensor_tensor(r_eq4, comb4, spread(r_over, EPG), ALU.mult))
            link(dve.tensor_tensor(comb32.rearrange("p t (g e) -> p t g e", g=NGRP), oneh.unsqueeze(3).broadcast_to([P, NT, 8, EPG]),
                                   r_eq4.unsqueeze(2).broadcast_to([P, NT, 8, EPG]), ALU.mult))
            dve.wait_ge(S("over_mm"), 1)
            link(dve.tensor_reduce(r_sum[0:1, 0:1], ACC[1][0:1, 64:64 + NT], AX.X, ALU.add))
            dve.tensor_copy(flag[0:1, 0:1], r_sum[0:1, 0:1]).then_inc(S("flag_in"), 1)
            dve.wait_ge(S("flag_in"), 1)
            dve.wait_ge(S("key_row"), 1)
            with dve.Fori(0, NGRP) as g:
                def feed_in(j):
                    p = P_MOE + j + SPL
                    dve.wait_ge(hi_done, g * PPG + (p + 1))
                    dve.tensor_tensor(wlo[:, p % SPL, :], wraw[:, p % RAW, :], whi[:, p % SPL, :].bitcast(F32),
                                      ALU.subtract).then_inc(lo_done, 1)

                def lo_in(i, parts):
                    dve.wait_ge(act_hi, g * 6 + (los[0] + i + 1))
                    for dst, src, hi_, gain in parts:
                        r = dve.scalar_tensor_tensor(dst, src, gain, hi_.bitcast(F32), ALU.mult, ALU.subtract)
                    r.then_inc(tp_free[i % 2], 1)

                def hidden(e):
                    dve.wait_ge(S("silu"), g * EPG + (e + 1))
                    dve.scalar_tensor_tensor(hid_sb[e % 2], ACC[e % 2][:, FF:2 * FF], wslot[:, e:e + 1], sg_sb[e % 2],
                                             ALU.mult, ALU.mult).then_inc(S("hid_done"), 1)
                    lo_in(2 + e, [(hd_lo[e % 2], TP[e % 2][:, 0:2 * P], hd_hi[e % 2], 1.0)])

                for t in range(NT):
                    dve.tensor_scalar(pick[:, t, :], iota_s, key[:, t:t + 1], None, ALU.is_equal)
                dve.tensor_scalar(put, keyrow, iota_p[:, 0:1], None, ALU.is_equal).then_inc(S("pick"), 1)
                dve.wait_ge(S("pick"), g + 1)
                dve.tensor_scalar(key, key, float(-P), None, ALU.add)
                dve.tensor_scalar(keyrow, keyrow, float(-P), None, ALU.add).then_inc(S("key_next"), 1)
                for i in range(2):
                    lo_in(i, [(xg_lo[:, 4 * i + k, :], TP[i][:, k * P:k * P + P], xg_hi[:, 4 * i + k, :],
                               g_ffn[:, 4 * i + k:4 * i + k + 1]) for k in range(4)])
                feed_in(0)
                feed_in(1)
                dve.wait_ge(S("ws_mm"), g + 1)
                dve.tensor_reduce(wslot, SC[0][:, 0:2 * EPG].rearrange("p (h e) -> p e h", h=2), AX.X, ALU.add
                                  ).then_inc(S("ws_read"), 1)
                dve.wait_ge(S("ws_read"), g + 1)
                hidden(0)
                feed_in(2)
                feed_in(3)
                hidden(1)
                for j in (4, 5, 6):
                    feed_in(j)
                hidden(2)
                for j in (7, 8, 9):
                    feed_in(j)
                hidden(3)
                feed_in(10)
                feed_in(11)
                for n in range(2):
                    dve.wait_ge(S("y_hi"), g * 2 + (n + 1))
                    dve.tensor_tensor(y_lo[:, 512 * n:512 * n + 512], ACC[2 + n], y_hi[:, 512 * n:512 * n + 512].bitcast(F32),
                                      ALU.subtract).then_inc(S("y_done"), 1)
                for i in range(2 * NT):
                    x = x1[:, i // 2, 512 * (i % 2):512 * (i % 2) + 512]
                    dve.wait_ge(S("sc_ready"), g * 8 + (i + 2))
                    dve.tensor_tensor(x, SC[i % 2], x, ALU.add).then_inc(S("sc_free"), 1)
                dve.wait_ge(S("key_next"), g + 1)
                dve.wait_ge(S("sc_free"), g * 8 + (8 + 2))
            los[0] += 6 * NGRP
            with dve.If(dve.value_load(flag[0:1, 0:1], min_val=0, max_val=T) > 0):
                with dve.Fori(0, NGRP * EPG) as e:
                    dve.wait_ge(S("gen_silu"), e + 1)
                    dve.tensor_tensor(gen_hid[:, 0, :], ACC[2], gen_sil[:, 0, :], ALU.mult)
                    dve.tensor_tensor(gen_hid[:, 1, :], ACC[3], gen_sil[:, 1, :], ALU.mult).then_inc(S("gen_hid"), 1)
                    for i in range(2 * NT):
                        t, n = i // 2, i % 2
                        x = x1[:, t, 512 * n:512 * n + 512]
                        dve.wait_ge(S("gen_y"), e * 8 + (8 + i + 1))
                        dve.scalar_tensor_tensor(x, SC[i % 2], comb32[:, t, bass.ds(e, 1)], x, ALU.mult, ALU.add
                                                 ).then_inc(S("gen_add"), 1)
                    dve.wait_ge(S("gen_add"), e * 8 + (8 + 2))
            end_phase(dve, "DVE")

            c = ns["final"]
            dve.wait_ge(norm_ss, so_far("final", 1, NT))
            mean("final", c, D)
            for t in range(NT):
                dve.scalar_tensor_tensor(xn[:, t, :], x1[:, t, :], c["rs"][:, t:t + 1], fin_g, ALU.mult, ALU.mult
                                         ).then_inc(S("fin_x"), 1)
            row_norm("n2", NT, D, lambda t: xn[:, t, :], dst=lambda t: x1[:, t, :])
            for k in range(KD):
                lo("n2", k, AT_perm(AT_lo, k), tb("n2", k).rearrange("p (t q r) -> p t q r", t=NT, r=4), AT_perm(AT_hi, k),
                   g_n2[0][:, k:k + 1])
            memory_stage(0)
            end_phase(dve, "DVE")

            dve.wait_ge(S("dil_in"), 64)
            ROUND, C1, C2 = 1.5 * 2 ** 23, 6.28125, 0.0019350051879882812
            C3 = 2 * np.pi - C1 - C2
            link(dve.tensor_copy(rot_p, posi[:, :]))
            link(dve.tensor_tensor(rot_a, rot_p.unsqueeze(2).broadcast_to([P, NT, 16]), inv2.unsqueeze(1).broadcast_to([P, NT, 16]),
                                   ALU.mult))
            link(dve.tensor_scalar(rot_k, rot_a, 1 / (2 * np.pi), ROUND, ALU.mult, ALU.add))
            link(dve.tensor_scalar(rot_k, rot_k, ROUND, None, ALU.subtract))
            for cc in (C1, C2, C3):
                link(dve.scalar_tensor_tensor(rot_a, rot_k, -float(cc), rot_a, ALU.mult, ALU.add))
            link(dve.tensor_scalar(rot_r, rot_a, 3.1415925, -3.1415925, ALU.min, ALU.max))
            link(dve.scalar_tensor_tensor(rot_c, rot_r, -1.0, rot_r, ALU.mult, ALU.min))
            dve.tensor_scalar(rot_c, rot_c, float(np.pi / 2), None, ALU.add).then_inc(S("rot_ang"), 1)
            for hp in range(4):
                for g in range(3):
                    n = 3 * hp + g
                    j = CH[f"qk{hp}{g}"]
                    during(j)
                    if n:
                        dve.wait_ge(tp_ready, TPU[f"qk{hp}"] + 4 * g if g else TPU[f"qk{hp - 1}"] + 12)
                    for t in range(NT):
                        dve.wait_ge(S("qk_sq"), NT * n + t + 1)
                        dve.tensor_reduce(qk_n["ss"][:, 4 * t:4 * t + 4], sqb.rearrange("p (h c) -> p h c", h=4), AX.X, ALU.add
                                          ).then_inc(S("qk_red"), 1)
                        dve.tensor_tensor(qk_t[:, t, :].rearrange("p (a h c) -> p a h c", a=2, h=2),
                                          ACC[t].rearrange("p (a h c) -> p a h c", a=2, h=2),
                                          qkg[:, g, :, :].unsqueeze(2).broadcast_to([P, 2, 2, P]), ALU.mult
                                          ).then_inc(acc_free[t], 1)
                    after(j)
                    dve.wait_ge(S("qk_red"), NT * n + NT)
                    dve.tensor_scalar(qk_n["ms"], qk_n["ss"], 1.0 / HD, EPS, ALU.mult, ALU.add).then_inc(S("qk_ms"), 1)
                    dve.wait_ge(S("qk_rt"), n + 1)
                    link(dve.reciprocal(qk_rs[:, g, :, :], qk_n["rt"].rearrange("p (t c) -> p t c", t=NT)))
                    q = qk_rs[:, g, :, 0:2]
                    link(dve.tensor_scalar(q, q, HD ** -0.5, None, ALU.mult))
                    dve.sem_inc(S("qk_rs"), 1)
                for h in range(2):
                    flow(f"v{hp}{h}")
                attention(f"dil{hp}", lambda i: dil_unit(hp, i), 8)
            end_phase(dve, "DVE")
            gates(0, silu_sb, res2, 64)
            row_norm("n3", NT, D, lambda t: res2[:, t, :], dst=lambda t: n3x[:, t, :])
            for k in range(KD):
                by_token = lambda a: a[:, k, :].rearrange("p (q r) -> p r q", r=4)
                lo("n3", k, by_token(AT_lo), tb("n3", k).rearrange("p (r q) -> p r q", r=4), by_token(AT_hi), g_n2[1][:, k:k + 1])
            end_phase(dve, "DVE")
            memory_stage(1)
            end_phase(dve, "DVE")

            dve.wait_ge(S("gla_in"), 64)
            dve.tensor_tensor(lbl[:, 1, :], lbl[:, 1, :], lbl[:, 0, :], ALU.subtract).then_inc(S("lb_in"), 1)
            dve.wait_ge(S("lb_ready"), 1)
            dve.wait_ge(S("gla_zero"), 1)
            diag = view(at_ltok, 2560, NT, 640)[:, :, 0:P]
            four = lambda a: a.rearrange("p (t c) -> p t c", t=NT)
            for hh in range(2):
                for nm in "qfv":
                    flow(f"{nm}l{hh}")
                wait_tp_read(dve, f"fl{hh}", 4)
                for i in range(4):
                    H = 4 * hh + i
                    dve.tensor_scalar(lf[:, i, :], lf[:, i, :], lb1[:, H:H + 1], lb[:, H:H + 1], ALU.mult, ALU.add)
                    r = dve.tensor_scalar(lk[:, i, :], lk[:, i, :], lb1[:, H:H + 1], None, ALU.mult)
                r.then_inc(S("lf_in"), 1)
                dve.wait_ge(S("lf_done"), hh + 1)
                dve.wait_ge(S("lf_in"), hh + 1)
                dve.wait_ge(S("lA_zero"), hh + 1)

                for h in range(4):
                    H = 4 * hh + h
                    if H:
                        dve.wait_ge(S("gl_e"), 9 * H)
                    dve.tensor_tensor_scan(G64, seg, lf[:, h, :], 0.0, ALU.mult, ALU.add)
                    link(dve.tensor_tensor_scan(G512, ones[:, 0:1].broadcast_to([P, T]), lf[:, h, :], 0.0, ALU.mult, ALU.add))

                    def halves(a, half):
                        v = a.rearrange("p (n s c) -> p n s c", s=2, c=half)
                        return v[:, :, 0, :], v[:, :, 1, :]

                    def exponents(i):
                        n, half = 9 * H + i, 1 << i
                        first, second = halves(G64 if half <= 64 else G512, half)
                        d1, d2 = halves(lexp[n % 2], half)
                        ref = first[:, :, half - 1:half].broadcast_to([P, T // (2 * half), half])
                        if n >= 2:
                            dve.wait_ge(S("gl_q"), n - 1)
                        dve.tensor_tensor(d1, ref, first, ALU.subtract)
                        if half == 64:
                            r = dve.tensor_copy(d2, second)
                        else:
                            r = dve.tensor_tensor(d2, second, ref, ALU.subtract)
                        r.then_inc(S("gl_e"), 1)

                    def operands(i):
                        n, half = 9 * H + i, 1 << i
                        dve.wait_ge(S("gl_x"), n + 1)
                        e1, e2 = halves(lexp[n % 2], half)
                        dve.tensor_tensor(halves(ke[n % 2], half)[0], halves(lk[:, h, :], half)[0], e1, ALU.mult)
                        dve.tensor_tensor(halves(qe[n % 2], half)[1], halves(lq[:, h, :], half)[1], e2, ALU.mult
                                          ).then_inc(S("gl_q"), 1)

                    def collect(i):
                        m = 10 * H + i
                        dve.wait_ge(S("gl_mm"), m + 1)
                        src = four(SC[m % 2])
                        if m:
                            dve.wait_ge(S("gl_c"), m)
                        if i <= 7:
                            mask = lmask[:, 7 if i == 0 else i - 1, :].bitcast(I32).unsqueeze(1).broadcast_to([P, NT, P])
                            dve.copy_predicated(diag, mask, src).then_inc(S("gl_c"), 1)
                        elif i == 8:
                            dve.tensor_copy(lA[:, 0, P:2 * P], src[:, 1, :])
                            dve.tensor_copy(lA[:, 2, 3 * P:4 * P], src[:, 3, :]).then_inc(S("gl_c"), 1)
                        else:
                            dve.tensor_copy(lA[:, 0:2, 2 * P:4 * P], SC[m % 2].rearrange("p (s t) -> p s t", s=2)
                                            ).then_inc(S("gl_c"), 1)

                    if H:
                        dve.wait_ge(S("gl_o"), H)
                    exponents(0)
                    for i in range(9):
                        if i + 1 < 9:
                            exponents(i + 1)
                        operands(i)
                        collect(i)
                    collect(9)
            end_phase(dve, "DVE")
            for t in range(NT):
                dve.wait_ge(S("gla_sq"), t + 1)
                dve.tensor_reduce(gl_n["ss"][:, 8 * t:8 * t + 8], lsq[:, t % 2, :].rearrange("p (h c) -> p h c", h=8), AX.X, ALU.add
                                  ).then_inc(S("gla_red"), 1)
            dve.wait_ge(S("gla_red"), NT)
            dve.tensor_scalar(gl_n["ms"], gl_n["ss"], 1.0 / HD, EPS, ALU.mult, ALU.add).then_inc(S("gla_ms"), 1)
            dve.wait_ge(S("gla_rt"), 1)
            link(dve.reciprocal(gl_n["rs"], gl_n["rt"]))
            for t in range(NT):
                for h in range(8):
                    m = mix[:, t, P * h:P * h + P]
                    r = dve.scalar_tensor_tensor(m, m, gl_n["rs"][:, 8 * t + h:8 * t + h + 1], og, ALU.mult, ALU.mult)
            link(r)
            gates(1, silu3, res3, 16)

        @block.tensor
        def _(pe):
            PASSES = lambda ah, al, bh, bl: ((ah, bh), (ah, bl), (al, bh))

            def project(name):
                j = CH[name]
                c = chunks[j]
                n, per, nt = c["n"], c["per"], c["nt"]
                for i in range(c["count"]):
                    p = c["first"] + i
                    pe.wait_ge(lo_done, p + 1)
                    for t in range(nt):
                        if i == 0 and bank_uses[j][t]:
                            pe.wait_ge(acc_free[t], bank_uses[j][t])
                        for kk in range(per):
                            kc = i * per + kk
                            cols = slice(t * P, t * P + P)
                            ah, al = ((AT_mem_hi[:, kc, cols], AT_mem_lo[:, kc, cols]) if c["mem"] else
                                      (AT_hi[:, c["at"] + kc, cols], AT_lo[:, c["at"] + kc, cols]))
                            bh, bl = (w[:, p % SPL, kk * n:kk * n + n] for w in (whi, wlo))
                            for q, (a, b) in enumerate(PASSES(ah, al, bh, bl)):
                                mm = pe.matmul(ACC[t][:, 0:n], a, b, start=kc == 0 and q == 0,
                                               stop=i == c["count"] - 1 and kk == per - 1 and q == 2)
                        if t == nt - 1:
                            mm.then_inc(piece_used, 1)
                        elif i == c["count"] - 1:
                            mm.then_inc(acc_ready, 1)

            def transposes(name, i, blocks):
                u = TPU[name] + i
                if u >= 2:
                    pe.wait_ge(tp_free[u % 2], u // 2)
                at = 0
                for b in blocks:
                    tr = pe.transpose(TP[u % 2][0:b.shape[1], at:at + P], b, ident)
                    at += P
                tr.then_inc(tp_ready, 1)

            def rows_t(name, n, rows, nt=NT):
                for k in range(n):
                    if k == 0:
                        pe.wait_ge(norm_xs, so_far(name, 2, nt))
                    transposes(name, k, [rows(t)[:, P * k:P * k + P] for t in range(nt)])
                wait_tp_read(pe, name, n)

            def attention(name, unit, n):
                U0 = AU[name]

                def scores(i):
                    u, U = unit(i), U0 + i
                    if i >= 2:
                        pe.wait_ge(att_done, U - 1)
                    for off, q, k, _, _ in u["s"]:
                        mm = pe.matmul(scores_out(U, off, k.shape[1]), q, k, start=True, stop=True)
                    mm.then_inc(att_s, 1)

                def probs_t(i):
                    u, U = unit(i), U0 + i
                    pe.wait_ge(att_p, U + 1)
                    nb = u["kw"] // P
                    per = -(-nb // 4)
                    for k in range(per):
                        transposes(name, per * i + k, [u["sb"][U % 2][:, P * b:P * b + P] for b in range(4 * k, min(nb, 4 * k + 4))])

                def output(i):
                    u, U = unit(i), U0 + i
                    nb = u["kw"] // P
                    per = -(-nb // 4)
                    for k in range(per):
                        tu = TPU[name] + per * i + k
                        pe.wait_ge(tp_free[tu % 2], tu // 2 + 1)
                    pt = u["pt"][i % len(u["pt"])]
                    for b in range(nb):
                        mm = pe.matmul(SC[U % 2][:, 0:u["dv"]], pt[:, P * b:P * b + P], u["v"][b], start=b == 0, stop=b == nb - 1)
                    mm.then_inc(att_o, 1)

                scores(0)
                for i in range(n):
                    if i + 1 < n:
                        scores(i + 1)
                    probs_t(i)
                    output(i)

            def read_all(name):
                for t in range(chunks[CH[name]]["nt"]):
                    wait_read(pe, name, t)

            def memory_stage(l):
                rows_t(f"mem{l}", KD, lambda t: memx[:, t, :], nt=2)
                project(f"mkv{l}0")
                project(f"mkv{l}1")
                for name, tok, nt in ((f"km{l}", km_tok, 2), (f"qm{l}", qm_tok, NT)):
                    if tok is qm_tok:
                        project(f"qm{l}")
                    pe.wait_ge(norm_xs, so_far(name, 2, MH * nt))
                    for h in range(MH):
                        transposes(name, h, [tok[:, t, P * h:P * h + P] for t in range(nt)])
                    wait_tp_read(pe, name, MH)
                read_all(f"mkv{l}1")
                attention(f"mat{l}", mem_unit, 16)

            def gates(l):
                for i in range(3):
                    project(f"gate{l}{i}")
                pe.wait_ge(S(f"gated{l}"), 3 * NT)
                for k in range(12):
                    transposes(f"y{l}", k, [mix[:, t, P * k:P * k + P] for t in range(NT)])
                wait_tp_read(pe, f"y{l}", 12)
                for i in range(2):
                    project(f"fin{l}{i}")

            pe.wait_ge(S("consts"), 16)
            rows_t("n1", KD, lambda t: xr[:, t, :])
            project("cqkv0")
            project("cqkv1")
            rows_t("cq", 3, lambda t: cqkv[:, t, 0:384])
            project("uq0")
            project("uq1")
            for h in range(H8):
                pe.wait_ge(S("qa_rot"), h // 4 + 1)
                transposes("qa", h, [qk_tok[:, t, h, :] for t in range(NT)])
            rows_t("ckv", 2, lambda t: cqkv[:, t, 384:640])
            project("uk")
            project("uv")
            read_all("uk")
            pe.wait_ge(S("ka_rot"), NT)
            for h in range(H8):
                transposes("ka", h, [qk_tok[:, t, h, :] for t in range(NT)])
            wait_tp_read(pe, "ka", H8)
            read_all("uv")
            attention("mla", mla_unit, 32)
            pe.wait_ge(att_done, AU["mla"] + 32)
            for k in range(4):
                transposes("oa", k, [o_tok[:, t, P * k:P * k + P] for t in range(NT)])
            end_phase(pe, "PE")

            for name in ("idx0", "idx1", "qkvb0", "qkvb1", "qkvb2", "ga0", "ga1", "oa0", "oa1"):
                project(name)
            pe.wait_ge(S("b_rot"), 2)
            for i in range(8):
                transposes("qkb", i, [qkvb[:, t, P * i:P * i + P] for t in range(NT)])
            for i in range(4):
                transposes("qi", i, [idx[:, t, P * i:P * i + P] for t in range(NT)])
            transposes("ki", 0, [kidup[:, t, :] for t in range(NT)])
            wait_tp_read(pe, "qkb", 8)
            wait_tp_read(pe, "qi", 4)
            wait_tp_read(pe, "ki", 1)
            for n in range(24):
                qt, h = 1 + n // 8, n % 8
                r0 = 64 * (h % 2)
                kw = P * (qt + 1)
                if n >= 2:
                    pe.wait_ge(S("idx_relu"), n - 1)
                pe.matmul(SC[n % 2][:, 0:kw], qiT[r0:r0 + 64, h // 2, qt * P:qt * P + P], kiT[r0:r0 + 64, 0:kw],
                          start=True, stop=True).then_inc(S("idx_mm"), 1)
            pe.wait_ge(S("idx_relu"), 24)
            attention("dsa", dsa_unit, 32)
            project("gb0")
            project("gb1")
            pe.wait_ge(att_done, AU["dsa"] + 32)
            for k in range(4):
                transposes("ob", k, [o_tokb[:, t, P * k:P * k + P] for t in range(NT)])
            wait_tp_read(pe, "ob", 4)
            project("ob0")
            project("ob1")
            pe.wait_ge(S("y_sum"), 2 * NT)
            for k in range(KD):
                transposes("y", k, [y1[:, t, P * k:P * k + P] for t in range(NT)])
            wait_tp_read(pe, "y", KD)
            project("out0")
            project("out1")
            end_phase(pe, "PE")

            pe.wait_ge(norm_xs, so_far("ffn", 2, NT))
            for k in range(KD):
                transposes("h2", k, [bigt[:, t, P * k:P * k + P] for t in range(NT)])
            wait_tp_read(pe, "h2", KD)
            pe.wait_ge(S("moe_in"), 96)
            for t in range(NT):
                for k in range(KD):
                    mm = pe.matmul(ACC[0][:, 40 * t:40 * t + 40], h2T[:, k, t * P:t * P + P], w_rt[:, k, :],
                                   start=k == 0, stop=k == KD - 1)
            mm.then_inc(S("rt_mm"), 1)
            pe.wait_ge(S("rt_oneh"), 1)
            for t in range(NT):
                for b in range(t + 1):
                    mm = pe.matmul(ACC[1][:, 8 * t:8 * t + 8], before if b == t else ones, oneh[:, b, :],
                                   start=b == 0, stop=b == t)
            mm.then_inc(S("rank_mm"), 1)
            pe.wait_ge(S("rt_over"), 1)
            pe.matmul(ACC[1][:, 64:64 + NT], ones, r_over, start=True, stop=True).then_inc(S("over_mm"), 1)
            pe.wait_ge(S("key_b"), 1)
            for t in range(NT):
                mm = pe.matmul(ACC[2][:, t * P:t * P + P], keyb[:, t, :], ident, start=True, stop=True)
            mm.then_inc(S("key_mm"), 1)
            pe.wait_ge(S("xs_lo"), NT)
            pe.wait_ge(S("comb_lo"), 1)
            pe.wait_ge(S("key_row"), 1)
            with pe.Fori(0, NGRP) as g:
                def piece(j):
                    pe.wait_ge(lo_done, g * PPG + (P_MOE + j + 1))
                    return (P_MOE + j) % SPL

                def bank_free(i):
                    u = TPU["moe"] + i
                    pe.wait_ge(tp_free[i % 2], g * 3 + u // 2)

                def bank_read(i):
                    u = TPU["moe"] + i
                    pe.wait_ge(tp_free[i % 2], g * 3 + (u // 2 + 1))

                def gather(i):
                    bank_free(i)
                    for k in range(4):
                        n = 0
                        cols = slice((4 * i + k) * P, (4 * i + k) * P + P)
                        for part in (xs_hi, xs_lo):
                            for t in range(NT):
                                mm = pe.matmul(TP[i][:, k * P:k * P + P], part[:, t, cols], pick[:, t, :], start=n == 0, stop=n == 7)
                                n += 1
                    mm.then_inc(tp_ready, 1)

                def gate_up(j, e, half):
                    s = piece(j)
                    if half == 0:
                        pe.wait_ge(S("hid_done"), g * EPG + (e + 1))
                    for kk in range(4):
                        k = 4 * half + kk
                        bh, bl = (w[:, s, kk * 512:kk * 512 + 512] for w in (whi, wlo))
                        for q, (a, b) in enumerate(PASSES(xg_hi[:, k, :], xg_lo[:, k, :], bh, bl)):
                            mm = pe.matmul(ACC[e % 2], a, b, start=k == 0 and q == 0, stop=k == 7 and q == 2)
                    mm.then_inc(piece_used, 1)

                def hidden_t(e):
                    bank_free(2 + e)
                    pe.wait_ge(S("hid_done"), g * EPG + (e + 3))
                    for b in range(2):
                        tr = pe.transpose(TP[e % 2][:, b * P:b * P + P], hid_sb[e % 2][:, b * P:b * P + P], ident)
                    tr.then_inc(tp_ready, 1)

                def down(j, e):
                    s = piece(j)
                    bank_read(2 + e)
                    for n in range(2):
                        if e == 0:
                            pe.wait_ge(S("y_done"), g * 2 + (n + 1))
                        for b in range(2):
                            bh, bl = (w[:, s, 1024 * b + 512 * n:1024 * b + 512 * n + 512] for w in (whi, wlo))
                            for q, (x, y) in enumerate(PASSES(hd_hi[e % 2][:, b * P:b * P + P], hd_lo[e % 2][:, b * P:b * P + P], bh, bl)):
                                mm = pe.matmul(ACC[2 + n], x, y, start=e == 0 and b == 0 and q == 0, stop=e == 3 and b == 1 and q == 2)
                    mm.then_inc(piece_used, 1)

                pe.wait_ge(S("pick"), g + 1)
                gather(0)
                gather(1)
                bank_read(0)
                bank_read(1)
                gate_up(0, 0, 0)
                gate_up(1, 0, 1)
                pe.wait_ge(S("sc_free"), g * 8 + 2)
                for t in range(NT):
                    mm = pe.matmul(SC[0][:, 0:2 * EPG], pick[:, t, :], comb_s[:, t, :], start=t == 0, stop=t == NT - 1)
                mm.then_inc(S("ws_mm"), 1)
                gate_up(2, 1, 0)
                gate_up(3, 1, 1)
                hidden_t(0)
                down(4, 0)
                gate_up(5, 2, 0)
                hidden_t(1)
                gate_up(6, 2, 1)
                down(7, 1)
                gate_up(8, 3, 0)
                hidden_t(2)
                gate_up(9, 3, 1)
                down(10, 2)
                hidden_t(3)
                down(11, 3)
                pe.wait_ge(S("y_done"), g * 2 + 4)
                for i in range(2 * NT):
                    t, n = i // 2, i % 2
                    pe.wait_ge(S("sc_free"), g * 8 + (i + 1))
                    for q, y in enumerate((y_hi, y_lo)):
                        mm = pe.matmul(SC[i % 2], put[:, t * P:t * P + P], y[:, 512 * n:512 * n + 512], start=q == 0, stop=q == 1)
                    mm.then_inc(S("sc_ready"), 1)
            pe.wait_ge(S("sc_free"), 8 * NGRP + 2)
            pe.sem_inc(S("moe_end"), 1)
            pe.wait_ge(S("flag_in"), 1)
            with pe.If(pe.value_load(flag[0:1, 0:1], min_val=0, max_val=T) > 0):
                with pe.Fori(0, NGRP * EPG) as e:
                    pe.wait_ge(S("gen_in"), e * 48 + 48)
                    for f in range(2):
                        for w in range(2):
                            for k in range(KD):
                                mm = pe.matmul(ACC[2 * w + f], gen_gu[:, w, k, f * P:f * P + P], h2T[:, k, :],
                                               start=k == 0, stop=k == KD - 1)
                    mm.then_inc(S("gen_gu"), 1)
                    pe.wait_ge(S("gen_hid"), e + 2)
                    for i in range(2 * NT):
                        t, n = i // 2, i % 2
                        pe.wait_ge(S("gen_add"), e * 8 + (i + 1))
                        for f in range(2):
                            mm = pe.matmul(SC[i % 2], gen_hid[:, f, t * P:t * P + P], gen_d[:, f, 512 * n:512 * n + 512],
                                           start=f == 0, stop=f == 1)
                        mm.then_inc(S("gen_y"), 1)
            end_phase(pe, "PE")

            rows_t("n2", KD, lambda t: x1[:, t, :])
            memory_stage(0)
            end_phase(pe, "PE")
            for hp in range(4):
                for g in range(3):
                    project(f"qk{hp}{g}")
                    pe.wait_ge(S("qk_rot"), 3 * hp + g + 1)
                    for i in range(4):
                        transposes(f"qk{hp}", 4 * g + i, [qk_t[:, t, P * i:P * i + P] for t in range(NT)])
                for h in range(2):
                    project(f"v{hp}{h}")
                wait_tp_read(pe, f"qk{hp}", 12)
                for h in range(2):
                    read_all(f"v{hp}{h}")
                attention(f"dil{hp}", lambda i: dil_unit(hp, i), 8)
            end_phase(pe, "PE")
            gates(0)
            rows_t("n3", KD, lambda t: n3x[:, t, :])
            end_phase(pe, "PE")
            memory_stage(1)
            end_phase(pe, "PE")

            for hh in range(2):
                if hh:
                    pe.wait_ge(S("gl_od"), 4)
                for nm in "qf":
                    project(f"{nm}l{hh}")
                    read_all(f"{nm}l{hh}")
                    for i in range(4):
                        transposes(f"{nm}l{hh}", i, [l_tok[:, t, P * i:P * i + P] for t in range(NT)])
                project(f"vl{hh}")
                read_all(f"vl{hh}")
                pe.wait_ge(S("lf_in"), hh + 1)
                for h in range(4):
                    H = 4 * hh + h
                    for i in range(10):
                        m = 10 * H + i
                        if m >= 2:
                            pe.wait_ge(S("gl_c"), m - 1)
                        if i == 0:
                            k, q = lk[:, h, :], lq[:, h, :]
                        else:
                            n = 9 * H + i - 1
                            pe.wait_ge(S("gl_q"), n + 1)
                            k, q = ke[n % 2], qe[n % 2]
                        tile = lambda a, t: a[:, t * P:t * P + P]
                        if i <= 7:
                            blocks = [(t * P, t, q[:, t * P:t * P + P]) for t in range(NT)]
                        elif i == 8:
                            blocks = [(t * P, t - 1, q[:, t * P:t * P + P]) for t in (1, 3)]
                        else:
                            blocks = [(2 * P * s, s, q[:, 2 * P:4 * P]) for s in range(2)]
                        for c0, s, rhs in blocks:
                            mm = pe.matmul(SC[m % 2][:, c0:c0 + rhs.shape[1]], tile(k, s), rhs, start=True, stop=True)
                        mm.then_inc(S("gl_mm"), 1)
                    pe.wait_ge(S("gl_c"), 10 * H + 10)
                    if H >= 2:
                        pe.wait_ge(S("gl_od"), H - 1)
                    for t in range(NT):
                        for s in range(t + 1):
                            mm = pe.matmul(ACC[H % 2][:, t * P:t * P + P], lA[:, s, t * P:t * P + P], lv[:, s, P * h:P * h + P],
                                           start=s == 0, stop=s == t)
                    mm.then_inc(S("gl_o"), 1)
            end_phase(pe, "PE")
            gates(1)


def kernel(x, norm_mix_g, w_in, mla_q_norm_g, w_uq, mla_kv_norm_g, w_uk, w_uv, w_o_a, w_o_b, w_out,
           norm_ffn_g, w_router_group, b_router_group, w_router_expert, b_router_expert, w_gate, w_up,
           w_down, final_norm_g, mem_2, positions_2, norm_gain_2, w_in_a_2, q_gain_a_2, k_gain_a_2,
           w_out_a_2, w_in_b_2, lb_logits_2, o_gain_b_2, w_out_b_2, mem_norm_gain_2, w_mem_kv_2,
           mem_q_gain_2, mem_k_gain_2):
    import concourse.bacc as bacc
    from concourse.bass_utils import run_bass_kernel_spmd

    arrays = dict(
        x=x, norm_mix_g=norm_mix_g, w_in=w_in, mla_q_norm_g=mla_q_norm_g, w_uq=w_uq, mla_kv_norm_g=mla_kv_norm_g,
        w_uk=w_uk, w_uv=w_uv, w_o_a=w_o_a, w_o_b=w_o_b, w_out=w_out, norm_ffn_g=norm_ffn_g,
        w_router_group=w_router_group, b_router_group=b_router_group, w_router_expert=w_router_expert,
        b_router_expert=b_router_expert, w_gate=w_gate, w_up=w_up, w_down=w_down, final_norm_g=final_norm_g,
        mem_2=mem_2, positions_2=positions_2, norm_gain_2=norm_gain_2, w_in_a_2=w_in_a_2, q_gain_a_2=q_gain_a_2,
        k_gain_a_2=k_gain_a_2, w_out_a_2=w_out_a_2, w_in_b_2=w_in_b_2, lb_logits_2=lb_logits_2, o_gain_b_2=o_gain_b_2,
        w_out_b_2=w_out_b_2, mem_norm_gain_2=mem_norm_gain_2, w_mem_kv_2=w_mem_kv_2, mem_q_gain_2=mem_q_gain_2,
        mem_k_gain_2=mem_k_gain_2)
    arrays = {name: np.ascontiguousarray(a) for name, a in arrays.items()}
    arrays["const"] = CONST
    nc = bacc.Bacc("TRN2", target_bir_lowering=False, num_devices=1)
    aps = {name: nc.dram_tensor(name, a.shape, mybir.dt.from_np(a.dtype), kind="ExternalInput").ap()
           for name, a in arrays.items()}
    out = nc.dram_tensor("out", (1, T, D), F32, kind="ExternalOutput").ap()
    build(nc, aps, out)
    return run_bass_kernel_spmd(nc, [arrays], core_ids=[0]).results[0]["out"]
```

```python
from contextlib import ExitStack

import numpy as np

import concourse.bass as bass
from concourse import mybir

F32 = mybir.dt.float32
F32R = mybir.dt.float32r
I32 = mybir.dt.int32
ALU = mybir.AluOpType
ACT = mybir.ActivationFunctionType
AX = mybir.AxisListType

P = 128
T, D = 512, 1024
NT, KD = T // P, D // P
EPS = 1e-6
NEG = -1e30
LOW = -3e38
GONE = -3.4e38
THETA = 500000.0
RAW, SPL = 6, 4
PIECE = 1024
H8 = 8
TOPK = min(256, T // 4)
NGRP, EPG, FF = 8, 4, 256
CAP = 128
DIL = ((128, 1), (512, 4), (2048, 16))
MEM = 256
MH = 4
HD = 128

C_CQ, C_CKV, C_KR, C_QB, C_KB, C_VB, C_QI, C_KI, C_WI, C_GA, C_GB = np.cumsum(
    [0, 384, 256, 32, 512, 512, 512, 512, 64, 8, 1024]).tolist()


def shape_constants():
    parts, at, n = [], {}, 0

    def add(name, a):
        nonlocal n
        a = np.ascontiguousarray(a, np.float32).reshape(P, -1)
        at[name] = (n, a.shape[1])
        parts.append(a)
        n += a.shape[1]

    p = np.arange(P)
    add("ident", np.eye(P))
    chunk_mask = np.where((p[None, :] // 64) <= (p[:, None] // 64), 0.0, NEG)
    add("cmask", np.concatenate([np.zeros((P, 384)), chunk_mask], 1))
    pos = (np.arange(NT)[None, :] * P + p[:, None]).astype(np.float32)
    for name, rot in (("A", 32), ("B", 16)):
        half = rot // 2
        inv = np.float32(THETA) ** (-np.arange(half, dtype=np.float32) * np.float32(2.0) / np.float32(rot))
        ang = pos[:, :, None] * inv.astype(np.float32)[None, None, :]
        add("cos" + name, np.cos(ang))
        add("sin" + name, np.sin(ang))
    add("ones", np.ones((P, P)))
    base_end = n
    add("before", (p[:, None] < p[None, :]).astype(np.float32))
    add("iota_g", np.broadcast_to(np.arange(8), (P, 8)))
    add("iota_s", np.broadcast_to(np.arange(P), (P, P)))
    add("iota_p", p[:, None])
    moe_end = n
    dp = 4 * (p[:, None] - p[None, :])
    add("wmask", np.stack([np.where((dp + d >= 0) & (dp + d <= 128), 0.0, NEG)
                           for d in (3, 2, 1, 0, -1, -2, -3)], 1))
    add("dmask", np.stack([np.where(p[None, :] <= p[:, None], 0.0, NEG),
                           np.where((p[None, :] <= p[:, None]) & ((p[:, None] - p[None, :]) % 4 == 0), 0.0, NEG)], 1))
    inv2 = np.float32(THETA) ** (-np.arange(0, 32, 2, dtype=np.float32) / np.float32(32))
    add("inv2", np.broadcast_to(inv2, (P, 16)))
    dil_end = n
    s, t = p[:, None], p[None, :]
    levels = []
    for half in (1, 2, 4, 8, 16, 32, 64):
        levels.append((s // (2 * half) == t // (2 * half)) & (s // half % 2 == 0) & (t // half % 2 == 1))
    levels.append(s == t)
    add("lmask", np.stack(levels, 1))
    sg = np.ones(T)
    sg[::64] = 0.0
    add("seg", np.broadcast_to(sg, (P, T)))
    return np.concatenate(parts, 1), at, (base_end, moe_end, dil_end, n)


CONST, CAT, (C_BASE, C_MOE, C_DIL, C_ALL) = shape_constants()


def build(nc, A, out):
    ctx = ExitStack()
    with ctx:
        def sb(name, shape, dt=F32):
            return ctx.enter_context(nc.sbuf_tensor(name, shape, dt))

        sems = {}

        def S(name):
            if name not in sems:
                sems[name] = ctx.enter_context(nc.semaphore(name))
            return sems[name]

        wraw = sb("wraw", [P, RAW, PIECE])
        whi = sb("whi", [P, SPL, PIECE], F32R)
        wlo = sb("wlo", [P, SPL, PIECE], F32R)
        AT_hi = sb("AT_hi", [P, 12, T], F32R)
        AT_lo = sb("AT_lo", [P, 12, T], F32R)
        y_hi = sb("y_hi", [P, 1024], F32R)
        y_lo = sb("y_lo", [P, 1024], F32R)
        comb_s = sb("comb_s", [P, NT, 8], F32R)
        small = sb("small", [P, 720])
        flag = sb("flag", [1, 2], I32)
        posi = sb("posi", [P, NT], I32)
        n_arena = 23700
        arena = sb("arena", [P, n_arena])
        pb = ctx.enter_context(nc.psum_tensor("pb", [P, 8, 512], F32))
        ACC = [pb[:, i, :] for i in range(4)]
        TP = [pb[:, 4 + i, :] for i in range(2)]
        SC = [pb[:, 6 + i, :] for i in range(2)]

        x_mid = nc.dram_tensor("x_mid", (T, D), F32, kind="Internal").ap()
        x_mid2 = nc.dram_tensor("x_mid2", (T, D), F32, kind="Internal").ap()

        top = [0]
        marks = {}

        def take(n, *shape, **kw):
            a = top[0]
            top[0] += n
            assert top[0] <= n_arena, (top[0], n_arena)
            return view(a, n, *shape)

        def view(a, n, *shape):
            v = arena[:, a:a + n]
            if len(shape) <= 1:
                return v
            names = "abcd"[:len(shape)]
            return v.rearrange("p (" + " ".join(names) + ") -> p " + " ".join(names),
                               **{k: m for k, m in zip(names, shape)})

        stat_at = [0]

        def stat(n):
            a = stat_at[0]
            stat_at[0] += n
            assert stat_at[0] <= 720
            return small[:, a:a + n]

        base0 = take(C_BASE)

        def const(name, where, first):
            a, n = CAT[name]
            return where[:, a - first:a - first + n]

        ident = const("ident", base0, 0)
        cmask = const("cmask", base0, 0)
        ones = const("ones", base0, 0)
        ropeA = [const(k + "A", base0, 0).rearrange("p (t c) -> p t c", t=NT) for k in ("cos", "sin")]
        ropeB = [const(k + "B", base0, 0).rearrange("p (t c) -> p t c", t=NT) for k in ("cos", "sin")]
        gains = take(64)
        g_mix, g_cq, g_ckv, g_ffn = gains[:, 0:8], gains[:, 8:11], gains[:, 11:13], gains[:, 13:21]
        g_n2 = [gains[:, 21:29], gains[:, 29:37]]
        g_mem = [gains[:, 37:45], gains[:, 45:53]]
        AT_mem_hi, AT_mem_lo = (a[:, 8:12, :].rearrange("p a b -> p (a b)").rearrange("p (k m) -> p k m", k=KD)
                                for a in (AT_hi, AT_lo))
        phase0 = top[0]

        pieces = []
        chunks = []
        CH = {}

        def chunk(name, srcs, n, at, k, per, nt=NT, mem=False):
            first = len(pieces)
            for k0 in range(0, k, per):
                loads, c0 = [], 0
                for s in srcs:
                    w = s.shape[2]
                    loads.append((c0, w, s[:, k0:k0 + per, :]))
                    c0 += w
                assert c0 == n and per * n <= PIECE
                pieces.append((loads, per, n))
            CH[name] = len(chunks)
            chunks.append(dict(first=first, count=k // per, n=n, at=at, per=per, nt=nt, mem=mem))

        def tiled(w):
            return w.rearrange("(k p) n -> p k n", p=P)

        w_in = tiled(A["w_in"][0])
        for i in range(2):
            chunk(f"cqkv{i}", [w_in[:, :, 336 * i:336 * i + 336]], 336, 0, 8, 2)
        w_uq = tiled(A["w_uq"][0])
        for i in range(2):
            chunk(f"uq{i}", [w_uq[:, :, 384 * i:384 * i + 384]], 384, 8, 3, 1)
        chunk("uk", [tiled(A["w_uk"][0])], 512, 8, 2, 2)
        chunk("uv", [tiled(A["w_uv"][0])], 512, 8, 2, 2)
        for i in range(2):
            chunk(f"idx{i}", [w_in[:, :, C_QI + 292 * i:C_QI + 292 * i + 292]], 292, 0, 8, 2)
        for i in range(3):
            chunk(f"qkvb{i}", [w_in[:, :, C_QB + 512 * i:C_QB + 512 * i + 512]], 512, 0, 8, 2)
        for ab, c0, w in (("a", C_GA, "w_o_a"), ("b", C_GB, "w_o_b")):
            for i in range(2):
                chunk(f"g{ab}{i}", [w_in[:, :, c0 + 512 * i:c0 + 512 * i + 512]], 512, 0, 8, 2)
            for i in range(2):
                chunk(f"o{ab}{i}", [tiled(A[w][0])[:, :, 512 * i:512 * i + 512]], 512, 8, 4, 2)
        for i in range(2):
            chunk(f"out{i}", [tiled(A["w_out"][0])[:, :, 512 * i:512 * i + 512]], 512, 0, 8, 2)
        P_MOE = len(pieces)
        GROUP_ORDER = [(kind, e, q) for kind, e, n in (("gu", 0, 4), ("gu", 1, 4), ("dn", 0, 2), ("gu", 2, 4), ("dn", 1, 2),
                                                       ("gu", 3, 4), ("dn", 2, 2), ("dn", 3, 2)) for q in range(n)]
        PPG = len(GROUP_ORDER)
        piece_of = {what: j for j, what in enumerate(GROUP_ORDER)}
        for what in range(NGRP * PPG):
            pieces.append(None)

        def memory_chunks(l):
            w = tiled(A["w_mem_kv_2"][l])
            for i in range(2):
                chunk(f"mkv{l}{i}", [w[:, :, 512 * i:512 * i + 512]], 512, 8, 8, 2, nt=2, mem=True)

        def gate_chunks(l, w, c0, w_out):
            for i in range(3):
                chunk(f"gate{l}{i}", [w[:, :, c0 + 512 * i:c0 + 512 * i + 512]], 512, 0, 8, 2)
            for i in range(2):
                chunk(f"fin{l}{i}", [tiled(w_out)[:, :, 512 * i:512 * i + 512]], 512, 0, 12, 2)

        AQ = 3 * 1024
        w_a = tiled(A["w_in_a_2"][0])
        memory_chunks(0)
        chunk("qm0", [w_a[:, :, 3 * AQ:3 * AQ + 512]], 512, 0, 8, 2)
        for hp in range(4):
            for g in range(3):
                c = 1024 * g + 256 * hp
                chunk(f"qk{hp}{g}", [w_a[:, :, c:c + 256], w_a[:, :, AQ + c:AQ + c + 256]], 512, 0, 8, 2)
            for h in range(2):
                c = 2 * AQ + 256 * hp + 128 * h
                chunk(f"v{hp}{h}", [w_a[:, :, c + 1024 * g:c + 1024 * g + 128] for g in range(3)], 384, 0, 8, 2)
        gate_chunks(0, w_a, 3 * AQ + 512, A["w_out_a_2"][0])
        w_b = tiled(A["w_in_b_2"][0])
        memory_chunks(1)
        chunk("qm1", [w_b[:, :, 3072:3584]], 512, 0, 8, 2)
        for hh in range(2):
            for i, nm in enumerate("qfv"):
                c = 1024 * i + 512 * hh
                chunk(f"{nm}l{hh}", [w_b[:, :, c:c + 512]], 512, 0, 8, 2)
        gate_chunks(1, w_b, 3584, A["w_out_b_2"][0])
        NP = len(pieces)
        bank_uses = [[sum(c["nt"] > t for c in chunks[:j]) for t in range(NT)] for j in range(len(chunks) + 1)]
        readies = [sum(c["nt"] - 1 for c in chunks[:j]) for j in range(len(chunks) + 1)]

        def slot_cols(p):
            return PIECE if pieces[p] is None else pieces[p][1] * pieces[p][2]

        TPU, ntp = {}, [0]

        def tpu(name, n):
            TPU[name] = ntp[0]
            ntp[0] += n

        for name, n in (("n1", 8), ("cq", 3), ("qa", 8), ("ckv", 2), ("ka", 8), ("mla", 32), ("oa", 4),
                        ("qkb", 8), ("qi", 4), ("ki", 1), ("dsa", 32), ("ob", 4), ("y", 8), ("h2", 8)):
            tpu(name, n)
        ntp[0] += ntp[0] % 2
        assert ntp[0] == TPU["h2"] + 8, "an even start keeps the loop's bank parity"
        tpu("moe", 2 * NGRP)
        tpu("n2", 8)

        def mem_units(l):
            for name, n in ((f"mem{l}", 8), (f"km{l}", 4), (f"qm{l}", 4), (f"mat{l}", 16)):
                tpu(name, n)
        mem_units(0)
        for hp in range(4):
            tpu(f"qk{hp}", 12)
            tpu(f"dil{hp}", 16)
        tpu("y0", 12)
        tpu("n3", 8)
        mem_units(1)
        for hh in range(2):
            tpu(f"ql{hh}", 4)
            tpu(f"fl{hh}", 4)
        tpu("y1", 12)
        AU, nau = {}, 0
        for name, n in (("mla", 32), ("dsa", 32), ("mat0", 16), ("dil0", 8), ("dil1", 8), ("dil2", 8),
                        ("dil3", 8), ("mat1", 16)):
            AU[name] = nau
            nau += n

        raw_in = [S(f"raw_in{i}") for i in range(RAW)]
        hi_done, lo_done = S("hi_done"), S("lo_done")
        piece_used = S("piece_used")
        acc_ready = S("acc_ready")
        acc_free = [S(f"acc_free{t}") for t in range(NT)]
        tp_ready = S("tp_ready")
        tp_free = [S(f"tp_free{i}") for i in range(2)]
        act_hi = S("act_hi")
        att_s, att_m, att_p = S("att_s"), S("att_m"), S("att_p")
        att_t, att_r, att_o, att_done = S("att_t"), S("att_r"), S("att_o"), S("att_done")
        phase = S("phase")

        xr = take(4096, NT, D)
        cqkv = view(phase0, 2688, NT, 672)
        top[0] = phase0 + 4096
        qk_tok = take(3072, NT, H8, 96)
        qaT = take(4096, H8, T)
        kaT = take(4096, H8, T)
        v_a = take(2048, NT, 512)
        work = take(3072)
        att_s_sb = [work[:, 512 * i:512 * i + 512] for i in range(4)]
        att_pt = [work[:, 2048:2560], work[:, 2560:3072]]
        o_tok = qk_tok.rearrange("p a b c -> p (a b c)")[:, 0:2048].rearrange("p (t c) -> p t c", t=NT)
        ropetmp = work[:, 0:2048]
        a0 = phase0
        qkvb = view(a0, 6144, NT, 1536)
        idx = view(a0 + 6144, 2336, NT, 584)
        score = view(a0 + 6144, 1536, 3, 512)
        qkbT = view(a0 + 8480, 4096, 8, T)
        qiT = view(a0 + 12576, 2048, 4, T)
        kiT = view(a0 + 14624, 512)
        o_tokb = qkvb[:, :, 0:512]
        y_pos = a0 + 8480 + 4096 + 2048 + 512
        y1 = view(y_pos, 4096, NT, D)
        gb = view(a0 + 8480, 4096, NT, D)
        x1 = view(a0, 4096, NT, D)
        work2 = view(y_pos + 4096, 3072)
        assert y_pos + 4096 + 3072 <= n_arena
        s_sb2 = [work2[:, 512 * i:512 * i + 512] for i in range(4)]
        pt2 = [work2[:, 2048:2560], work2[:, 2560:3072]]
        rel = [work2[:, 0:512], work2[:, 512:1024]]
        tk = work2[:, 1024:1536]
        kidup = work2[:, 2048:2560].rearrange("p (t c) -> p t c", t=NT)
        ropetmp2 = work2[:, 0:3072]
        wi_s = stat(32).rearrange("p (t h) -> p t h", t=NT)
        max8 = stat(8)

        def norm_cols(n):
            return dict(ss=stat(n), ms=stat(n), rt=stat(n), rs=stat(n))

        ns = {name: norm_cols(4) for name in ("n1", "cq", "ckv", "ffn", "final", "n2", "n3")}
        for l in range(2):
            ns[f"mem{l}"] = norm_cols(2)
            ns[f"km{l}"] = norm_cols(8)
            ns[f"qm{l}"] = norm_cols(16)
        qk_n = norm_cols(16)
        qk_rs = stat(3 * NT * 4).rearrange("p (g t c) -> p g t c", g=3, t=NT)
        gl_n = norm_cols(32)
        att_mx, att_nm, att_l, att_rl = stat(12), stat(4), stat(4), stat(4)

        w_slot = lambda buf, p, i: buf[:, i, 0:slot_cols(p)]

        def mla_unit(i):
            h, qt = i // NT, i % NT
            kw = P * (qt + 1)
            return dict(s=[(0, qaT[0:96, h, qt * P:qt * P + P], kaT[0:96, h, 0:kw], cmask[:, 512 - kw:512], 96 ** -0.5)],
                        kw=kw, v=[v_a[:, b, 64 * h:64 * h + 64] for b in range(qt + 1)],
                        dv=64, o=o_tok[:, qt, 64 * h:64 * h + 64], sb=att_s_sb, pt=att_pt, look=LOOK)

        def dsa_unit(i):
            h, qt = i // NT, i % NT
            kw = P * (qt + 1)
            r0 = 64 * (h % 2)
            mask = cmask[:, 384:512] if qt == 0 else score[:, qt - 1, 0:kw]
            return dict(s=[(0, qkbT[r0:r0 + 64, h // 2, qt * P:qt * P + P], qkbT[r0:r0 + 64, 4 + h // 2, 0:kw], mask, 0.125)],
                        kw=kw, v=[qkvb[:, b, 1024 + 64 * h:1088 + 64 * h] for b in range(qt + 1)],
                        dv=64, o=o_tokb[:, qt, 64 * h:64 * h + 64], sb=s_sb2, pt=pt2, look=LOOK)

        top[0] = a0 + 4096
        c_moe = take(C_MOE - C_BASE)
        before, iota_g, iota_s, iota_p = (const(k, c_moe, C_BASE) for k in ("before", "iota_g", "iota_s", "iota_p"))
        h2T = take(4096, KD, T)
        w_rt = take(KD * 40, KD, 40)
        b_rt = take(40)
        lg = take(NT * 40, NT, 40)
        rt = take(1200)
        key = take(NT)
        keyb = take(NT * P, NT, P)
        keyrow = take(T)
        comb4 = take(NT * EPG, NT, EPG)
        comb32 = take(NT * 32, NT, 32)
        wslot = take(EPG)
        sg_sb = [take(FF) for _ in range(2)]
        hid_sb = [take(FF) for _ in range(2)]
        fin_g = take(D)
        big = take(4096)
        bigt = big.rearrange("p (t d) -> p t d", t=NT)
        rt_at = [0]

        def route(*shape):
            n = int(np.prod(shape))
            a = rt[:, rt_at[0]:rt_at[0] + n]
            rt_at[0] += n
            assert rt_at[0] <= 1200
            names = "abc"[:len(shape)]
            return a if len(shape) == 1 else a.rearrange("p (" + " ".join(names) + ") -> p " + " ".join(names),
                                                         **dict(zip(names, shape)))

        r_gmax, r_gi, r_m1, r_m2, r_min4, r_d2, r_e2, r_sum, r_w1, r_w2, r_rank, r_over = (route(NT) for _ in range(12))
        r_d, r_e, r_eq, r_cand, oneh = (route(NT, 8) for _ in range(5))
        r_in4, r_in4b, r_eq4, r_cand4, r_oh1, r_oh2 = (route(NT, EPG) for _ in range(6))
        r_el = route(NT, 8, EPG)
        gen_gu = big.rearrange("p (w k f) -> p w k f", w=2, k=KD)
        gen_d = take(2048, 2, D)
        gen_sil = take(1024, 2, T)
        gen_hid = take(1024, 2, T)
        xs_hi = AT_hi[:, 0:8, :].rearrange("p a b -> p (a b)").rearrange("p (t d) -> p t d", t=NT)
        xs_lo = AT_lo[:, 0:8, :].rearrange("p a b -> p (a b)").rearrange("p (t d) -> p t d", t=NT)
        spare_hi = AT_hi[:, 8:12, :].rearrange("p a b -> p (a b)")
        spare_lo = AT_lo[:, 8:12, :].rearrange("p a b -> p (a b)")
        xg_hi = spare_hi[:, 0:1024].rearrange("p (k s) -> p k s", k=KD)
        xg_lo = spare_lo[:, 0:1024].rearrange("p (k s) -> p k s", k=KD)
        hd_hi = [spare_hi[:, 1024 + 256 * i:1280 + 256 * i] for i in range(2)]
        hd_lo = [spare_lo[:, 1024 + 256 * i:1280 + 256 * i] for i in range(2)]
        pick = spare_hi[:, 1536:2048].rearrange("p (t s) -> p t s", t=NT)
        put = spare_lo[:, 1536:2048]
        w_g_e = A["w_gate"][0].rearrange("e (k p) f -> e p k f", p=P)
        w_u_e = A["w_up"][0].rearrange("e (k p) f -> e p k f", p=P)
        w_d_e = A["w_down"][0].rearrange("e (k p) d -> e p k d", p=P)

        top[0] = phase0
        mix = take(6144, NT, 1536)
        l2_0 = top[0]
        memx = take(2048, 2, D)
        km_tok = take(1024, 2, 512)
        vm = take(1024, 2, 512)
        kmT = take(1024, MH, MEM)
        qm_tok = take(2048, NT, 512)
        qmT = take(2048, MH, T)
        mg = take(256)
        mwork = take(2048)
        ms_sb = [mwork[:, 256 * i:256 * i + 256] for i in range(4)]
        mpt = [mwork[:, 1024:1280], mwork[:, 1280:1536]]
        msq = mwork[:, 1536:2048]
        xn = take(4096, NT, D)
        junkD = km_tok.rearrange("p a b -> p (a b)")
        mjunk = mwork[:, 0:1024]
        top[0] = l2_0
        c_dil = take(C_DIL - C_MOE)
        wmask, dmask, inv2 = (const(k, c_dil, C_MOE) for k in ("wmask", "dmask", "inv2"))
        qkg = take(768, 3, 2, P)
        cos2 = take(64, NT, 16)
        sin2 = take(64, NT, 16)
        qT = take(3072, 3, 2, T)
        kT = take(3072, 3, 2, T)
        v2 = take(3072, NT, 2, 3 * P)
        qk_t = take(2048, NT, 512)
        d_s = [take(768) for _ in range(2)]
        d_pt = [take(768)]
        rtmp = take(768)
        sqb = d_s[0][:, 0:512]
        rot_r, rot_c, rot_a, rot_k = (rtmp[:, 64 * i:64 * i + 64].rearrange("p (t c) -> p t c", t=NT) for i in range(4))
        rot_p = rtmp[:, 256:256 + NT]
        junkE = qk_t.rearrange("p a b -> p (a b)")[:, 0:1024]
        n3x = view(phase0, 4096, NT, D)
        res2 = view(l2_0 + (C_DIL - C_MOE) + 896, 4096, NT, D)
        silu_sb = [d_s[0][:, 0:512], d_s[1][:, 0:512]]
        dil_end = top[0]
        top[0] = l2_0
        c_gla = take(C_ALL - C_DIL)
        lmask, seg = (const(k, c_gla, C_DIL) for k in ("lmask", "seg"))
        lmask = lmask.rearrange("p (l c) -> p l c", c=P)
        og = take(P)
        lbl = take(16, 2, 8)
        lb = take(8)
        lb1 = take(8)
        at_ltok = top[0]
        l_tok = take(2048, NT, 512)
        lA = l_tok.rearrange("p a b -> p (a b)").rearrange("p (s t) -> p s t", s=NT)
        at_lq = top[0]
        lq = take(2048, 4, T)
        lk = take(2048, 4, T)
        lf = take(2048, 4, T)
        lv = take(2048, NT, 512)
        G64 = take(T)
        G512 = take(T)
        lexp = [take(T) for _ in range(2)]
        qe = [take(T) for _ in range(2)]
        ke = [take(T) for _ in range(2)]
        res3 = view(at_lq + 2048, 4096, NT, D)
        lsq = view(at_lq, 2048, 2, D)
        silu3 = [lsq[:, i, 0:512] for i in range(2)]

        def AT_perm(a, k):
            return a[:, k, :].rearrange("p (r t q) -> p t q r", r=4, t=NT)

        def mem_unit(i):
            h, qt = i // NT, i % NT
            return dict(s=[(0, qmT[:, h, qt * P:qt * P + P], kmT[:, h, :], None, HD ** -0.5)], kw=MEM,
                        v=[vm[:, b, P * h:P * h + P] for b in range(2)], dv=P,
                        o=mix[:, qt, 1024 + P * h:1152 + P * h], sb=ms_sb, pt=mpt, look=LOOK)

        def dil_unit(hp, i):
            h, r = i // NT, i % NT
            q = lambda g: qT[:, g, h, r * P:r * P + P]
            sc = lambda g: qk_rs[:, g, r, h:h + 1]
            return dict(s=[(0, q(0), kT[:, 0, h, :], wmask[:, (3 - r) * P:(7 - r) * P], sc(0)),
                           (512, q(1), kT[:, 1, h, r * P:r * P + P], dmask[:, 0:P], sc(1)),
                           (640, q(2), kT[:, 2, h, r * P:r * P + P], dmask[:, P:2 * P], sc(2))],
                        kw=768, v=[v2[:, b, h, 0:P] for b in range(4)] + [v2[:, r, h, P:2 * P], v2[:, r, h, 2 * P:3 * P]],
                        dv=P, o=mix[:, r, P * (2 * hp + h):P * (2 * hp + h) + P], sb=d_s, pt=d_pt, look=1)


        LOOK = 3

        def scores_out(u, off, n, wide=False):
            if wide:
                return ACC[u % 2][:, off:off + n] if off < 512 else ACC[2 + u % 2][:, off - 512:off - 512 + n]
            return ACC[u % 4][:, off:off + n]

        block = ctx.enter_context(nc.Block())

        @block.sync
        def _(sp):
            for t in range(NT):
                sp.dma_start(xr[:, t, :], A["x"][0, t * P:t * P + P, :]).then_inc(S(f"x_in{t}"), 16)

            def load(p):
                loads, per, n = pieces[p]
                if p >= RAW:
                    sp.wait_ge(lo_done, p - RAW + 1)
                dst = wraw[:, p % RAW, 0:per * n].rearrange("p (k n) -> p k n", k=per)
                share = 96 // len(loads)
                for c0, w, src in loads:
                    sp.dma_start(dst[:, :, c0:c0 + w], src).then_inc(raw_in[p % RAW], share)

            for p in range(P_MOE):
                load(p)
            with sp.Fori(0, NGRP) as g:
                for j, (kind, e, q) in enumerate(GROUP_ORDER):
                    p = P_MOE + j
                    one = bass.ds(sp.snap(g * EPG + e), 1)
                    sp.wait_ge(lo_done, g * PPG + (p - RAW + 1))
                    if kind == "gu":
                        dst = wraw[:, p % RAW, :].rearrange("p (k n) -> p k n", k=2)
                        for i, w in enumerate((w_g_e, w_u_e)):
                            sp.dma_start(dst[:, :, FF * i:FF * i + FF],
                                         w[one, :, 2 * q:2 * q + 2, :].rearrange("e p k f -> p (e k) f")
                                         ).then_inc(raw_in[p % RAW], 48)
                    else:
                        sp.dma_start(wraw[:, p % RAW, :], w_d_e[one, :, q, :].rearrange("e p f -> p (e f)")
                                     ).then_inc(raw_in[p % RAW], 96)
            for p in range(P_MOE + NGRP * PPG, NP):
                load(p)

        NORMS = (("n1", 4, 4, 0), ("cq", 4, 4, 0), ("ckv", 4, 4, 0), ("ffn", 4, 4, 0), ("final", 4, 0, 0), ("n2", 4, 4, 0),
                 ("mem0", 2, 2, 0), ("km0", 0, 8, 2), ("qm0", 0, 16, 4), ("n3", 4, 4, 0), ("mem1", 2, 2, 0), ("km1", 0, 8, 2),
                 ("qm1", 0, 16, 4))
        ORDER = [n[0] for n in NORMS]
        norm_ss, norm_ms, norm_rt, norm_xs = S("norm_ss"), S("norm_ms"), S("norm_rt"), S("norm_xs")
        head_sq, head_red = S("head_sq"), S("head_red")

        def so_far(name, what, n):
            return sum(row[what] for row in NORMS[:ORDER.index(name)]) + n

        def wait_acc(eng, j, t):
            c = chunks[j]
            if t == c["nt"] - 1:
                eng.wait_ge(piece_used, c["first"] + c["count"])
            else:
                eng.wait_ge(acc_ready, readies[j] + t + 1)

        def wait_tp_read(eng, name, n):
            for par in range(2):
                last = max(u for u in range(TPU[name], TPU[name] + n) if u % 2 == par) if n > 1 or TPU[name] % 2 == par else None
                if last is not None:
                    eng.wait_ge(tp_free[par], last // 2 + 1)

        def wait_used(eng, name):
            eng.wait_ge(piece_used, chunks[CH[name]]["first"] + chunks[CH[name]]["count"])

        def wait_read(eng, name, t):
            eng.wait_ge(acc_free[t], bank_uses[CH[name]][t] + 1)

        phases = {"PE": 0, "ACT": 0, "DVE": 0, "POOL": 0}

        def end_phase(eng, who):
            phases[who] += 1
            eng.drain().then_inc(phase, 1)
            eng.wait_ge(phase, 4 * phases[who])

        @block.gpsimd
        def _(pool):
            chain = [0]

            def link(ins):
                chain[0] += 1
                ins.then_inc(S("pool_step"), 1)
                pool.wait_ge(S("pool_step"), chain[0])

            def rope(x1, x2, cos, sin, tmp, shape):
                n = int(np.prod(shape))
                v = [tmp[:, i * n:i * n + n].rearrange("p (t h c) -> p t h c", t=shape[0], h=shape[1]) for i in range(4)]
                bc = lambda a: a.unsqueeze(2).broadcast_to([P] + list(shape))
                c, s = bc(cos), bc(sin)
                pool.tensor_tensor(v[0], x1, c, ALU.mult)
                pool.tensor_tensor(v[1], x2, s, ALU.mult)
                pool.tensor_tensor(v[2], x2, c, ALU.mult)
                link(pool.tensor_tensor(v[3], x1, s, ALU.mult))
                pool.tensor_tensor(x1, v[0], v[1], ALU.subtract)
                return pool.tensor_tensor(x2, v[2], v[3], ALU.add)

            pool.wait_ge(S("consts"), 16)

            def load_memory(l):
                pool.dma_start(memx, A["mem_2"][0].rearrange("(t p) d -> p t d", p=P)).then_inc(S(f"memx{l}"), 16)
                for i, w in enumerate(("mem_q_gain_2", "mem_k_gain_2")):
                    pool.dma_start(mg[:, P * i:P * i + P], A[w][l:l + 1, :].broadcast_to([P, P])).then_inc(S(f"memx{l}"), 16)

            for i in range(2):
                for t in range(NT):
                    wait_read(pool, f"uq{i}", t)
                q = qk_tok[:, :, 4 * i:4 * i + 4, :]
                for t in range(NT):
                    r = rope(q[:, t:t + 1, :, 64:80], q[:, t:t + 1, :, 80:96], ropeA[0][:, t:t + 1], ropeA[1][:, t:t + 1],
                             ropetmp[:, 256 * t:256 * t + 256], (1, 4, 16))
                r.then_inc(S("qa_rot"), 1)
            kr = cqkv[:, :, 640:672].unsqueeze(2)
            link(rope(kr[:, :, :, 0:16], kr[:, :, :, 16:32], ropeA[0], ropeA[1], ropetmp[:, 1024:1280], (NT, 1, 16)))
            wait_tp_read(pool, "qa", 8)
            for t in range(NT):
                pool.tensor_copy(qk_tok[:, t, :, 64:96],
                                 kr[:, t, :, :].broadcast_to([P, H8, 32])).then_inc(S("ka_rot"), 1)
            end_phase(pool, "POOL")

            for tok, n, last in ((idx, 9, "idx1"), (qkvb, 16, "qkvb2")):
                for t in range(NT):
                    wait_read(pool, last, t)
                x = tok[:, :, 0:64 * n].rearrange("p t (h c) -> p t h c", h=n)
                for t in range(NT):
                    r = rope(x[:, t:t + 1, :, 0:8], x[:, t:t + 1, :, 8:16], ropeB[0][:, t:t + 1], ropeB[1][:, t:t + 1],
                             ropetmp2[:, 512 * t:512 * t + 512], (1, n, 8))
                link(r)
                if tok is idx:
                    for half in range(2):
                        pool.tensor_copy(kidup[:, :, 64 * half:64 * half + 64], idx[:, :, 512:576])
                    r = pool.tensor_scalar(wi_s, idx[:, :, 576:584], H8 ** -0.5, None, ALU.mult)
                else:
                    r = pool.nop()
                r.then_inc(S("b_rot"), 1)
            wait_tp_read(pool, "ob", 4)
            pool.dma_start(x1, A["x"][0].rearrange("(t p) d -> p t d", p=P)).then_inc(S("res1"), 16)
            pool.wait_ge(S("res1"), 16)
            end_phase(pool, "POOL")

            pool.dma_start(c_moe, A["const"][:, C_BASE:C_MOE]).then_inc(S("moe_in"), 16)
            pool.dma_start(w_rt[:, :, 0:8], tiled(A["w_router_group"][0])).then_inc(S("moe_in"), 16)
            pool.dma_start(w_rt[:, :, 8:40], tiled(A["w_router_expert"][0])).then_inc(S("moe_in"), 16)
            pool.dma_start(b_rt[:, 0:8], A["b_router_group"][0:1, :].broadcast_to([P, 8])).then_inc(S("moe_in"), 16)
            pool.dma_start(b_rt[:, 8:40], A["b_router_expert"][0:1, :].broadcast_to([P, 32])).then_inc(S("moe_in"), 16)
            pool.dma_start(fin_g, A["final_norm_g"].unsqueeze(0).broadcast_to([P, D])).then_inc(S("moe_in"), 16)
            pool.wait_ge(S("moe_in"), 96)
            pool.wait_ge(S("flag_in"), 1)
            pool.wait_ge(S("moe_end"), 1)
            with pool.If(pool.value_load(flag[0:1, 0:1], min_val=0, max_val=T) > 0):
                with pool.Fori(0, NGRP * EPG) as e:
                    one = bass.ds(e, 1)
                    pool.wait_ge(S("gen_y"), e * 8 + 8)
                    pool.dma_start(gen_gu[:, 0, :, :], w_g_e[one].rearrange("e p k f -> p (e k) f")).then_inc(S("gen_in"), 16)
                    pool.dma_start(gen_gu[:, 1, :, :], w_u_e[one].rearrange("e p k f -> p (e k) f")).then_inc(S("gen_in"), 16)
                    pool.dma_start(gen_d, w_d_e[one].rearrange("e p k f -> p (e k) f")).then_inc(S("gen_in"), 16)
            end_phase(pool, "POOL")

            load_memory(0)
            for t in range(NT):
                pool.wait_ge(S("fin_x"), t + 1)
                pool.dma_start(x_mid[t * P:t * P + P, :], xn[:, t, :]).then_inc(S("mid_out"), 16)
            pool.wait_ge(S("mid_out"), 16 * NT)
            end_phase(pool, "POOL")

            pool.dma_start(c_dil, A["const"][:, C_MOE:C_DIL]).then_inc(S("dil_in"), 16)
            for i, w in enumerate(("q_gain_a_2", "k_gain_a_2")):
                pool.dma_start(qkg[:, :, i, :], A[w][0:1].broadcast_to([P, 3, P])).then_inc(S("dil_in"), 16)
            pool.dma_start(posi[:, :], A["positions_2"].rearrange("o (p r) -> (o p) r", r=4)).then_inc(S("dil_in"), 16)
            pool.wait_ge(S("rot2"), 1)
            for n in range(12):
                pool.wait_ge(S("qk_rs"), n + 1)
                for t in range(NT):
                    k = qk_t[:, t, 256:512].rearrange("p (h c) -> p h c", h=2)
                    r = pool.tensor_tensor(k, k, qk_rs[:, n % 3, t, 2:4].unsqueeze(2).broadcast_to([P, 2, P]), ALU.mult)
                link(r)
                for t in range(NT):
                    x = qk_t[:, t:t + 1, :].rearrange("p t (h c) -> p t h c", h=4)
                    r = rope(x[:, :, :, 0:16], x[:, :, :, 16:32], cos2[:, t:t + 1], sin2[:, t:t + 1],
                             rtmp[:, 256 * (t % 3):256 * (t % 3) + 256], (1, 4, 16))
                r.then_inc(S("qk_rot"), 1)
            end_phase(pool, "POOL")
            for r in range(NT):
                pool.dma_start(res2[:, r, :], x_mid.rearrange("(p r) d -> r p d", r=4)[r]).then_inc(S("res2"), 16)
            for r in range(NT):
                wait_read(pool, "fin01", r)
                pool.dma_start(x_mid2.rearrange("(p r) d -> r p d", r=4)[r], res2[:, r, :]).then_inc(S("mid_out2"), 16)
            pool.wait_ge(S("mid_out2"), 16 * NT)
            end_phase(pool, "POOL")

            load_memory(1)
            end_phase(pool, "POOL")

            pool.dma_start(c_gla, A["const"][:, C_DIL:C_ALL]).then_inc(S("gla_in"), 16)
            pool.dma_start(og, A["o_gain_b_2"][0:1, :].broadcast_to([P, P])).then_inc(S("gla_in"), 16)
            with nc.allow_non_contiguous_dma(reason="a column of lower bounds for each head"):
                for i in range(2):
                    pool.dma_start(lbl[:, i, :], A["lb_logits_2"][i].rearrange("(h c) -> c h", c=P)).then_inc(S("gla_in"), 16)
            for b in qe + ke:
                r = pool.memset(b, 0.0)
            r.then_inc(S("gla_zero"), 1)
            for hh in range(2):
                wait_tp_read(pool, f"fl{hh}", 4)
                pool.memset(lA, 0.0).then_inc(S("lA_zero"), 1)
            end_phase(pool, "POOL")
            pool.dma_start(res3, x_mid2.rearrange("(t p) d -> p t d", p=P)).then_inc(S("res3"), 16)
            for t in range(NT):
                wait_read(pool, "fin11", t)
                pool.dma_start(out[0, t * P:t * P + P, :], res3[:, t, :]).then_inc(S("out_done"), 16)
            pool.wait_ge(S("out_done"), 16 * NT)

        @block.scalar
        def _(act):
            his = [0]

            def feed(p):
                if p >= NP:
                    return
                act.wait_ge(raw_in[p % RAW], 96 * (p // RAW + 1))
                if p >= SPL:
                    act.wait_ge(piece_used, p - SPL + 1)
                act.activation(w_slot(whi, p, p % SPL), w_slot(wraw, p, p % RAW), ACT.Copy).then_inc(hi_done, 1)

            def during(j):
                for i in range(chunks[j]["count"] - 1):
                    feed(chunks[j]["first"] + i + SPL)

            def after(j):
                feed(chunks[j]["first"] + chunks[j]["count"] - 1 + SPL)

            def evac(name, dst, func=ACT.Copy, scale=1.0):
                j = CH[name]
                during(j)
                for t in range(chunks[j]["nt"]):
                    wait_acc(act, j, t)
                    src = ACC[t][:, 0:chunks[j]["n"]]
                    d = dst(t)
                    if len(d.shape) == 3:
                        src = src.rearrange("p (h c) -> p h c", h=d.shape[1])
                    act.activation(d, src, func, scale=scale).then_inc(acc_free[t], 1)
                after(j)

            def hi(name, i, dst, src, gain=None):
                act.wait_ge(tp_ready, TPU[name] + i + 1)
                act.activation(dst, src, ACT.Copy, scale=1.0 if gain is None else gain).then_inc(act_hi, 1)

            def tcopy(name, i, dst, src, scale=1.0):
                u = TPU[name] + i
                act.wait_ge(tp_ready, u + 1)
                act.activation(dst, src, ACT.Copy, scale=scale).then_inc(tp_free[u % 2], 1)

            def tb(name, i):
                return TP[(TPU[name] + i) % 2]

            def sumsq(src, junk, ss, name, t):
                if t:
                    act.wait_ge(norm_ss, so_far(name, 1, t))
                act.activation(junk, src, ACT.Square, accum_out=ss).then_inc(norm_ss, 1)

            def root(name, c):
                act.wait_ge(norm_ms, ORDER.index(name) + 1)
                act.activation(c["rt"], c["ms"], ACT.Sqrt).then_inc(norm_rt, 1)

            def attention(name, unit, n):
                U0 = AU[name]

                def out_of_psum(i):
                    u = unit(i)
                    U = U0 + i
                    act.wait_ge(att_o, U + 1)
                    act.wait_ge(att_r, U + 1)
                    act.activation(u["o"], SC[U % 2][:, 0:u["dv"]], ACT.Copy, scale=att_rl[:, U % 4:U % 4 + 1]
                                   ).then_inc(att_done, 1)

                def exponentials(i):
                    u = unit(i)
                    U = U0 + i
                    act.wait_ge(att_m, U + 1)
                    s = u["sb"][U % len(u["sb"])][:, 0:u["kw"]]
                    masked = u["s"][0][3] is not None
                    act.activation(s, s if masked else scores_out(U, 0, u["kw"]), ACT.Exp, bias=att_nm[:, U % 4:U % 4 + 1],
                                   scale=1.0 if masked else u["s"][0][4],
                                   accum_out=att_l[:, U % 4:U % 4 + 1]).then_inc(att_p, 1)

                for i in range(n + 2):
                    if i < n:
                        exponentials(i)
                    if i >= 2:
                        out_of_psum(i - 2)

            def head_norm(name, chunk, tok, nt, dst, sq):
                for t in range(nt):
                    if t:
                        act.wait_ge(head_red, so_far(name, 3, t))
                    wait_read(act, chunk, t)
                    act.activation(sq, tok[:, t, :], ACT.Square).then_inc(head_sq, 1)
                root(name, dst)

            def memory_stage(l):
                act.wait_ge(S(f"memx{l}"), 48)
                for t in range(2):
                    sumsq(memx[:, t, :], mjunk, ns[f"mem{l}"]["ss"][:, t:t + 1], f"mem{l}", t)
                root(f"mem{l}", ns[f"mem{l}"])
                for k in range(KD):
                    hi(f"mem{l}", k, AT_mem_hi[:, k, :], tb(f"mem{l}", k)[:, 0:MEM], g_mem[l][:, k:k + 1])
                evac(f"mkv{l}0", lambda t: km_tok[:, t, :])
                head_norm(f"km{l}", f"mkv{l}0", km_tok, 2, ns[f"km{l}"], msq)
                evac(f"mkv{l}1", lambda t: vm[:, t, :])
                for h in range(MH):
                    tcopy(f"km{l}", h, kmT[:, h, :], tb(f"km{l}", h)[:, 0:MEM])
                evac(f"qm{l}", lambda t: qm_tok[:, t, :])
                head_norm(f"qm{l}", f"qm{l}", qm_tok, NT, ns[f"qm{l}"], msq)
                for h in range(MH):
                    tcopy(f"qm{l}", h, qmT[:, h, :], tb(f"qm{l}", h))
                attention(f"mat{l}", mem_unit, 16)

            def gates(l, tmp):
                for i in range(3):
                    j = CH[f"gate{l}{i}"]
                    during(j)
                    for t in range(NT):
                        n = NT * i + t
                        wait_acc(act, j, t)
                        if n >= 2:
                            act.wait_ge(S(f"gated{l}"), n - 1)
                        act.activation(tmp[n % 2], ACC[t][:, :], ACT.Silu).then_inc(acc_free[t], 1)
                    after(j)
                wait_used(act, f"gate{l}2")
                for k in range(12):
                    hi(f"y{l}", k, AT_hi[:, k, :], tb(f"y{l}", k))
                for i in range(2):
                    j = CH[f"fin{l}{i}"]
                    during(j)
                    after(j)

            act.dma_start(base0, A["const"][:, 0:C_BASE]).then_inc(S("consts"), 16)
            with nc.allow_non_contiguous_dma(reason="gains as columns"):
                for dst, src in ((g_mix, A["norm_mix_g"][0]), (g_cq, A["mla_q_norm_g"][0]), (g_ckv, A["mla_kv_norm_g"][0]),
                                 (g_ffn, A["norm_ffn_g"][0]), (g_n2[0], A["norm_gain_2"][0]), (g_n2[1], A["norm_gain_2"][1]),
                                 (g_mem[0], A["mem_norm_gain_2"][0]), (g_mem[1], A["mem_norm_gain_2"][1])):
                    act.dma_start(dst, src.rearrange("(k p) -> p k", p=P)).then_inc(S("gains_in"), 16)
            for p in range(SPL):
                feed(p)
            for t in range(NT):
                act.wait_ge(S(f"x_in{t}"), 16)
                sumsq(xr[:, t, :], work[:, 0:1024], ns["n1"]["ss"][:, t:t + 1], "n1", t)
            root("n1", ns["n1"])
            act.wait_ge(S("gains_in"), 128)
            for k in range(KD):
                hi("n1", k, AT_hi[:, k, :], tb("n1", k), g_mix[:, k:k + 1])
            for i in range(2):
                evac(f"cqkv{i}", lambda t: cqkv[:, t, 336 * i:336 * i + 336])
            for name, c0, w in (("cq", 0, 384), ("ckv", 384, 256)):
                for t in range(NT):
                    act.wait_ge(acc_free[t], 2)
                    sumsq(cqkv[:, t, c0:c0 + w], work[:, 0:w], ns[name]["ss"][:, t:t + 1], name, t)
                root(name, ns[name])
            for k in range(3):
                hi("cq", k, AT_hi[:, 8 + k, :], tb("cq", k), g_cq[:, k:k + 1])
            for i in range(2):
                evac(f"uq{i}", lambda t: qk_tok[:, t, 4 * i:4 * i + 4, :])
            for h in range(H8):
                tcopy("qa", h, qaT[0:96, h, :], tb("qa", h)[0:96, :])
            wait_used(act, "uq1")
            for k in range(2):
                hi("ckv", k, AT_hi[:, 8 + k, :], tb("ckv", k), g_ckv[:, k:k + 1])
            evac("uk", lambda t: qk_tok[:, t, :, 0:64])
            evac("uv", lambda t: v_a[:, t, :])
            for h in range(H8):
                tcopy("ka", h, kaT[0:96, h, :], tb("ka", h)[0:96, :])
            attention("mla", mla_unit, 32)
            for k in range(4):
                hi("oa", k, AT_hi[:, 8 + k, :], tb("oa", k))
            end_phase(act, "ACT")

            for name, tok, c0 in (("idx0", idx, 0), ("idx1", idx, 292), ("qkvb0", qkvb, 0), ("qkvb1", qkvb, 512),
                                  ("qkvb2", qkvb, 1024)):
                evac(name, lambda t: tok[:, t, c0:c0 + chunks[CH[name]]["n"]])
            for i in range(2):
                evac(f"ga{i}", lambda t: y1[:, t, 512 * i:512 * i + 512], ACT.Sigmoid)
            for i in range(2):
                during(CH[f"oa{i}"])
                after(CH[f"oa{i}"])
            for i in range(8):
                tcopy("qkb", i, qkbT[:, i, :], tb("qkb", i))
            for i in range(4):
                tcopy("qi", i, qiT[:, i, :], tb("qi", i))
            tcopy("ki", 0, kiT, tb("ki", 0))
            for n in range(24):
                kw = P * (n // 8 + 2)
                act.wait_ge(S("idx_mm"), n + 1)
                if n >= 2:
                    act.wait_ge(S("idx_add"), n - 1)
                act.activation(rel[n % 2][:, 0:kw], SC[n % 2][:, 0:kw], ACT.Relu, scale=0.125).then_inc(S("idx_relu"), 1)
            attention("dsa", dsa_unit, 32)
            for i in range(2):
                evac(f"gb{i}", lambda t: gb[:, t, 512 * i:512 * i + 512], ACT.Sigmoid)
            wait_used(act, "oa1")
            for k in range(4):
                hi("ob", k, AT_hi[:, 8 + k, :], tb("ob", k))
            for i in range(2):
                during(CH[f"ob{i}"])
                after(CH[f"ob{i}"])
            wait_used(act, "gb1")
            for k in range(KD):
                hi("y", k, AT_hi[:, k, :], tb("y", k))
            for i in range(2):
                during(CH[f"out{i}"])
                after(CH[f"out{i}"])
            end_phase(act, "ACT")

            for t in range(NT):
                sumsq(x1[:, t, :], big[:, 0:1024], ns["ffn"]["ss"][:, t:t + 1], "ffn", t)
            root("ffn", ns["ffn"])
            for t in range(NT):
                act.wait_ge(norm_xs, so_far("ffn", 2, t + 1))
                act.activation(xs_hi[:, t, :], bigt[:, t, :], ACT.Copy).then_inc(S("xs_hi"), 1)
            for k in range(KD):
                tcopy("h2", k, h2T[:, k, :], tb("h2", k), g_ffn[:, k:k + 1])
            act.wait_ge(S("rt_exp"), 1)
            act.activation(r_e, r_d, ACT.Exp).then_inc(S("rt_exp_done"), 1)
            act.wait_ge(S("rt_exp"), 2)
            act.activation(r_e2, r_d2, ACT.Exp).then_inc(S("rt_exp_done"), 1)
            act.wait_ge(S("rt_comb"), 1)
            act.activation(comb_s[:, :, 0:4], comb4, ACT.Copy).then_inc(S("comb_hi"), 1)
            act.wait_ge(S("key_mm"), 1)
            act.activation(keyrow, ACC[2], ACT.Copy).then_inc(S("key_row"), 1)
            def feed_in(g, j):
                p = P_MOE + j + SPL
                if isinstance(g, int):
                    return feed(g * PPG + p)
                act.wait_ge(raw_in[p % RAW], g * (96 * PPG // RAW) + 96 * (p // RAW + 1))
                act.wait_ge(piece_used, g * PPG + (P_MOE + j + 1))
                act.activation(whi[:, p % SPL, :], wraw[:, p % RAW, :], ACT.Copy).then_inc(hi_done, 1)

            def feeds(g, kind, e, qs):
                for q in qs:
                    feed_in(g, piece_of[kind, e, q])

            def gathered(g, i):
                act.wait_ge(tp_ready, g * 2 + (TPU["moe"] + i + 1))
                for k in range(4):
                    r = act.activation(xg_hi[:, 4 * i + k, :], TP[i][:, k * P:k * P + P], ACT.Copy,
                                       scale=g_ffn[:, 4 * i + k:4 * i + k + 1])
                r.then_inc(act_hi, 1)

            def silu(g, e):
                act.wait_ge(piece_used, g * PPG + (P_MOE + piece_of["gu", e, 3] + 1))
                act.wait_ge(S("hid_done"), g * EPG + (e + 1))
                act.activation(sg_sb[e % 2], ACC[e % 2][:, 0:FF], ACT.Silu).then_inc(S("silu"), 1)

            def hidden_hi(g, e):
                act.wait_ge(S("hd_t"), g * EPG + (e + 1))
                act.activation(hd_hi[e % 2], SC[e % 2][:, 0:FF], ACT.Copy).then_inc(S("hd_hi"), 1)

            def first_expert(g):
                feeds(g, "gu", 0, (0, 1, 2))
                silu(g, 0)
                feeds(g, "gu", 0, (3,))

            def group(g, last):
                for e in (1, 2, 3):
                    feeds(g, "gu", e, (0, 1, 2))
                    silu(g, e)
                    feeds(g, "gu", e, (3,))
                    hidden_hi(g, e - 1)
                    if e < 3:
                        feeds(g, "dn", e - 1, (0, 1))
                if not last:
                    gathered(g + 1, 0)
                feeds(g, "dn", 2, (0, 1))
                hidden_hi(g, 3)
                if not last:
                    gathered(g + 1, 1)
                feeds(g, "dn", 3, (0,))
                act.wait_ge(piece_used, g * PPG + (P_MOE + PPG))
                act.wait_ge(S("sc_ready"), g * 8 + 1)
                for n in range(2):
                    act.activation(y_hi[:, 512 * n:512 * n + 512], ACC[2 + n], ACT.Copy).then_inc(S("y_hi"), 1)
                feeds(g, "dn", 3, (1,))
                if not last:
                    first_expert(g + 1)

            gathered(0, 0)
            gathered(0, 1)
            first_expert(0)
            with act.Fori(0, NGRP - 1) as g:
                group(g, False)
            group(NGRP - 1, True)
            act.wait_ge(S("flag_in"), 1)
            with act.If(act.value_load(flag[0:1, 0:1], min_val=0, max_val=T) > 0):
                with act.Fori(0, NGRP * EPG) as e:
                    act.wait_ge(S("gen_gu"), e + 1)
                    act.wait_ge(S("gen_hid"), e + 1)
                    act.activation(gen_sil[:, 0, :], ACC[0], ACT.Silu)
                    act.activation(gen_sil[:, 1, :], ACC[1], ACT.Silu).then_inc(S("gen_silu"), 1)
            end_phase(act, "ACT")

            for t in range(NT):
                sumsq(x1[:, t, :], junkD, ns["final"]["ss"][:, t:t + 1], "final", t)
            root("final", ns["final"])
            for t in range(NT):
                act.wait_ge(S("fin_x"), t + 1)
                sumsq(xn[:, t, :], junkD, ns["n2"]["ss"][:, t:t + 1], "n2", t)
            root("n2", ns["n2"])
            for k in range(KD):
                hi("n2", k, AT_perm(AT_hi, k), tb("n2", k).rearrange("p (t q r) -> p t q r", t=NT, r=4), g_n2[0][:, k:k + 1])
            memory_stage(0)
            end_phase(act, "ACT")

            act.wait_ge(S("rot_ang"), 1)
            act.activation(sin2, rot_r, ACT.Sin)
            act.activation(cos2, rot_c, ACT.Sin).then_inc(S("rot2"), 1)
            for hp in range(4):
                for g in range(3):
                    n = 3 * hp + g
                    j = CH[f"qk{hp}{g}"]
                    during(j)
                    for t in range(NT):
                        wait_acc(act, j, t)
                        if t or n:
                            act.wait_ge(S("qk_red"), NT * n + t)
                        act.activation(sqb, ACC[t][:, :], ACT.Square).then_inc(S("qk_sq"), 1)
                    after(j)
                    act.wait_ge(S("qk_ms"), n + 1)
                    act.activation(qk_n["rt"], qk_n["ms"], ACT.Sqrt).then_inc(S("qk_rt"), 1)
                    for i in range(4):
                        tcopy(f"qk{hp}", 4 * g + i, (qT if i < 2 else kT)[:, g, i % 2, :], tb(f"qk{hp}", 4 * g + i))
                for h in range(2):
                    evac(f"v{hp}{h}", lambda t: v2[:, t, h, :])
                attention(f"dil{hp}", lambda i: dil_unit(hp, i), 8)
            end_phase(act, "ACT")
            gates(0, silu_sb)
            for t in range(NT):
                wait_read(act, "fin01", t)
                sumsq(res2[:, t, :], junkE, ns["n3"]["ss"][:, t:t + 1], "n3", t)
            root("n3", ns["n3"])
            wait_used(act, "fin01")
            for k in range(KD):
                hi("n3", k, AT_hi[:, k, :].rearrange("p (q r) -> p r q", r=4),
                   tb("n3", k).rearrange("p (r q) -> p r q", r=4), g_n2[1][:, k:k + 1])
            end_phase(act, "ACT")
            memory_stage(1)
            end_phase(act, "ACT")

            act.wait_ge(S("lb_in"), 1)
            act.activation(lb, lbl[:, 1, :], ACT.Sigmoid)
            act.activation(lb1, lbl[:, 1, :], ACT.Sigmoid, scale=-1.0).then_inc(S("lb_ready"), 1)
            for hh in range(2):
                if hh:
                    act.wait_ge(S("gl_o"), 4)
                evac(f"ql{hh}", lambda t: l_tok[:, t, :])
                for i in range(4):
                    tcopy(f"ql{hh}", i, lq[:, i, :], tb(f"ql{hh}", i))
                evac(f"fl{hh}", lambda t: l_tok[:, t, :])
                for i in range(4):
                    u = TPU[f"fl{hh}"] + i
                    act.wait_ge(tp_ready, u + 1)
                    act.activation(lf[:, i, :], TP[u % 2], ACT.Sigmoid)
                    act.activation(lk[:, i, :], TP[u % 2], ACT.Sigmoid, scale=-1.0).then_inc(tp_free[u % 2], 1)
                evac(f"vl{hh}", lambda t: lv[:, t, :])
                act.wait_ge(S("lf_in"), hh + 1)
                act.activation(lf, lf, ACT.Ln).then_inc(S("lf_done"), 1)
                for h in range(4):
                    H = 4 * hh + h
                    for i in range(9):
                        n = 9 * H + i
                        act.wait_ge(S("gl_e"), n + 1)
                        act.activation(lexp[n % 2], lexp[n % 2], ACT.Exp).then_inc(S("gl_x"), 1)
                    act.wait_ge(S("gl_o"), H + 1)
                    act.activation(mix[:, :, P * H:P * H + P], ACC[H % 2].rearrange("p (t c) -> p t c", t=NT),
                                   ACT.Copy).then_inc(S("gl_od"), 1)
            end_phase(act, "ACT")
            for t in range(NT):
                if t >= 2:
                    act.wait_ge(S("gla_red"), t - 1)
                act.activation(lsq[:, t % 2, :], mix[:, t, 0:1024], ACT.Square).then_inc(S("gla_sq"), 1)
            act.wait_ge(S("gla_ms"), 1)
            act.activation(gl_n["rt"], gl_n["ms"], ACT.Sqrt).then_inc(S("gla_rt"), 1)
            act.wait_ge(S("gla_red"), NT)
            gates(1, silu3)


        @block.vector
        def _(dve):
            chain, los = [0], [0]

            def link(ins):
                chain[0] += 1
                ins.then_inc(S("dve_step"), 1)
                dve.wait_ge(S("dve_step"), chain[0])

            def feed(p):
                if p >= NP:
                    return
                dve.wait_ge(hi_done, p + 1)
                dve.tensor_tensor(w_slot(wlo, p, p % SPL), w_slot(wraw, p, p % RAW), w_slot(whi, p, p % SPL).bitcast(F32),
                                  ALU.subtract).then_inc(lo_done, 1)

            def during(j):
                for i in range(chunks[j]["count"] - 1):
                    feed(chunks[j]["first"] + i + SPL)

            def after(j):
                feed(chunks[j]["first"] + chunks[j]["count"] - 1 + SPL)

            def flow(name):
                during(CH[name])
                after(CH[name])

            def lo(name, i, dst, src, hi, gain=None):
                u = TPU[name] + i
                los[0] += 1
                dve.wait_ge(act_hi, los[0])
                if gain is None:
                    r = dve.tensor_tensor(dst, src, hi.bitcast(F32), ALU.subtract)
                else:
                    r = dve.scalar_tensor_tensor(dst, src, gain, hi.bitcast(F32), ALU.mult, ALU.subtract)
                r.then_inc(tp_free[u % 2], 1)

            def tb(name, i):
                return TP[(TPU[name] + i) % 2]

            def mean(name, c, width):
                dve.tensor_scalar(c["ms"], c["ss"], 1.0 / width, EPS, ALU.mult, ALU.add).then_inc(norm_ms, 1)
                dve.wait_ge(norm_rt, ORDER.index(name) + 1)
                link(dve.reciprocal(c["rs"], c["rt"]))

            def row_norm(name, nt, width, rows, dst=None):
                dve.wait_ge(norm_ss, so_far(name, 1, nt))
                mean(name, ns[name], width)
                for t in range(nt):
                    dve.tensor_scalar((dst or rows)(t), rows(t), ns[name]["rs"][:, t:t + 1], None, ALU.mult
                                      ).then_inc(norm_xs, 1)

            def head_norm(name, tok, nt, gain, sq):
                c = ns[name]
                for t in range(nt):
                    dve.wait_ge(head_sq, so_far(name, 3, t + 1))
                    dve.tensor_reduce(c["ss"][:, MH * t:MH * t + MH], sq.rearrange("p (h c) -> p h c", h=MH),
                                      AX.X, ALU.add).then_inc(head_red, 1)
                dve.wait_ge(head_red, so_far(name, 3, nt))
                mean(name, c, HD)
                for t in range(nt):
                    for h in range(MH):
                        x = tok[:, t, P * h:P * h + P]
                        dve.scalar_tensor_tensor(x, x, c["rs"][:, MH * t + h:MH * t + h + 1], gain, ALU.mult, ALU.mult
                                                 ).then_inc(norm_xs, 1)

            def attention(name, unit, n):
                U0 = AU[name]

                def maxima(i):
                    u, U = unit(i), U0 + i
                    r = U % 4
                    nm = att_nm[:, r:r + 1]
                    mx = att_mx[:, 3 * r:3 * r + len(u["s"])]
                    dve.wait_ge(att_s, U + 1)
                    if u["s"][0][3] is None:
                        link(dve.tensor_reduce(mx, scores_out(U, 0, u["kw"]), AX.X, ALU.max))
                        dve.tensor_scalar(nm, mx, -u["s"][0][4], None, ALU.mult).then_inc(att_m, 1)
                        return
                    for k, (off, _, keys, mask, scale) in enumerate(u["s"]):
                        w = keys.shape[1]
                        ins = dve.tensor_tensor_reduce(u["sb"][U % len(u["sb"])][:, off:off + w],
                                                       scores_out(U, off, w, u["kw"] > 512), mask, scale, LOW,
                                                       ALU.add, ALU.max, mx[:, k:k + 1])
                    link(ins)
                    if len(u["s"]) > 1:
                        link(dve.tensor_reduce(nm, mx, AX.X, ALU.max))
                        mx = nm
                    dve.tensor_scalar(nm, mx, -1.0, None, ALU.mult).then_inc(att_m, 1)

                look = unit(0)["look"]
                for i in range(look):
                    maxima(i)
                for i in range(n):
                    u, U = unit(i), U0 + i
                    if i + look < n:
                        maxima(i + look)
                    nb = u["kw"] // P
                    per = -(-nb // 4)
                    pt = u["pt"][i % len(u["pt"])]
                    if i >= len(u["pt"]):
                        dve.wait_ge(att_o, U - len(u["pt"]) + 1)
                    for k in range(per):
                        tu = TPU[name] + per * i + k
                        w = P * min(4, nb - 4 * k)
                        dve.wait_ge(tp_ready, tu + 1)
                        dve.tensor_copy(pt[:, 512 * k:512 * k + w], TP[tu % 2][:, 0:w]).then_inc(tp_free[tu % 2], 1)
                    dve.wait_ge(att_p, U + 1)
                    dve.reciprocal(att_rl[:, U % 4:U % 4 + 1], att_l[:, U % 4:U % 4 + 1]).then_inc(att_r, 1)

            def accumulate(name, dst):
                j = CH[name]
                during(j)
                for t in range(NT):
                    wait_acc(dve, j, t)
                    d = dst(t)
                    dve.tensor_tensor(d, ACC[t][:, :], d, ALU.add).then_inc(acc_free[t], 1)
                after(j)

            def memory_stage(l):
                row_norm(f"mem{l}", 2, D, lambda t: memx[:, t, :])
                for k in range(KD):
                    lo(f"mem{l}", k, AT_mem_lo[:, k, :], tb(f"mem{l}", k)[:, 0:MEM], AT_mem_hi[:, k, :], g_mem[l][:, k:k + 1])
                flow(f"mkv{l}0")
                head_norm(f"km{l}", km_tok, 2, mg[:, P:2 * P], msq)
                flow(f"mkv{l}1")
                flow(f"qm{l}")
                head_norm(f"qm{l}", qm_tok, NT, mg[:, 0:P], msq)
                attention(f"mat{l}", mem_unit, 16)

            def gates(l, tmp, res, res_in):
                for i in range(3):
                    j = CH[f"gate{l}{i}"]
                    during(j)
                    for t in range(NT):
                        wait_read(dve, f"gate{l}{i}", t)
                        m = mix[:, t, 512 * i:512 * i + 512]
                        dve.tensor_tensor(m, m, tmp[(NT * i + t) % 2], ALU.mult).then_inc(S(f"gated{l}"), 1)
                    after(j)
                for k in range(12):
                    lo(f"y{l}", k, AT_lo[:, k, :], tb(f"y{l}", k), AT_hi[:, k, :])
                dve.wait_ge(S(f"res{l + 2}"), res_in)
                for i in range(2):
                    accumulate(f"fin{l}{i}", lambda t: res[:, t, 512 * i:512 * i + 512])

            dve.sem_inc(S("hid_done"), 2)
            dve.sem_inc(S("y_done"), 2)
            dve.sem_inc(S("sc_ready"), 1)
            dve.sem_inc(S("sc_free"), 2)
            dve.sem_inc(S("gen_y"), 8)
            dve.sem_inc(S("gen_hid"), 1)
            dve.sem_inc(S("gen_add"), 2)
            for p in range(SPL):
                feed(p)
            row_norm("n1", NT, D, lambda t: xr[:, t, :])
            dve.wait_ge(S("gains_in"), 128)
            dve.wait_ge(S("consts"), 16)
            for k in range(KD):
                lo("n1", k, AT_lo[:, k, :], tb("n1", k), AT_hi[:, k, :], g_mix[:, k:k + 1])
            flow("cqkv0")
            flow("cqkv1")
            row_norm("cq", NT, 384, lambda t: cqkv[:, t, 0:384])
            row_norm("ckv", NT, 256, lambda t: cqkv[:, t, 384:640])
            for k in range(3):
                lo("cq", k, AT_lo[:, 8 + k, :], tb("cq", k), AT_hi[:, 8 + k, :], g_cq[:, k:k + 1])
            flow("uq0")
            flow("uq1")
            for k in range(2):
                lo("ckv", k, AT_lo[:, 8 + k, :], tb("ckv", k), AT_hi[:, 8 + k, :], g_ckv[:, k:k + 1])
            flow("uk")
            flow("uv")
            attention("mla", mla_unit, 32)
            for k in range(4):
                lo("oa", k, AT_lo[:, 8 + k, :], tb("oa", k), AT_hi[:, 8 + k, :])
            end_phase(dve, "DVE")

            for name in ("idx0", "idx1", "qkvb0", "qkvb1", "qkvb2", "ga0", "ga1"):
                flow(name)
            for i in range(2):
                j = CH[f"oa{i}"]
                during(j)
                for t in range(NT):
                    wait_acc(dve, j, t)
                    wait_read(dve, f"ga{i}", t)
                    y = y1[:, t, 512 * i:512 * i + 512]
                    dve.tensor_tensor(y, ACC[t][:, :], y, ALU.mult).then_inc(acc_free[t], 1)
                after(j)
            dve.wait_ge(S("b_rot"), 2)
            dve.wait_ge(tp_ready, TPU["ki"] + 1)
            for n in range(24):
                qt, h = 1 + n // 8, n % 8
                kw = P * (qt + 1)
                sc, w = score[:, qt - 1, 0:kw], wi_s[:, qt, h:h + 1]
                dve.wait_ge(S("idx_relu"), n + 1)
                if h == 0:
                    dve.tensor_scalar(sc, rel[n % 2][:, 0:kw], w, None, ALU.mult).then_inc(S("idx_add"), 1)
                else:
                    dve.wait_ge(S("idx_add"), n)
                    dve.scalar_tensor_tensor(sc, rel[n % 2][:, 0:kw], w, sc, ALU.mult, ALU.add).then_inc(S("idx_add"), 1)
                if h == 7:
                    dve.wait_ge(S("idx_add"), n + 1)
                    link(dve.tensor_tensor(sc[:, kw - P:kw], sc[:, kw - P:kw], cmask[:, 384:512], ALU.add))
            for qt in range(1, NT):
                kw = P * (qt + 1)
                sc, left = score[:, qt - 1, 0:kw], tk[:, 0:kw]
                for r in range(TOPK // 8):
                    src = left if r else sc
                    link(dve.max(max8, src))
                    link(dve.match_replace(left, max8, src, GONE))
                link(dve.tensor_tensor(sc, left, sc, ALU.is_equal))
                link(dve.tensor_scalar(sc, sc, NEG, None, ALU.mult))
            attention("dsa", dsa_unit, 32)
            flow("gb0")
            flow("gb1")
            for k in range(4):
                lo("ob", k, AT_lo[:, 8 + k, :], tb("ob", k), AT_hi[:, 8 + k, :])
            for i in range(2):
                j = CH[f"ob{i}"]
                during(j)
                for t in range(NT):
                    wait_acc(dve, j, t)
                    wait_read(dve, f"gb{i}", t)
                    b = gb[:, t, 512 * i:512 * i + 512]
                    dve.tensor_tensor(b, ACC[t][:, :], b, ALU.mult).then_inc(acc_free[t], 1)
                for t in range(NT):
                    y = y1[:, t, 512 * i:512 * i + 512]
                    wait_read(dve, f"ob{i}", t)
                    dve.tensor_tensor(y, y, gb[:, t, 512 * i:512 * i + 512], ALU.add).then_inc(S("y_sum"), 1)
                after(j)
            for k in range(KD):
                lo("y", k, AT_lo[:, k, :], tb("y", k), AT_hi[:, k, :])
            dve.wait_ge(S("res1"), 16)
            for i in range(2):
                accumulate(f"out{i}", lambda t: x1[:, t, 512 * i:512 * i + 512])
            end_phase(dve, "DVE")

            row_norm("ffn", NT, D, lambda t: x1[:, t, :], dst=lambda t: bigt[:, t, :])
            for t in range(NT):
                dve.wait_ge(S("xs_hi"), t + 1)
                dve.tensor_tensor(xs_lo[:, t, :], bigt[:, t, :], xs_hi[:, t, :].bitcast(F32), ALU.subtract
                                  ).then_inc(S("xs_lo"), 1)
            spread = lambda a, n: a.unsqueeze(2).broadcast_to([P, NT, n])
            rows = lambda a, n: a.unsqueeze(1).broadcast_to([P, NT, n])
            dve.wait_ge(S("moe_in"), 96)
            dve.wait_ge(S("rt_mm"), 1)
            link(dve.tensor_tensor(lg, ACC[0][:, 0:NT * 40].rearrange("p (t c) -> p t c", t=NT), rows(b_rt, 40), ALU.add))
            glg = lg[:, :, 0:8]
            link(dve.tensor_reduce(r_gmax, glg, AX.X, ALU.max))
            dve.tensor_tensor(r_d, glg, spread(r_gmax, 8), ALU.subtract).then_inc(S("rt_exp"), 1)
            link(dve.tensor_tensor(r_eq, glg, spread(r_gmax, 8), ALU.is_equal))
            link(dve.scalar_tensor_tensor(r_cand, r_eq, -8.0, rows(iota_g, 8), ALU.mult, ALU.add))
            link(dve.tensor_reduce(r_gi, r_cand, AX.X, ALU.min))
            dve.tensor_tensor(oneh, r_cand, spread(r_gi, 8), ALU.is_equal).then_inc(S("rt_oneh"), 1)
            dve.wait_ge(S("rt_oneh"), 1)
            link(dve.tensor_tensor(r_el, lg[:, :, 8:40].rearrange("p t (g e) -> p t g e", g=8),
                                   oneh.unsqueeze(3).broadcast_to([P, NT, 8, EPG]), ALU.mult))
            link(dve.tensor_reduce(r_in4, r_el.rearrange("p t g e -> p t e g"), AX.X, ALU.add))
            src = r_in4
            for m, oh in ((r_m1, r_oh1), (r_m2, r_oh2)):
                link(dve.tensor_reduce(m, src, AX.X, ALU.max))
                link(dve.tensor_tensor(r_eq4, src, spread(m, EPG), ALU.is_equal))
                link(dve.scalar_tensor_tensor(r_cand4, r_eq4, -8.0, rows(iota_g[:, 0:EPG], EPG), ALU.mult, ALU.add))
                link(dve.tensor_reduce(r_min4, r_cand4, AX.X, ALU.min))
                link(dve.tensor_tensor(oh, r_cand4, spread(r_min4, EPG), ALU.is_equal))
                if m is r_m1:
                    link(dve.scalar_tensor_tensor(r_in4b, r_oh1, LOW, r_in4, ALU.mult, ALU.add))
                    src = r_in4b
            dve.tensor_tensor(r_d2, r_m2, r_m1, ALU.subtract).then_inc(S("rt_exp"), 1)
            dve.wait_ge(S("rt_exp_done"), 2)
            link(dve.tensor_reduce(r_sum, r_e, AX.X, ALU.add))
            link(dve.tensor_scalar(r_w1, r_e2, 1.0, None, ALU.add))
            link(dve.tensor_tensor(r_w1, r_w1, r_sum, ALU.mult))
            link(dve.reciprocal(r_w1, r_w1))
            link(dve.tensor_tensor(r_w2, r_w1, r_e2, ALU.mult))
            dve.tensor_tensor(r_oh1, r_oh1, spread(r_w1, EPG), ALU.mult)
            link(dve.tensor_tensor(r_oh2, r_oh2, spread(r_w2, EPG), ALU.mult))
            dve.tensor_tensor(comb4, r_oh1, r_oh2, ALU.add).then_inc(S("rt_comb"), 1)
            dve.wait_ge(S("comb_hi"), 1)
            dve.tensor_tensor(comb_s[:, :, 4:8], comb4, comb_s[:, :, 0:4].bitcast(F32), ALU.subtract).then_inc(S("comb_lo"), 1)
            dve.wait_ge(S("rank_mm"), 1)
            link(dve.tensor_tensor(r_eq, ACC[1][:, 0:NT * 8].rearrange("p (t c) -> p t c", t=NT), oneh, ALU.mult))
            link(dve.tensor_reduce(r_rank, r_eq, AX.X, ALU.add))
            dve.tensor_scalar(r_over, r_rank, float(CAP), None, ALU.is_ge).then_inc(S("rt_over"), 1)
            link(dve.scalar_tensor_tensor(key, r_gi, float(P), r_rank, ALU.mult, ALU.add))
            link(dve.tensor_scalar(key, key, float(8 * P), None, ALU.add))
            link(dve.scalar_tensor_tensor(key, r_over, 1e6, key, ALU.mult, ALU.add))
            dve.tensor_copy(keyb, spread(key, P)).then_inc(S("key_b"), 1)
            dve.wait_ge(S("rt_over"), 1)
            link(dve.tensor_tensor(r_eq4, comb4, spread(r_over, EPG), ALU.mult))
            link(dve.tensor_tensor(comb32.rearrange("p t (g e) -> p t g e", g=NGRP), oneh.unsqueeze(3).broadcast_to([P, NT, 8, EPG]),
                                   r_eq4.unsqueeze(2).broadcast_to([P, NT, 8, EPG]), ALU.mult))
            dve.wait_ge(S("over_mm"), 1)
            link(dve.tensor_reduce(r_sum[0:1, 0:1], ACC[1][0:1, 64:64 + NT], AX.X, ALU.add))
            dve.tensor_copy(flag[0:1, 0:1], r_sum[0:1, 0:1]).then_inc(S("flag_in"), 1)
            dve.wait_ge(S("flag_in"), 1)
            dve.wait_ge(S("key_row"), 1)
            def feed_in(g, j):
                p = P_MOE + j + SPL
                if isinstance(g, int):
                    return feed(g * PPG + p)
                dve.wait_ge(hi_done, g * PPG + (p + 1))
                dve.tensor_tensor(wlo[:, p % SPL, :], wraw[:, p % RAW, :], whi[:, p % SPL, :].bitcast(F32),
                                  ALU.subtract).then_inc(lo_done, 1)

            def feeds(g, kind, e, qs):
                for q in qs:
                    feed_in(g, piece_of[kind, e, q])

            def picks():
                for t in range(NT):
                    r = dve.tensor_scalar(pick[:, t, :], iota_s, key[:, t:t + 1], None, ALU.is_equal)
                r.then_inc(S("pick"), 1)

            def puts():
                dve.tensor_scalar(put, keyrow, iota_p[:, 0:1], None, ALU.is_equal).then_inc(S("put"), 1)

            def gathered(g, i):
                dve.wait_ge(act_hi, g * 2 + (los[0] + i + 1))
                for k in range(4):
                    r = dve.scalar_tensor_tensor(xg_lo[:, 4 * i + k, :], TP[i][:, k * P:k * P + P], g_ffn[:, 4 * i + k:4 * i + k + 1],
                                                 xg_hi[:, 4 * i + k, :].bitcast(F32), ALU.mult, ALU.subtract)
                r.then_inc(tp_free[i], 1)

            def slot_weights(g):
                dve.wait_ge(S("ws_mm"), g + 1)
                dve.tensor_reduce(wslot, ACC[1][:, 0:2 * EPG].rearrange("p (h e) -> p e h", h=2), AX.X, ALU.add
                                  ).then_inc(S("ws_read"), 1)

            def hidden(g, e):
                dve.wait_ge(S("ws_read"), g + 1)
                dve.wait_ge(S("silu"), g * EPG + (e + 1))
                dve.scalar_tensor_tensor(hid_sb[e % 2], ACC[e % 2][:, FF:2 * FF], wslot[:, e:e + 1], sg_sb[e % 2],
                                         ALU.mult, ALU.mult).then_inc(S("hid_done"), 1)

            def hidden_lo(g, e):
                dve.wait_ge(S("hd_hi"), g * EPG + (e + 1))
                dve.tensor_tensor(hd_lo[e % 2], SC[e % 2][:, 0:FF], hd_hi[e % 2].bitcast(F32), ALU.subtract
                                  ).then_inc(S("hd_split"), 1)

            def spread_sums(g, tiles):
                for i in tiles:
                    x = x1[:, i // 2, 512 * (i % 2):512 * (i % 2) + 512]
                    dve.wait_ge(S("sc_ready"), g * 8 + (i + 2))
                    dve.tensor_tensor(x, SC[i % 2], x, ALU.add).then_inc(S("sc_free"), 1)

            def group(g, last):
                if not last:
                    dve.wait_ge(S("pick"), g + 1)
                    dve.tensor_scalar(key, key, float(-P), None, ALU.add).then_inc(S("key_next"), 1)
                    dve.wait_ge(S("ws_mm"), g + 1)
                    dve.wait_ge(S("key_next"), g + 1)
                    picks()
                for e in (1, 2, 3):
                    feeds(g, "gu", e, (0, 1, 2))
                    hidden(g, e)
                    feeds(g, "gu", e, (3,))
                    hidden_lo(g, e - 1)
                    if e < 3:
                        feeds(g, "dn", e - 1, (0, 1))
                if not last:
                    gathered(g + 1, 0)
                feeds(g, "dn", 2, (0, 1))
                hidden_lo(g, 3)
                if not last:
                    gathered(g + 1, 1)
                    slot_weights(g + 1)
                feeds(g, "dn", 3, (0,))
                for n in range(2):
                    dve.wait_ge(S("y_hi"), g * 2 + (n + 1))
                    dve.tensor_tensor(y_lo[:, 512 * n:512 * n + 512], ACC[2 + n], y_hi[:, 512 * n:512 * n + 512].bitcast(F32),
                                      ALU.subtract).then_inc(S("y_done"), 1)
                feeds(g, "dn", 3, (1,))
                if last:
                    spread_sums(g, range(8))
                    return
                feeds(g + 1, "gu", 0, (0, 1))
                spread_sums(g, (0, 1))
                feeds(g + 1, "gu", 0, (2,))
                spread_sums(g, (2, 3))
                hidden(g + 1, 0)
                feeds(g + 1, "gu", 0, (3,))
                spread_sums(g, (4, 5, 6, 7))
                dve.wait_ge(S("put"), g + 1)
                dve.tensor_scalar(keyrow, keyrow, float(-P), None, ALU.add).then_inc(S("row_next"), 1)
                dve.wait_ge(S("row_next"), g + 1)
                puts()
                dve.wait_ge(S("sc_free"), g * 8 + (8 + 2))

            picks()
            puts()
            gathered(0, 0)
            gathered(0, 1)
            slot_weights(0)
            feeds(0, "gu", 0, (0, 1, 2))
            hidden(0, 0)
            feeds(0, "gu", 0, (3,))
            with dve.Fori(0, NGRP - 1) as g:
                group(g, False)
            group(NGRP - 1, True)
            dve.wait_ge(S("sc_free"), 8 * NGRP + 2)
            los[0] += 2 * NGRP
            with dve.If(dve.value_load(flag[0:1, 0:1], min_val=0, max_val=T) > 0):
                with dve.Fori(0, NGRP * EPG) as e:
                    dve.wait_ge(S("gen_silu"), e + 1)
                    dve.tensor_tensor(gen_hid[:, 0, :], ACC[2], gen_sil[:, 0, :], ALU.mult)
                    dve.tensor_tensor(gen_hid[:, 1, :], ACC[3], gen_sil[:, 1, :], ALU.mult).then_inc(S("gen_hid"), 1)
                    for i in range(2 * NT):
                        t, n = i // 2, i % 2
                        x = x1[:, t, 512 * n:512 * n + 512]
                        dve.wait_ge(S("gen_y"), e * 8 + (8 + i + 1))
                        dve.scalar_tensor_tensor(x, SC[i % 2], comb32[:, t, bass.ds(e, 1)], x, ALU.mult, ALU.add
                                                 ).then_inc(S("gen_add"), 1)
                    dve.wait_ge(S("gen_add"), e * 8 + (8 + 2))
            end_phase(dve, "DVE")

            c = ns["final"]
            dve.wait_ge(norm_ss, so_far("final", 1, NT))
            mean("final", c, D)
            for t in range(NT):
                dve.scalar_tensor_tensor(xn[:, t, :], x1[:, t, :], c["rs"][:, t:t + 1], fin_g, ALU.mult, ALU.mult
                                         ).then_inc(S("fin_x"), 1)
            row_norm("n2", NT, D, lambda t: xn[:, t, :], dst=lambda t: x1[:, t, :])
            for k in range(KD):
                lo("n2", k, AT_perm(AT_lo, k), tb("n2", k).rearrange("p (t q r) -> p t q r", t=NT, r=4), AT_perm(AT_hi, k),
                   g_n2[0][:, k:k + 1])
            memory_stage(0)
            end_phase(dve, "DVE")

            dve.wait_ge(S("dil_in"), 64)
            ROUND, C1, C2 = 1.5 * 2 ** 23, 6.28125, 0.0019350051879882812
            C3 = 2 * np.pi - C1 - C2
            link(dve.tensor_copy(rot_p, posi[:, :]))
            link(dve.tensor_tensor(rot_a, rot_p.unsqueeze(2).broadcast_to([P, NT, 16]), inv2.unsqueeze(1).broadcast_to([P, NT, 16]),
                                   ALU.mult))
            link(dve.tensor_scalar(rot_k, rot_a, 1 / (2 * np.pi), ROUND, ALU.mult, ALU.add))
            link(dve.tensor_scalar(rot_k, rot_k, ROUND, None, ALU.subtract))
            for cc in (C1, C2, C3):
                link(dve.scalar_tensor_tensor(rot_a, rot_k, -float(cc), rot_a, ALU.mult, ALU.add))
            link(dve.tensor_scalar(rot_r, rot_a, 3.1415925, -3.1415925, ALU.min, ALU.max))
            link(dve.scalar_tensor_tensor(rot_c, rot_r, -1.0, rot_r, ALU.mult, ALU.min))
            dve.tensor_scalar(rot_c, rot_c, float(np.pi / 2), None, ALU.add).then_inc(S("rot_ang"), 1)
            for hp in range(4):
                for g in range(3):
                    n = 3 * hp + g
                    j = CH[f"qk{hp}{g}"]
                    during(j)
                    if n:
                        dve.wait_ge(tp_ready, TPU[f"qk{hp}"] + 4 * g if g else TPU[f"qk{hp - 1}"] + 12)
                    for t in range(NT):
                        dve.wait_ge(S("qk_sq"), NT * n + t + 1)
                        dve.tensor_reduce(qk_n["ss"][:, 4 * t:4 * t + 4], sqb.rearrange("p (h c) -> p h c", h=4), AX.X, ALU.add
                                          ).then_inc(S("qk_red"), 1)
                        dve.tensor_tensor(qk_t[:, t, :].rearrange("p (a h c) -> p a h c", a=2, h=2),
                                          ACC[t].rearrange("p (a h c) -> p a h c", a=2, h=2),
                                          qkg[:, g, :, :].unsqueeze(2).broadcast_to([P, 2, 2, P]), ALU.mult
                                          ).then_inc(acc_free[t], 1)
                    after(j)
                    dve.wait_ge(S("qk_red"), NT * n + NT)
                    dve.tensor_scalar(qk_n["ms"], qk_n["ss"], 1.0 / HD, EPS, ALU.mult, ALU.add).then_inc(S("qk_ms"), 1)
                    dve.wait_ge(S("qk_rt"), n + 1)
                    link(dve.reciprocal(qk_rs[:, g, :, :], qk_n["rt"].rearrange("p (t c) -> p t c", t=NT)))
                    q = qk_rs[:, g, :, 0:2]
                    link(dve.tensor_scalar(q, q, HD ** -0.5, None, ALU.mult))
                    dve.sem_inc(S("qk_rs"), 1)
                for h in range(2):
                    flow(f"v{hp}{h}")
                attention(f"dil{hp}", lambda i: dil_unit(hp, i), 8)
            end_phase(dve, "DVE")
            gates(0, silu_sb, res2, 64)
            row_norm("n3", NT, D, lambda t: res2[:, t, :], dst=lambda t: n3x[:, t, :])
            for k in range(KD):
                by_token = lambda a: a[:, k, :].rearrange("p (q r) -> p r q", r=4)
                lo("n3", k, by_token(AT_lo), tb("n3", k).rearrange("p (r q) -> p r q", r=4), by_token(AT_hi), g_n2[1][:, k:k + 1])
            end_phase(dve, "DVE")
            memory_stage(1)
            end_phase(dve, "DVE")

            dve.wait_ge(S("gla_in"), 64)
            dve.tensor_tensor(lbl[:, 1, :], lbl[:, 1, :], lbl[:, 0, :], ALU.subtract).then_inc(S("lb_in"), 1)
            dve.wait_ge(S("lb_ready"), 1)
            dve.wait_ge(S("gla_zero"), 1)
            diag = view(at_ltok, 2560, NT, 640)[:, :, 0:P]
            four = lambda a: a.rearrange("p (t c) -> p t c", t=NT)
            for hh in range(2):
                for nm in "qfv":
                    flow(f"{nm}l{hh}")
                wait_tp_read(dve, f"fl{hh}", 4)
                for i in range(4):
                    H = 4 * hh + i
                    dve.tensor_scalar(lf[:, i, :], lf[:, i, :], lb1[:, H:H + 1], lb[:, H:H + 1], ALU.mult, ALU.add)
                    r = dve.tensor_scalar(lk[:, i, :], lk[:, i, :], lb1[:, H:H + 1], None, ALU.mult)
                r.then_inc(S("lf_in"), 1)
                dve.wait_ge(S("lf_done"), hh + 1)
                dve.wait_ge(S("lf_in"), hh + 1)
                dve.wait_ge(S("lA_zero"), hh + 1)

                for h in range(4):
                    H = 4 * hh + h
                    if H:
                        dve.wait_ge(S("gl_e"), 9 * H)
                    dve.tensor_tensor_scan(G64, seg, lf[:, h, :], 0.0, ALU.mult, ALU.add)
                    link(dve.tensor_tensor_scan(G512, ones[:, 0:1].broadcast_to([P, T]), lf[:, h, :], 0.0, ALU.mult, ALU.add))

                    def halves(a, half):
                        v = a.rearrange("p (n s c) -> p n s c", s=2, c=half)
                        return v[:, :, 0, :], v[:, :, 1, :]

                    def exponents(i):
                        n, half = 9 * H + i, 1 << i
                        first, second = halves(G64 if half <= 64 else G512, half)
                        d1, d2 = halves(lexp[n % 2], half)
                        ref = first[:, :, half - 1:half].broadcast_to([P, T // (2 * half), half])
                        if n >= 2:
                            dve.wait_ge(S("gl_q"), n - 1)
                        dve.tensor_tensor(d1, ref, first, ALU.subtract)
                        if half == 64:
                            r = dve.tensor_copy(d2, second)
                        else:
                            r = dve.tensor_tensor(d2, second, ref, ALU.subtract)
                        r.then_inc(S("gl_e"), 1)

                    def operands(i):
                        n, half = 9 * H + i, 1 << i
                        dve.wait_ge(S("gl_x"), n + 1)
                        e1, e2 = halves(lexp[n % 2], half)
                        dve.tensor_tensor(halves(ke[n % 2], half)[0], halves(lk[:, h, :], half)[0], e1, ALU.mult)
                        dve.tensor_tensor(halves(qe[n % 2], half)[1], halves(lq[:, h, :], half)[1], e2, ALU.mult
                                          ).then_inc(S("gl_q"), 1)

                    def collect(i):
                        m = 10 * H + i
                        dve.wait_ge(S("gl_mm"), m + 1)
                        src = four(SC[m % 2])
                        if m:
                            dve.wait_ge(S("gl_c"), m)
                        if i <= 7:
                            mask = lmask[:, 7 if i == 0 else i - 1, :].bitcast(I32).unsqueeze(1).broadcast_to([P, NT, P])
                            dve.copy_predicated(diag, mask, src).then_inc(S("gl_c"), 1)
                        elif i == 8:
                            dve.tensor_copy(lA[:, 0, P:2 * P], src[:, 1, :])
                            dve.tensor_copy(lA[:, 2, 3 * P:4 * P], src[:, 3, :]).then_inc(S("gl_c"), 1)
                        else:
                            dve.tensor_copy(lA[:, 0:2, 2 * P:4 * P], SC[m % 2].rearrange("p (s t) -> p s t", s=2)
                                            ).then_inc(S("gl_c"), 1)

                    if H:
                        dve.wait_ge(S("gl_o"), H)
                    exponents(0)
                    for i in range(9):
                        if i + 1 < 9:
                            exponents(i + 1)
                        operands(i)
                        collect(i)
                    collect(9)
            end_phase(dve, "DVE")
            for t in range(NT):
                dve.wait_ge(S("gla_sq"), t + 1)
                dve.tensor_reduce(gl_n["ss"][:, 8 * t:8 * t + 8], lsq[:, t % 2, :].rearrange("p (h c) -> p h c", h=8), AX.X, ALU.add
                                  ).then_inc(S("gla_red"), 1)
            dve.wait_ge(S("gla_red"), NT)
            dve.tensor_scalar(gl_n["ms"], gl_n["ss"], 1.0 / HD, EPS, ALU.mult, ALU.add).then_inc(S("gla_ms"), 1)
            dve.wait_ge(S("gla_rt"), 1)
            link(dve.reciprocal(gl_n["rs"], gl_n["rt"]))
            for t in range(NT):
                for h in range(8):
                    m = mix[:, t, P * h:P * h + P]
                    r = dve.scalar_tensor_tensor(m, m, gl_n["rs"][:, 8 * t + h:8 * t + h + 1], og, ALU.mult, ALU.mult)
            link(r)
            gates(1, silu3, res3, 16)

        @block.tensor
        def _(pe):
            PASSES = lambda ah, al, bh, bl: ((ah, bh), (ah, bl), (al, bh))

            def project(name):
                j = CH[name]
                c = chunks[j]
                n, per, nt = c["n"], c["per"], c["nt"]
                for i in range(c["count"]):
                    p = c["first"] + i
                    pe.wait_ge(lo_done, p + 1)
                    for t in range(nt):
                        if i == 0 and bank_uses[j][t]:
                            pe.wait_ge(acc_free[t], bank_uses[j][t])
                        for kk in range(per):
                            kc = i * per + kk
                            cols = slice(t * P, t * P + P)
                            ah, al = ((AT_mem_hi[:, kc, cols], AT_mem_lo[:, kc, cols]) if c["mem"] else
                                      (AT_hi[:, c["at"] + kc, cols], AT_lo[:, c["at"] + kc, cols]))
                            bh, bl = (w[:, p % SPL, kk * n:kk * n + n] for w in (whi, wlo))
                            for q, (a, b) in enumerate(PASSES(ah, al, bh, bl)):
                                mm = pe.matmul(ACC[t][:, 0:n], a, b, start=kc == 0 and q == 0,
                                               stop=i == c["count"] - 1 and kk == per - 1 and q == 2)
                        if t == nt - 1:
                            mm.then_inc(piece_used, 1)
                        elif i == c["count"] - 1:
                            mm.then_inc(acc_ready, 1)

            def transposes(name, i, blocks):
                u = TPU[name] + i
                if u >= 2:
                    pe.wait_ge(tp_free[u % 2], u // 2)
                at = 0
                for b in blocks:
                    tr = pe.transpose(TP[u % 2][0:b.shape[1], at:at + P], b, ident)
                    at += P
                tr.then_inc(tp_ready, 1)

            def rows_t(name, n, rows, nt=NT):
                for k in range(n):
                    if k == 0:
                        pe.wait_ge(norm_xs, so_far(name, 2, nt))
                    transposes(name, k, [rows(t)[:, P * k:P * k + P] for t in range(nt)])
                wait_tp_read(pe, name, n)

            def attention(name, unit, n):
                U0 = AU[name]

                def scores(i):
                    u, U = unit(i), U0 + i
                    for off, q, k, _, _ in u["s"]:
                        mm = pe.matmul(scores_out(U, off, k.shape[1], u["kw"] > 512), q, k, start=True, stop=True)
                    mm.then_inc(att_s, 1)

                def probs_t(i):
                    u, U = unit(i), U0 + i
                    pe.wait_ge(att_p, U + 1)
                    nb = u["kw"] // P
                    per = -(-nb // 4)
                    s = u["sb"][U % len(u["sb"])]
                    for k in range(per):
                        transposes(name, per * i + k, [s[:, P * b:P * b + P] for b in range(4 * k, min(nb, 4 * k + 4))])

                def output(i):
                    u, U = unit(i), U0 + i
                    nb = u["kw"] // P
                    per = -(-nb // 4)
                    for k in range(per):
                        tu = TPU[name] + per * i + k
                        pe.wait_ge(tp_free[tu % 2], tu // 2 + 1)
                    if U >= 2:
                        pe.wait_ge(att_done, U - 1)
                    pt = u["pt"][i % len(u["pt"])]
                    for b in range(nb):
                        mm = pe.matmul(SC[U % 2][:, 0:u["dv"]], pt[:, P * b:P * b + P], u["v"][b], start=b == 0, stop=b == nb - 1)
                    mm.then_inc(att_o, 1)

                look, behind = unit(0)["look"], len(unit(0)["pt"]) - 1
                for i in range(look):
                    scores(i)
                for i in range(n + behind):
                    if i + look < n:
                        scores(i + look)
                    if i < n:
                        probs_t(i)
                    if i >= behind:
                        output(i - behind)

            def read_all(name):
                for t in range(chunks[CH[name]]["nt"]):
                    wait_read(pe, name, t)

            def memory_stage(l):
                rows_t(f"mem{l}", KD, lambda t: memx[:, t, :], nt=2)
                project(f"mkv{l}0")
                project(f"mkv{l}1")
                for name, tok, nt in ((f"km{l}", km_tok, 2), (f"qm{l}", qm_tok, NT)):
                    if tok is qm_tok:
                        project(f"qm{l}")
                    pe.wait_ge(norm_xs, so_far(name, 2, MH * nt))
                    for h in range(MH):
                        transposes(name, h, [tok[:, t, P * h:P * h + P] for t in range(nt)])
                    wait_tp_read(pe, name, MH)
                read_all(f"mkv{l}1")
                read_all(f"qm{l}")
                attention(f"mat{l}", mem_unit, 16)

            def gates(l):
                for i in range(3):
                    project(f"gate{l}{i}")
                pe.wait_ge(S(f"gated{l}"), 3 * NT)
                for k in range(12):
                    transposes(f"y{l}", k, [mix[:, t, P * k:P * k + P] for t in range(NT)])
                wait_tp_read(pe, f"y{l}", 12)
                for i in range(2):
                    project(f"fin{l}{i}")

            pe.wait_ge(S("consts"), 16)
            rows_t("n1", KD, lambda t: xr[:, t, :])
            project("cqkv0")
            project("cqkv1")
            rows_t("cq", 3, lambda t: cqkv[:, t, 0:384])
            project("uq0")
            project("uq1")
            for h in range(H8):
                pe.wait_ge(S("qa_rot"), h // 4 + 1)
                transposes("qa", h, [qk_tok[:, t, h, :] for t in range(NT)])
            rows_t("ckv", 2, lambda t: cqkv[:, t, 384:640])
            project("uk")
            project("uv")
            read_all("uk")
            pe.wait_ge(S("ka_rot"), NT)
            for h in range(H8):
                transposes("ka", h, [qk_tok[:, t, h, :] for t in range(NT)])
            wait_tp_read(pe, "ka", H8)
            read_all("uv")
            attention("mla", mla_unit, 32)
            pe.wait_ge(att_done, AU["mla"] + 32)
            for k in range(4):
                transposes("oa", k, [o_tok[:, t, P * k:P * k + P] for t in range(NT)])
            end_phase(pe, "PE")

            for name in ("idx0", "idx1", "qkvb0", "qkvb1", "qkvb2", "ga0", "ga1", "oa0", "oa1"):
                project(name)
            pe.wait_ge(S("b_rot"), 2)
            for i in range(8):
                transposes("qkb", i, [qkvb[:, t, P * i:P * i + P] for t in range(NT)])
            for i in range(4):
                transposes("qi", i, [idx[:, t, P * i:P * i + P] for t in range(NT)])
            transposes("ki", 0, [kidup[:, t, :] for t in range(NT)])
            wait_tp_read(pe, "qkb", 8)
            wait_tp_read(pe, "qi", 4)
            wait_tp_read(pe, "ki", 1)
            for n in range(24):
                qt, h = 1 + n // 8, n % 8
                r0 = 64 * (h % 2)
                kw = P * (qt + 1)
                if n >= 2:
                    pe.wait_ge(S("idx_relu"), n - 1)
                pe.matmul(SC[n % 2][:, 0:kw], qiT[r0:r0 + 64, h // 2, qt * P:qt * P + P], kiT[r0:r0 + 64, 0:kw],
                          start=True, stop=True).then_inc(S("idx_mm"), 1)
            pe.wait_ge(S("idx_relu"), 24)
            read_all("oa1")
            attention("dsa", dsa_unit, 32)
            project("gb0")
            project("gb1")
            pe.wait_ge(att_done, AU["dsa"] + 32)
            for k in range(4):
                transposes("ob", k, [o_tokb[:, t, P * k:P * k + P] for t in range(NT)])
            wait_tp_read(pe, "ob", 4)
            project("ob0")
            project("ob1")
            pe.wait_ge(S("y_sum"), 2 * NT)
            for k in range(KD):
                transposes("y", k, [y1[:, t, P * k:P * k + P] for t in range(NT)])
            wait_tp_read(pe, "y", KD)
            project("out0")
            project("out1")
            end_phase(pe, "PE")

            pe.wait_ge(norm_xs, so_far("ffn", 2, NT))
            for k in range(KD):
                transposes("h2", k, [bigt[:, t, P * k:P * k + P] for t in range(NT)])
            wait_tp_read(pe, "h2", KD)
            pe.wait_ge(S("moe_in"), 96)
            for t in range(NT):
                for k in range(KD):
                    mm = pe.matmul(ACC[0][:, 40 * t:40 * t + 40], h2T[:, k, t * P:t * P + P], w_rt[:, k, :],
                                   start=k == 0, stop=k == KD - 1)
            mm.then_inc(S("rt_mm"), 1)
            pe.wait_ge(S("rt_oneh"), 1)
            for t in range(NT):
                for b in range(t + 1):
                    mm = pe.matmul(ACC[1][:, 8 * t:8 * t + 8], before if b == t else ones, oneh[:, b, :],
                                   start=b == 0, stop=b == t)
            mm.then_inc(S("rank_mm"), 1)
            pe.wait_ge(S("rt_over"), 1)
            pe.matmul(ACC[1][:, 64:64 + NT], ones, r_over, start=True, stop=True).then_inc(S("over_mm"), 1)
            pe.wait_ge(S("key_b"), 1)
            for t in range(NT):
                mm = pe.matmul(ACC[2][:, t * P:t * P + P], keyb[:, t, :], ident, start=True, stop=True)
            mm.then_inc(S("key_mm"), 1)
            pe.wait_ge(S("xs_lo"), NT)
            pe.wait_ge(S("comb_lo"), 1)
            pe.wait_ge(S("key_row"), 1)
            def piece(g, what):
                pe.wait_ge(lo_done, g * PPG + (P_MOE + piece_of[what] + 1))
                return (P_MOE + piece_of[what]) % SPL

            def gather(g, i):
                pe.wait_ge(tp_free[i], g + (TPU["moe"] // 2))
                for k in range(4):
                    n = 0
                    cols = slice((4 * i + k) * P, (4 * i + k) * P + P)
                    for part in (xs_hi, xs_lo):
                        for t in range(NT):
                            mm = pe.matmul(TP[i][:, k * P:k * P + P], part[:, t, cols], pick[:, t, :], start=n == 0, stop=n == 7)
                            n += 1
                mm.then_inc(tp_ready, 1)

            def slot_weights(g):
                for t in range(NT):
                    mm = pe.matmul(ACC[1][:, 0:2 * EPG], pick[:, t, :], comb_s[:, t, :], start=t == 0, stop=t == NT - 1)
                mm.then_inc(S("ws_mm"), 1)

            def gate_up(g, e, qs=range(4)):
                for q in qs:
                    s = piece(g, ("gu", e, q))
                    if q == 0:
                        pe.wait_ge(S("hid_done"), g * EPG + (e + 1))
                    if e == 1 and q == 0:
                        pe.wait_ge(S("ws_read"), g + 1)
                    if e == 0 and q % 2 == 0:
                        pe.wait_ge(tp_free[q // 2], g + (TPU["moe"] // 2 + 1))
                    for kk in range(2):
                        k = 2 * q + kk
                        bh, bl = (w[:, s, kk * 512:kk * 512 + 512] for w in (whi, wlo))
                        for n, (a, b) in enumerate(PASSES(xg_hi[:, k, :], xg_lo[:, k, :], bh, bl)):
                            mm = pe.matmul(ACC[e % 2], a, b, start=k == 0 and n == 0, stop=k == 7 and n == 2)
                    mm.then_inc(piece_used, 1)

            def hidden_t(g, e):
                if e == 0:
                    pe.wait_ge(S("sc_free"), g * 8 + 2)
                pe.wait_ge(S("hid_done"), g * EPG + (e + 3))
                for b in range(2):
                    tr = pe.transpose(SC[e % 2][:, b * P:b * P + P], hid_sb[e % 2][:, b * P:b * P + P], ident)
                tr.then_inc(S("hd_t"), 1)

            def down(g, e):
                for b in range(2):
                    s = piece(g, ("dn", e, b))
                    if b == 0:
                        pe.wait_ge(S("hd_split"), g * EPG + (e + 1))
                    for n in range(2):
                        if e == 0 and b == 0:
                            pe.wait_ge(S("y_done"), g * 2 + (n + 1))
                        bh, bl = (w[:, s, 512 * n:512 * n + 512] for w in (whi, wlo))
                        for q, (x, y) in enumerate(PASSES(hd_hi[e % 2][:, b * P:b * P + P], hd_lo[e % 2][:, b * P:b * P + P], bh, bl)):
                            mm = pe.matmul(ACC[2 + n], x, y, start=e == 0 and b == 0 and q == 0, stop=e == 3 and b == 1 and q == 2)
                    mm.then_inc(piece_used, 1)

            def scatter(g, tiles):
                for i in tiles:
                    t, n = i // 2, i % 2
                    if i == 0:
                        pe.wait_ge(S("put"), g + 1)
                    if i < 2:
                        pe.wait_ge(S("y_done"), g * 2 + (i + 3))
                    pe.wait_ge(S("sc_free"), g * 8 + (i + 1))
                    for q, y in enumerate((y_hi, y_lo)):
                        mm = pe.matmul(SC[i % 2], put[:, t * P:t * P + P], y[:, 512 * n:512 * n + 512], start=q == 0, stop=q == 1)
                    mm.then_inc(S("sc_ready"), 1)

            def group(g, last):
                gate_up(g, 1)
                hidden_t(g, 0)
                down(g, 0)
                gate_up(g, 2)
                hidden_t(g, 1)
                down(g, 1)
                gate_up(g, 3)
                hidden_t(g, 2)
                if not last:
                    pe.wait_ge(S("pick"), g + 2)
                    gather(g + 1, 0)
                down(g, 2)
                hidden_t(g, 3)
                if not last:
                    gather(g + 1, 1)
                    slot_weights(g + 1)
                down(g, 3)
                if last:
                    scatter(g, range(8))
                    return
                gate_up(g + 1, 0, (0, 1))
                scatter(g, (0, 1))
                gate_up(g + 1, 0, (2,))
                scatter(g, (2, 3))
                gate_up(g + 1, 0, (3,))
                scatter(g, (4, 5, 6, 7))

            pe.wait_ge(S("pick"), 1)
            gather(0, 0)
            gather(0, 1)
            slot_weights(0)
            gate_up(0, 0)
            with pe.Fori(0, NGRP - 1) as g:
                group(g, False)
            group(NGRP - 1, True)
            pe.wait_ge(S("sc_free"), 8 * NGRP + 2)
            pe.sem_inc(S("moe_end"), 1)
            pe.wait_ge(S("flag_in"), 1)
            with pe.If(pe.value_load(flag[0:1, 0:1], min_val=0, max_val=T) > 0):
                with pe.Fori(0, NGRP * EPG) as e:
                    pe.wait_ge(S("gen_in"), e * 48 + 48)
                    for f in range(2):
                        for w in range(2):
                            for k in range(KD):
                                mm = pe.matmul(ACC[2 * w + f], gen_gu[:, w, k, f * P:f * P + P], h2T[:, k, :],
                                               start=k == 0, stop=k == KD - 1)
                    mm.then_inc(S("gen_gu"), 1)
                    pe.wait_ge(S("gen_hid"), e + 2)
                    for i in range(2 * NT):
                        t, n = i // 2, i % 2
                        pe.wait_ge(S("gen_add"), e * 8 + (i + 1))
                        for f in range(2):
                            mm = pe.matmul(SC[i % 2], gen_hid[:, f, t * P:t * P + P], gen_d[:, f, 512 * n:512 * n + 512],
                                           start=f == 0, stop=f == 1)
                        mm.then_inc(S("gen_y"), 1)
            end_phase(pe, "PE")

            rows_t("n2", KD, lambda t: x1[:, t, :])
            memory_stage(0)
            end_phase(pe, "PE")
            for hp in range(4):
                for g in range(3):
                    project(f"qk{hp}{g}")
                    pe.wait_ge(S("qk_rot"), 3 * hp + g + 1)
                    for i in range(4):
                        transposes(f"qk{hp}", 4 * g + i, [qk_t[:, t, P * i:P * i + P] for t in range(NT)])
                for h in range(2):
                    project(f"v{hp}{h}")
                wait_tp_read(pe, f"qk{hp}", 12)
                for h in range(2):
                    read_all(f"v{hp}{h}")
                attention(f"dil{hp}", lambda i: dil_unit(hp, i), 8)
            end_phase(pe, "PE")
            gates(0)
            rows_t("n3", KD, lambda t: n3x[:, t, :])
            end_phase(pe, "PE")
            memory_stage(1)
            end_phase(pe, "PE")

            for hh in range(2):
                if hh:
                    pe.wait_ge(S("gl_od"), 4)
                for nm in "qf":
                    project(f"{nm}l{hh}")
                    read_all(f"{nm}l{hh}")
                    for i in range(4):
                        transposes(f"{nm}l{hh}", i, [l_tok[:, t, P * i:P * i + P] for t in range(NT)])
                project(f"vl{hh}")
                read_all(f"vl{hh}")
                pe.wait_ge(S("lf_in"), hh + 1)
                for h in range(4):
                    H = 4 * hh + h
                    for i in range(10):
                        m = 10 * H + i
                        if m >= 2:
                            pe.wait_ge(S("gl_c"), m - 1)
                        if i == 0:
                            k, q = lk[:, h, :], lq[:, h, :]
                        else:
                            n = 9 * H + i - 1
                            pe.wait_ge(S("gl_q"), n + 1)
                            k, q = ke[n % 2], qe[n % 2]
                        tile = lambda a, t: a[:, t * P:t * P + P]
                        if i <= 7:
                            blocks = [(t * P, t, q[:, t * P:t * P + P]) for t in range(NT)]
                        elif i == 8:
                            blocks = [(t * P, t - 1, q[:, t * P:t * P + P]) for t in (1, 3)]
                        else:
                            blocks = [(2 * P * s, s, q[:, 2 * P:4 * P]) for s in range(2)]
                        for c0, s, rhs in blocks:
                            mm = pe.matmul(SC[m % 2][:, c0:c0 + rhs.shape[1]], tile(k, s), rhs, start=True, stop=True)
                        mm.then_inc(S("gl_mm"), 1)
                    pe.wait_ge(S("gl_c"), 10 * H + 10)
                    if H >= 2:
                        pe.wait_ge(S("gl_od"), H - 1)
                    for t in range(NT):
                        for s in range(t + 1):
                            mm = pe.matmul(ACC[H % 2][:, t * P:t * P + P], lA[:, s, t * P:t * P + P], lv[:, s, P * h:P * h + P],
                                           start=s == 0, stop=s == t)
                    mm.then_inc(S("gl_o"), 1)
            end_phase(pe, "PE")
            gates(1)


def kernel(x, norm_mix_g, w_in, mla_q_norm_g, w_uq, mla_kv_norm_g, w_uk, w_uv, w_o_a, w_o_b, w_out,
           norm_ffn_g, w_router_group, b_router_group, w_router_expert, b_router_expert, w_gate, w_up,
           w_down, final_norm_g, mem_2, positions_2, norm_gain_2, w_in_a_2, q_gain_a_2, k_gain_a_2,
           w_out_a_2, w_in_b_2, lb_logits_2, o_gain_b_2, w_out_b_2, mem_norm_gain_2, w_mem_kv_2,
           mem_q_gain_2, mem_k_gain_2):
    import concourse.bacc as bacc
    from concourse.bass_utils import run_bass_kernel_spmd

    arrays = dict(
        x=x, norm_mix_g=norm_mix_g, w_in=w_in, mla_q_norm_g=mla_q_norm_g, w_uq=w_uq, mla_kv_norm_g=mla_kv_norm_g,
        w_uk=w_uk, w_uv=w_uv, w_o_a=w_o_a, w_o_b=w_o_b, w_out=w_out, norm_ffn_g=norm_ffn_g,
        w_router_group=w_router_group, b_router_group=b_router_group, w_router_expert=w_router_expert,
        b_router_expert=b_router_expert, w_gate=w_gate, w_up=w_up, w_down=w_down, final_norm_g=final_norm_g,
        mem_2=mem_2, positions_2=positions_2, norm_gain_2=norm_gain_2, w_in_a_2=w_in_a_2, q_gain_a_2=q_gain_a_2,
        k_gain_a_2=k_gain_a_2, w_out_a_2=w_out_a_2, w_in_b_2=w_in_b_2, lb_logits_2=lb_logits_2, o_gain_b_2=o_gain_b_2,
        w_out_b_2=w_out_b_2, mem_norm_gain_2=mem_norm_gain_2, w_mem_kv_2=w_mem_kv_2, mem_q_gain_2=mem_q_gain_2,
        mem_k_gain_2=mem_k_gain_2)
    arrays = {name: np.ascontiguousarray(a) for name, a in arrays.items()}
    arrays["const"] = CONST
    nc = bacc.Bacc("TRN2", target_bir_lowering=False, num_devices=1)
    aps = {name: nc.dram_tensor(name, a.shape, mybir.dt.from_np(a.dtype), kind="ExternalInput").ap()
           for name, a in arrays.items()}
    out = nc.dram_tensor("out", (1, T, D), F32, kind="ExternalOutput").ap()
    build(nc, aps, out)
    return run_bass_kernel_spmd(nc, [arrays], core_ids=[0]).results[0]["out"]
```

```python
from contextlib import ExitStack

import numpy as np

import concourse.bass as bass
from concourse import mybir

F32 = mybir.dt.float32
F32R = mybir.dt.float32r
I32 = mybir.dt.int32
ALU = mybir.AluOpType
ACT = mybir.ActivationFunctionType
AX = mybir.AxisListType

P = 128
T, D = 512, 1024
NT, KD = T // P, D // P
EPS = 1e-6
NEG = -1e30
LOW = -3e38
GONE = -3.4e38
THETA = 500000.0
RAW, SPL = 6, 4
PIECE = 1024
H8 = 8
TOPK = min(256, T // 4)
NGRP, EPG, FF = 8, 4, 256
CAP = 128
DIL = ((128, 1), (512, 4), (2048, 16))
MEM = 256
MH = 4
HD = 128

C_CQ, C_CKV, C_KR, C_QB, C_KB, C_VB, C_QI, C_KI, C_WI, C_GA, C_GB = np.cumsum(
    [0, 384, 256, 32, 512, 512, 512, 512, 64, 8, 1024]).tolist()


def shape_constants():
    parts, at, n = [], {}, 0

    def add(name, a):
        nonlocal n
        a = np.ascontiguousarray(a, np.float32).reshape(P, -1)
        at[name] = (n, a.shape[1])
        parts.append(a)
        n += a.shape[1]

    p = np.arange(P)
    add("ident", np.eye(P))
    chunk_mask = np.where((p[None, :] // 64) <= (p[:, None] // 64), 0.0, NEG)
    add("cmask", np.concatenate([np.zeros((P, 384)), chunk_mask], 1))
    pos = (np.arange(NT)[None, :] * P + p[:, None]).astype(np.float32)
    for name, rot in (("A", 32), ("B", 16)):
        half = rot // 2
        inv = np.float32(THETA) ** (-np.arange(half, dtype=np.float32) * np.float32(2.0) / np.float32(rot))
        ang = pos[:, :, None] * inv.astype(np.float32)[None, None, :]
        add("cos" + name, np.cos(ang))
        add("sin" + name, np.sin(ang))
    add("ones", np.ones((P, P)))
    base_end = n
    add("before", (p[:, None] < p[None, :]).astype(np.float32))
    add("iota_g", np.broadcast_to(np.arange(8), (P, 8)))
    add("iota_s", np.broadcast_to(np.arange(P), (P, P)))
    add("iota_p", p[:, None])
    moe_end = n
    dp = 4 * (p[:, None] - p[None, :])
    add("wmask", np.stack([np.where((dp + d >= 0) & (dp + d <= 128), 0.0, NEG)
                           for d in (3, 2, 1, 0, -1, -2, -3)], 1))
    add("dmask", np.stack([np.where(p[None, :] <= p[:, None], 0.0, NEG),
                           np.where((p[None, :] <= p[:, None]) & ((p[:, None] - p[None, :]) % 4 == 0), 0.0, NEG)], 1))
    inv2 = np.float32(THETA) ** (-np.arange(0, 32, 2, dtype=np.float32) / np.float32(32))
    add("inv2", np.broadcast_to(inv2, (P, 16)))
    dil_end = n
    s, t = p[:, None], p[None, :]
    levels = []
    for half in (1, 2, 4, 8, 16, 32, 64):
        levels.append((s // (2 * half) == t // (2 * half)) & (s // half % 2 == 0) & (t // half % 2 == 1))
    levels.append(s == t)
    add("lmask", np.stack(levels, 1))
    sg = np.ones(T)
    sg[::64] = 0.0
    add("seg", np.broadcast_to(sg, (P, T)))
    return np.concatenate(parts, 1), at, (base_end, moe_end, dil_end, n)


CONST, CAT, (C_BASE, C_MOE, C_DIL, C_ALL) = shape_constants()


def build(nc, A, out):
    ctx = ExitStack()
    with ctx:
        def sb(name, shape, dt=F32):
            return ctx.enter_context(nc.sbuf_tensor(name, shape, dt))

        sems = {}

        def S(name):
            if name not in sems:
                sems[name] = ctx.enter_context(nc.semaphore(name))
            return sems[name]

        wraw = sb("wraw", [P, RAW, PIECE])
        whi = sb("whi", [P, SPL, PIECE], F32R)
        wlo = sb("wlo", [P, SPL, PIECE], F32R)
        AT_hi = sb("AT_hi", [P, 12, T], F32R)
        AT_lo = sb("AT_lo", [P, 12, T], F32R)
        y_hi = sb("y_hi", [P, 1024], F32R)
        y_lo = sb("y_lo", [P, 1024], F32R)
        comb_s = sb("comb_s", [P, NT, 8], F32R)
        small = sb("small", [P, 720])
        flag = sb("flag", [1, 2], I32)
        posi = sb("posi", [P, NT], I32)
        n_arena = 23760
        arena = sb("arena", [P, n_arena])
        pb = ctx.enter_context(nc.psum_tensor("pb", [P, 8, 512], F32))
        ACC = [pb[:, i, :] for i in range(4)]
        TP = [pb[:, 4 + i, :] for i in range(2)]
        SC = [pb[:, 6 + i, :] for i in range(2)]

        x_mid = nc.dram_tensor("x_mid", (T, D), F32, kind="Internal").ap()
        x_mid2 = nc.dram_tensor("x_mid2", (T, D), F32, kind="Internal").ap()

        top = [0]
        marks = {}

        def take(n, *shape, **kw):
            a = top[0]
            top[0] += n
            assert top[0] <= n_arena, (top[0], n_arena)
            return view(a, n, *shape)

        def view(a, n, *shape):
            v = arena[:, a:a + n]
            if len(shape) <= 1:
                return v
            names = "abcd"[:len(shape)]
            return v.rearrange("p (" + " ".join(names) + ") -> p " + " ".join(names),
                               **{k: m for k, m in zip(names, shape)})

        stat_at = [0]

        def stat(n):
            a = stat_at[0]
            stat_at[0] += n
            assert stat_at[0] <= 720
            return small[:, a:a + n]

        base0 = take(C_BASE)

        def const(name, where, first):
            a, n = CAT[name]
            return where[:, a - first:a - first + n]

        ident = const("ident", base0, 0)
        cmask = const("cmask", base0, 0)
        ones = const("ones", base0, 0)
        ropeA = [const(k + "A", base0, 0).rearrange("p (t c) -> p t c", t=NT) for k in ("cos", "sin")]
        ropeB = [const(k + "B", base0, 0).rearrange("p (t c) -> p t c", t=NT) for k in ("cos", "sin")]
        gains = take(64)
        g_mix, g_cq, g_ckv, g_ffn = gains[:, 0:8], gains[:, 8:11], gains[:, 11:13], gains[:, 13:21]
        g_n2 = [gains[:, 21:29], gains[:, 29:37]]
        g_mem = [gains[:, 37:45], gains[:, 45:53]]
        AT_mem_hi, AT_mem_lo = (a[:, 8:12, :].rearrange("p a b -> p (a b)").rearrange("p (k m) -> p k m", k=KD)
                                for a in (AT_hi, AT_lo))
        phase0 = top[0]

        pieces = []
        chunks = []
        CH = {}

        def chunk(name, srcs, n, at, k, per, nt=NT, mem=False, order=None):
            first = len(pieces)
            for k0 in (order or range(k))[::per]:
                loads, c0 = [], 0
                for s in srcs:
                    w = s.shape[2]
                    loads.append((c0, w, s[:, k0:k0 + per, :]))
                    c0 += w
                assert c0 == n and per * n <= PIECE
                pieces.append((loads, per, n))
            CH[name] = len(chunks)
            chunks.append(dict(first=first, count=k // per, n=n, at=at, per=per, nt=nt, mem=mem))

        def tiled(w):
            return w.rearrange("(k p) n -> p k n", p=P)

        w_in = tiled(A["w_in"][0])
        for i in range(2):
            chunk(f"cqkv{i}", [w_in[:, :, 336 * i:336 * i + 336]], 336, 0, 8, 2)
        w_uq = tiled(A["w_uq"][0])
        for i in range(2):
            chunk(f"uq{i}", [w_uq[:, :, 384 * i:384 * i + 384]], 384, 8, 3, 1)
        chunk("uv", [tiled(A["w_uv"][0])], 512, 8, 2, 2)
        chunk("uk", [tiled(A["w_uk"][0])], 512, 8, 2, 2)
        for i in range(2):
            chunk(f"idx{i}", [w_in[:, :, C_QI + 292 * i:C_QI + 292 * i + 292]], 292, 0, 8, 2)
        for i in range(3):
            chunk(f"qkvb{i}", [w_in[:, :, C_QB + 512 * i:C_QB + 512 * i + 512]], 512, 0, 8, 2)
        for ab, c0, w in (("a", C_GA, "w_o_a"), ("b", C_GB, "w_o_b")):
            for i in range(2):
                chunk(f"g{ab}{i}", [w_in[:, :, c0 + 512 * i:c0 + 512 * i + 512]], 512, 0, 8, 2)
            for i in range(2):
                chunk(f"o{ab}{i}", [tiled(A[w][0])[:, :, 512 * i:512 * i + 512]], 512, 8, 4, 2)
        for i in range(2):
            chunk(f"out{i}", [tiled(A["w_out"][0])[:, :, 512 * i:512 * i + 512]], 512, 0, 8, 2)
        P_MOE = len(pieces)
        GROUP_ORDER = [(kind, e, q) for kind, e, n in (("gu", 0, 4), ("gu", 1, 4), ("dn", 0, 2), ("gu", 2, 4), ("dn", 1, 2),
                                                       ("gu", 3, 4), ("dn", 2, 2), ("dn", 3, 2)) for q in range(n)]
        PPG = len(GROUP_ORDER)
        piece_of = {what: j for j, what in enumerate(GROUP_ORDER)}
        for what in range(NGRP * PPG):
            pieces.append(None)

        def memory_chunks(l, w_q):
            w = tiled(A["w_mem_kv_2"][l])
            chunk(f"mkv{l}0", [w[:, :, 0:512]], 512, 8, 8, 2, nt=2, mem=True)
            chunk(f"qm{l}", [w_q], 512, 0, 8, 2)
            chunk(f"mkv{l}1", [w[:, :, 512:1024]], 512, 8, 8, 2, nt=2, mem=True)

        def gate_chunks(l, w, c0, w_out):
            for i in THIRDS[l] if l == 0 else ():
                chunk(f"gate{l}{i}", [w[:, :, c0 + 512 * i:c0 + 512 * i + 512]], 512, 0, 8, 2)
            for i in range(2):
                chunk(f"fin{l}{i}", [tiled(w_out)[:, :, 512 * i:512 * i + 512]], 512, 8, 12, 2,
                      order=[4 * i + k for i in THIRDS[l] for k in range(4)])

        THIRDS = ((0, 2, 1), (2, 0, 1))
        AQ = 3 * 1024
        w_a = tiled(A["w_in_a_2"][0])
        memory_chunks(0, w_a[:, :, 3 * AQ:3 * AQ + 512])
        for hd in range(8):
            for i, nm in enumerate("qkv"):
                c = AQ * i + P * hd
                chunk(f"{nm}d{hd}", [w_a[:, :, c + D * g:c + D * g + P] for g in range(3)], 384, 0, 8, 2)
        gate_chunks(0, w_a, 3 * AQ + 512, A["w_out_a_2"][0])
        w_b = tiled(A["w_in_b_2"][0])
        GATES = THIRDS[1][:1], THIRDS[1][1:]
        memory_chunks(1, w_b[:, :, 3072:3584])
        for hh in range(2):
            for i, nm in enumerate("qfv"):
                c = 1024 * i + 512 * hh
                chunk(f"{nm}l{hh}", [w_b[:, :, c:c + 512]], 512, 0, 8, 2)
            for i in GATES[hh]:
                chunk(f"gate1{i}", [w_b[:, :, 3584 + 512 * i:4096 + 512 * i]], 512, 0, 8, 2)
        gate_chunks(1, w_b, 3584, A["w_out_b_2"][0])
        NP = len(pieces)
        bank_uses = [[sum(c["nt"] > t for c in chunks[:j]) for t in range(NT)] for j in range(len(chunks) + 1)]
        readies = [sum(c["nt"] - 1 for c in chunks[:j]) for j in range(len(chunks) + 1)]

        BESIDE_PICKS = range(chunks[CH["ga0"]]["first"] + SPL, chunks[CH["gb0"]]["first"] + chunks[CH["gb0"]]["count"] + SPL)

        POOL_OF_8 = (1, 3, 7)
        assert PPG % 8 == 0

        def lo_by_pool(p):
            return p in BESIDE_PICKS or P_MOE <= p < P_MOE + NGRP * PPG and p % 8 in POOL_OF_8

        def slot_cols(p):
            return PIECE if pieces[p] is None else pieces[p][1] * pieces[p][2]

        TPU, ntp = {}, [0]

        def tpu(name, n):
            TPU[name] = ntp[0]
            ntp[0] += n

        for name, n in (("n1", 8), ("cq", 3), ("ckv", 2), ("qa", 8), ("ka", 8), ("mla", 32), ("oa", 4),
                        ("qi", 4), ("ki", 1), ("qkb", 8), ("dsa", 32), ("ob", 4), ("y", 8), ("h2", 8)):
            tpu(name, n)
        ntp[0] += ntp[0] % 2
        assert ntp[0] == TPU["h2"] + 8, "an even start keeps the loop's bank parity"
        tpu("moe", 2 * NGRP)
        def mem_units(l):
            for name, n in ((f"mem{l}", 8), (f"n{l + 2}", 8), (f"km{l}", 4), (f"qm{l}", 4), (f"mat{l}", 16)):
                tpu(name, n)
        mem_units(0)
        for hd in range(9):
            for name, n, there in (("da0", 2, hd), ("da1", 2, hd), ("dq", 3, hd < 8), ("da2", 2, hd), ("da3", 2, hd), ("dk", 3, hd < 8)):
                if there:
                    tpu(f"{name}_{hd - (name[1] == 'a')}", n)
                elif name == "dq":
                    tpu("y00", 4)
        tpu("y01", 4)
        tpu("y02", 4)
        mem_units(1)
        for hh in range(2):
            tpu(f"ql{hh}", 4)
            tpu(f"fl{hh}", 4)
        for c in range(3):
            tpu(f"y1{c}", 4)
        AU, nau = {}, 0
        for name, n in (("mla", 32), ("dsa", 32), ("mat0", 16), ("dil", 32), ("mat1", 16)):
            AU[name] = nau
            nau += n

        raw_in = [S(f"raw_in{i}") for i in range(RAW)]
        hi_done = S("hi_done")
        lo_done = [S(f"lo_done{i}") for i in range(SPL)]
        piece_used = S("piece_used")
        acc_ready = S("acc_ready")
        acc_free = [S(f"acc_free{t}") for t in range(NT)]
        tp_ready = S("tp_ready")
        tp_free = [S(f"tp_free{i}") for i in range(2)]
        act_hi = S("act_hi")
        att_s, att_m, att_p = S("att_s"), S("att_m"), S("att_p")
        att_r, att_o, att_done = S("att_r"), S("att_o"), S("att_done")
        phase = S("phase")

        xr = take(4096, NT, D)
        cqkv = view(phase0, 2688, NT, 672)
        top[0] = phase0 + 4096
        qk_tok = take(3072, NT, H8, 96)
        qaT = take(4096, H8, T)
        kaT = take(4096, H8, T)
        v_a = take(2048, NT, 512)
        work = take(3072)
        att_s_sb = [work[:, 512 * i:512 * i + 512] for i in range(4)]
        att_pt = [work[:, 2048:2560], work[:, 2560:3072]]
        o_tok = qk_tok.rearrange("p a b c -> p (a b c)")[:, 0:2048].rearrange("p (t c) -> p t c", t=NT)
        ropetmp = work[:, 0:2048]
        a0 = phase0
        qkvb = view(a0, 6144, NT, 1536)
        idx = view(a0 + 6144, 2336, NT, 584)
        score = view(a0 + 6144, 1536, 3, 512)
        qkbT = view(a0 + 8480, 4096, 8, T)
        qiT = view(a0 + 12576, 2048, 4, T)
        kiT = view(a0 + 14624, 512)
        o_tokb = qkvb[:, :, 0:512]
        y_pos = a0 + 8480 + 4096 + 2048 + 512
        y1 = view(y_pos, 4096, NT, D)
        gb = [view(a0 + 12576, 2048, NT, 512),
              view(a0 + 8480, 2048, NT, 512)]
        x1 = view(a0, 4096, NT, D)
        work2 = view(y_pos + 4096, 3072)
        assert y_pos + 4096 + 3072 <= n_arena
        s_sb2 = [work2[:, 512 * i:512 * i + 512] for i in range(4)]
        pt2 = [work2[:, 2048:2560], work2[:, 2560:3072]]
        rel = [work2[:, 0:512], work2[:, 512:1024]]
        tk = work2[:, 1024:1536]
        kidup = work2[:, 2048:2560].rearrange("p (t c) -> p t c", t=NT)
        ropetmp2 = work2[:, 0:3072]
        wi_s = stat(32).rearrange("p (t h) -> p t h", t=NT)
        max8 = stat(8)

        def norm_cols(n):
            return dict(ss=stat(n), ms=stat(n), rt=stat(n), rs=stat(n))

        ns = {name: norm_cols(4) for name in ("n1", "cq", "ckv", "ffn", "final", "n2", "n3")}
        for l in range(2):
            ns[f"mem{l}"] = norm_cols(2)
            ns[f"km{l}"] = norm_cols(8)
            ns[f"qm{l}"] = norm_cols(16)
        qk_n = norm_cols(12)
        q_rs = [stat(12).rearrange("p (t g) -> p t g", t=NT) for _ in range(2)]
        k_rs = stat(12).rearrange("p (t g) -> p t g", t=NT)
        gl_n = norm_cols(32)
        att_mx, att_nm, att_l, att_rl = stat(12), stat(4), stat(4), stat(4)

        w_slot = lambda buf, p, i: buf[:, i, 0:slot_cols(p)]

        def mla_unit(i):
            h, qt = i // NT, i % NT
            kw = P * (qt + 1)
            return dict(q=qaT[0:96, h, qt * P:qt * P + P], k=kaT[0:96, h, 0:kw], mask=cmask[:, 512 - kw:512], scale=96 ** -0.5,
                        kw=kw, v=[v_a[:, b, 64 * h:64 * h + 64] for b in range(qt + 1)],
                        dv=64, o=o_tok[:, qt, 64 * h:64 * h + 64], sb=att_s_sb, pt=att_pt)

        def dsa_unit(i):
            h, qt = i // NT, i % NT
            kw = P * (qt + 1)
            r0 = 64 * (h % 2)
            mask = cmask[:, 384:512] if qt == 0 else score[:, qt - 1, 0:kw]
            return dict(q=qkbT[r0:r0 + 64, h // 2, qt * P:qt * P + P], k=qkbT[r0:r0 + 64, 4 + h // 2, 0:kw], mask=mask, scale=0.125,
                        kw=kw, v=[qkvb[:, b, 1024 + 64 * h:1088 + 64 * h] for b in range(qt + 1)],
                        dv=64, o=o_tokb[:, qt, 64 * h:64 * h + 64], sb=s_sb2, pt=pt2)

        top[0] = a0 + 4096
        c_moe = take(C_MOE - C_BASE)
        before, iota_g, iota_s, iota_p = (const(k, c_moe, C_BASE) for k in ("before", "iota_g", "iota_s", "iota_p"))
        h2T = take(4096, KD, T)
        w_rt = take(KD * 40, KD, 40)
        b_rt = take(40)
        gen_d = view(top[0], 2048, 2, D)
        lg = take(NT * 40, NT, 40)
        rt = take(1200)
        key = take(NT)
        keyb = take(NT * P, NT, P)
        keyrow = take(T)
        comb4 = take(NT * EPG, NT, EPG)
        comb32 = take(NT * 32, NT, 32)
        wslot = take(EPG)
        sg_sb = [take(FF) for _ in range(2)]
        hid_sb = [take(FF) for _ in range(2)]
        fin_g = take(D)
        big = take(4096)
        bigt = big.rearrange("p (t d) -> p t d", t=NT)
        rt_at = [0]

        def route(*shape):
            n = int(np.prod(shape))
            a = rt[:, rt_at[0]:rt_at[0] + n]
            rt_at[0] += n
            assert rt_at[0] <= 1200
            names = "abc"[:len(shape)]
            return a if len(shape) == 1 else a.rearrange("p (" + " ".join(names) + ") -> p " + " ".join(names),
                                                         **dict(zip(names, shape)))

        r_gmax, r_gi, r_m1, r_m2, r_min4, r_d2, r_e2, r_sum, r_w1, r_w2, r_rank, r_over = (route(NT) for _ in range(12))
        r_d, r_e, r_eq, r_cand, oneh = (route(NT, 8) for _ in range(5))
        r_in4, r_in4b, r_eq4, r_cand4, r_oh1, r_oh2 = (route(NT, EPG) for _ in range(6))
        r_el = route(NT, 8, EPG)
        gen_gu = big.rearrange("p (w k f) -> p w k f", w=2, k=KD)
        gen_sil = take(1024, 2, T)
        gen_hid = take(1024, 2, T)
        xs_hi = AT_hi[:, 0:8, :].rearrange("p a b -> p (a b)").rearrange("p (t d) -> p t d", t=NT)
        xs_lo = AT_lo[:, 0:8, :].rearrange("p a b -> p (a b)").rearrange("p (t d) -> p t d", t=NT)
        spare_hi = AT_hi[:, 8:12, :].rearrange("p a b -> p (a b)")
        spare_lo = AT_lo[:, 8:12, :].rearrange("p a b -> p (a b)")
        xg_hi = spare_hi[:, 0:1024].rearrange("p (k s) -> p k s", k=KD)
        xg_lo = spare_lo[:, 0:1024].rearrange("p (k s) -> p k s", k=KD)
        hd_hi = [spare_hi[:, 1024 + 256 * i:1280 + 256 * i] for i in range(2)]
        hd_lo = [spare_lo[:, 1024 + 256 * i:1280 + 256 * i] for i in range(2)]
        pick = spare_hi[:, 1536:2048].rearrange("p (t s) -> p t s", t=NT)
        put = spare_lo[:, 1536:2048]
        w_g_e = A["w_gate"][0].rearrange("e (k p) f -> e p k f", p=P)
        w_u_e = A["w_up"][0].rearrange("e (k p) f -> e p k f", p=P)
        w_d_e = A["w_down"][0].rearrange("e (k p) d -> e p k d", p=P)

        moe_top = top[0]

        top[0] = phase0
        mix = take(6144, NT, 1536)
        l2_0 = top[0]
        mem_at = a0 + 19712
        assert mem_at >= moe_top
        memx = [view(mem_at, 2048, 2, D), take(2048, 2, D)]
        km_tok = take(1024, 2, 512)
        vm = take(1024, 2, 512)
        kmT = take(1024, MH, MEM)
        qm_tok = take(2048, NT, 512)
        qmT = take(2048, MH, T)
        mg = [view(mem_at + 2048, 256), take(256)]
        mwork = take(2048)
        ms_sb = [mwork[:, 256 * i:256 * i + 256] for i in range(4)]
        mpt = [mwork[:, 1024:1280], mwork[:, 1280:1536]]
        msq = mwork[:, 1536:2048]
        xn_at = take(2048)
        assert top[0] <= mem_at
        xn = [memx[1][:, t, :] for t in range(2)] + [xn_at[:, D * t:D * t + D] for t in range(2)]
        junkD = km_tok.rearrange("p a b -> p (a b)")
        mjunk = mwork[:, 0:1024]
        top[0] = l2_0
        c_dil = take(C_DIL - C_MOE)
        wmask, dmask, inv2 = (const(k, c_dil, C_MOE) for k in ("wmask", "dmask", "inv2"))
        qkg = take(768, 3, 2, P)
        cos2 = take(64, NT, 16)
        sin2 = take(64, NT, 16)
        qT = take(3072, 2, 3, T)
        kT = take(3072, 2, 3, T)
        v2 = take(3072, 2, NT, 3 * P)
        qk_t = take(1536, NT, 3 * P)
        d_s = take(768)
        d_pt = take(768)
        rtmp = take(768)
        sqb = take(384)
        silu_sb = [qk_t.rearrange("p a b -> p (a b)")[:, 512 * i:512 * i + 512] for i in range(2)]
        rot_r, rot_c, rot_a, rot_k = (rtmp[:, 64 * i:64 * i + 64].rearrange("p (t c) -> p t c", t=NT) for i in range(4))
        rot_p = rtmp[:, 256:256 + NT]
        junkE = qk_t.rearrange("p a b -> p (a b)")[:, 0:1024]
        n3x = view(phase0, 4096, NT, D)
        res2 = view(l2_0 + (C_DIL - C_MOE) + 896, 4096, NT, D)
        top[0] = l2_0
        c_gla = take(C_ALL - C_DIL)
        lmask, seg = (const(k, c_gla, C_DIL) for k in ("lmask", "seg"))
        lmask = lmask.rearrange("p (l c) -> p l c", c=P)
        og = take(P)
        lbl = take(16, 2, 8)
        lb = take(8)
        lb1 = take(8)
        at_ltok = top[0]
        l_tok = take(2048, NT, 512)
        lA = l_tok.rearrange("p a b -> p (a b)").rearrange("p (s t) -> p s t", s=NT)
        at_lq = top[0]
        lq = take(2048, 4, T)
        lk = take(2048, 4, T)
        lf = take(2048, 4, T)
        lv = take(2048, NT, 512)
        G64, G512 = ([take(T) for _ in range(2)] for _ in range(2))
        kq = [take(T) for _ in range(5)]
        res3 = view(at_lq + 2048, 4096, NT, D)
        lsq = [[lv[:, t, :] for t in range(NT)], kq[0:NT]]
        silu_b = [lq[:, t, :] for t in range(3)] + [G64[0]]

        def halves(a, half):
            v = a.rearrange("p (n s c) -> p n s c", s=2, c=half)
            return v[:, :, 0, :], v[:, :, 1, :]

        def AT_perm(a, k):
            return a[:, k, :].rearrange("p (r t q) -> p t q r", r=4, t=NT)

        def mem_unit(i):
            h, qt = i // NT, i % NT
            return dict(q=qmT[:, h, qt * P:qt * P + P], k=kmT[:, h, :], mask=None, scale=HD ** -0.5, kw=MEM,
                        v=[vm[:, b, P * h:P * h + P] for b in range(2)], dv=P,
                        o=mix[:, qt, 1024 + P * h:1152 + P * h], sb=ms_sb, pt=mpt)

        def dil_unit(hd, r):
            b = hd % 2
            q = lambda g: qT[:, b, g, r * P:r * P + P]
            sc = lambda g: q_rs[b][:, r, g:g + 1]
            return dict(s=[(DS[0], q(0), kT[:, b, 0, :], wmask[:, (3 - r) * P:(7 - r) * P], sc(0)),
                           (DS[1], q(1), kT[:, b, 1, r * P:r * P + P], dmask[:, 0:P], sc(1)),
                           (DS[2], q(2), kT[:, b, 2, r * P:r * P + P], dmask[:, P:2 * P], sc(2))],
                        v=[v2[:, b, c, 0:P] for c in range(4)] + [v2[:, b, r, P:2 * P], v2[:, b, r, 2 * P:3 * P]],
                        o=mix[:, r, P * hd:P * hd + P], U=AU["dil"] + NT * hd + r)

        DS = [SC[0], SC[1][:, 0:P], SC[1][:, P:2 * P]]
        D_OUT = SC[1][:, 2 * P:3 * P]

        def attention_step(i):
            return ("scores", "probs", "output")[i % 3], i // 3

        AHEAD = 3
        LOOK = 3

        def gate_steps(hh):
            pairs = [(f"gate1{i}", q, t) for i in GATES[hh] for q in range(4) for t in range(NT)]
            return [(2 + 2 * s if hh == 0 else 1 + s + 4 * (s // 16),) + step for s, step in enumerate(pairs)]

        def halving(m):
            return 9 * (m // 10) + max(m % 10, 1) - 1

        def scores_out(u, n):
            return ACC[u % 4][:, 0:n]

        block = ctx.enter_context(nc.Block())

        @block.sync
        def _(sp):
            for t in range(NT):
                sp.dma_start(xr[:, t, :], A["x"][0, t * P:t * P + P, :]).then_inc(S(f"x_in{t}"), 16)

            def load(p):
                loads, per, n = pieces[p]
                if p >= RAW:
                    sp.wait_ge(lo_done[(p - RAW) % SPL], (p - RAW) // SPL + 1)
                dst = wraw[:, p % RAW, 0:per * n].rearrange("p (k n) -> p k n", k=per)
                share = 96 // len(loads)
                for c0, w, src in loads:
                    sp.dma_start(dst[:, :, c0:c0 + w], src).then_inc(raw_in[p % RAW], share)

            for p in range(P_MOE):
                load(p)
            with sp.Fori(0, NGRP) as g:
                for j, (kind, e, q) in enumerate(GROUP_ORDER):
                    p = P_MOE + j
                    one = bass.ds(sp.snap(g * EPG + e), 1)
                    sp.wait_ge(lo_done[(p - RAW) % SPL], g * (PPG // SPL) + ((p - RAW) // SPL + 1))
                    if kind == "gu":
                        dst = wraw[:, p % RAW, :].rearrange("p (k n) -> p k n", k=2)
                        for i, w in enumerate((w_g_e, w_u_e)):
                            sp.dma_start(dst[:, :, FF * i:FF * i + FF],
                                         w[one, :, 2 * q:2 * q + 2, :].rearrange("e p k f -> p (e k) f")
                                         ).then_inc(raw_in[p % RAW], 48)
                    else:
                        sp.dma_start(wraw[:, p % RAW, :], w_d_e[one, :, q, :].rearrange("e p f -> p (e f)")
                                     ).then_inc(raw_in[p % RAW], 96)
            for p in range(P_MOE + NGRP * PPG, NP):
                load(p)

        NORMS = (("n1", 4, 4, 0), ("cq", 4, 4, 0), ("ckv", 4, 4, 0), ("ffn", 4, 4, 0), ("mem0", 2, 2, 0), ("final", 4, 0, 0),
                 ("n2", 4, 4, 0), ("km0", 0, 8, 2), ("qm0", 0, 16, 4), ("mem1", 2, 2, 0), ("n3", 4, 4, 0), ("km1", 0, 8, 2),
                 ("qm1", 0, 16, 4))
        ORDER = [n[0] for n in NORMS]
        norm_ss, norm_ms, norm_rt, norm_xs = S("norm_ss"), S("norm_ms"), S("norm_rt"), S("norm_xs")
        head_sq, head_red = S("head_sq"), S("head_red")

        def so_far(name, what, n):
            return sum(row[what] for row in NORMS[:ORDER.index(name)]) + n

        def wait_acc(eng, j, t):
            c = chunks[j]
            if t == c["nt"] - 1:
                eng.wait_ge(piece_used, c["first"] + c["count"])
            else:
                eng.wait_ge(acc_ready, readies[j] + t + 1)

        def wait_tp_read(eng, name, n):
            for par in range(2):
                last = max(u for u in range(TPU[name], TPU[name] + n) if u % 2 == par) if n > 1 or TPU[name] % 2 == par else None
                if last is not None:
                    eng.wait_ge(tp_free[par], last // 2 + 1)

        def wait_used(eng, name):
            eng.wait_ge(piece_used, chunks[CH[name]]["first"] + chunks[CH[name]]["count"])

        def wait_read(eng, name, t):
            eng.wait_ge(acc_free[t], bank_uses[CH[name]][t] + 1)

        phases = {"PE": 0, "ACT": 0, "DVE": 0, "POOL": 0}

        def end_phase(eng, who):
            phases[who] += 1
            eng.drain().then_inc(phase, 1)
            eng.wait_ge(phase, 4 * phases[who])

        @block.gpsimd
        def _(pool):
            chain = [0]

            def link(ins):
                chain[0] += 1
                ins.then_inc(S("pool_step"), 1)
                pool.wait_ge(S("pool_step"), chain[0])

            def rope(x1, x2, cos, sin, tmp, shape):
                n = int(np.prod(shape))
                v = [tmp[:, i * n:i * n + n].rearrange("p (t h c) -> p t h c", t=shape[0], h=shape[1]) for i in range(4)]
                bc = lambda a: a.unsqueeze(2).broadcast_to([P] + list(shape))
                c, s = bc(cos), bc(sin)
                pool.tensor_tensor(v[0], x1, c, ALU.mult)
                pool.tensor_tensor(v[1], x2, s, ALU.mult)
                pool.tensor_tensor(v[2], x2, c, ALU.mult)
                link(pool.tensor_tensor(v[3], x1, s, ALU.mult))
                pool.tensor_tensor(x1, v[0], v[1], ALU.subtract)
                return pool.tensor_tensor(x2, v[2], v[3], ALU.add)

            pool.wait_ge(S("consts"), 16)

            def load_memory(l):
                pool.dma_start(memx[l], A["mem_2"][0].rearrange("(t p) d -> p t d", p=P)).then_inc(S(f"memx{l}"), 16)
                for i, w in enumerate(("mem_q_gain_2", "mem_k_gain_2")):
                    pool.dma_start(mg[l][:, P * i:P * i + P], A[w][l:l + 1, :].broadcast_to([P, P])).then_inc(S(f"memx{l}"), 16)

            for i in range(2):
                for t in range(NT):
                    wait_read(pool, f"uq{i}", t)
                q = qk_tok[:, :, 4 * i:4 * i + 4, :]
                for t in range(NT):
                    r = rope(q[:, t:t + 1, :, 64:80], q[:, t:t + 1, :, 80:96], ropeA[0][:, t:t + 1], ropeA[1][:, t:t + 1],
                             ropetmp[:, 256 * t:256 * t + 256], (1, 4, 16))
                r.then_inc(S("qa_rot"), 1)
            kr = cqkv[:, :, 640:672].unsqueeze(2)
            rope(kr[:, :, :, 0:16], kr[:, :, :, 16:32], ropeA[0], ropeA[1], ropetmp[:, 1024:1280], (NT, 1, 16)
                 ).then_inc(S("kr_rot"), 1)
            end_phase(pool, "POOL")

            for tok, n, last in ((idx, 9, "idx1"), (qkvb, 16, "qkvb1")):
                for t in range(NT):
                    wait_read(pool, last, t)
                x = tok[:, :, 0:64 * n].rearrange("p t (h c) -> p t h c", h=n)
                for t in range(NT):
                    r = rope(x[:, t:t + 1, :, 0:8], x[:, t:t + 1, :, 8:16], ropeB[0][:, t:t + 1], ropeB[1][:, t:t + 1],
                             ropetmp2[:, 512 * t:512 * t + 512], (1, n, 8))
                link(r)
                if tok is idx:
                    for half in range(2):
                        pool.tensor_copy(kidup[:, :, 64 * half:64 * half + 64], idx[:, :, 512:576])
                    r = pool.tensor_scalar(wi_s, idx[:, :, 576:584], H8 ** -0.5, None, ALU.mult)
                else:
                    r = pool.nop()
                r.then_inc(S("b_rot"), 1)
            for p in BESIDE_PICKS:
                pool.wait_ge(hi_done, p + 1)
                pool.tensor_tensor(w_slot(wlo, p, p % SPL), w_slot(wraw, p, p % RAW), w_slot(whi, p, p % SPL).bitcast(F32),
                                   ALU.subtract).then_inc(lo_done[p % SPL], 1)
            wait_tp_read(pool, "ob", 4)
            pool.dma_start(x1, A["x"][0].rearrange("(t p) d -> p t d", p=P)).then_inc(S("res1"), 16)

            pool.wait_ge(S("y_sum"), 2 * NT)
            pool.dma_start(c_moe, A["const"][:, C_BASE:C_MOE]).then_inc(S("moe_in"), 16)
            pool.dma_start(w_rt[:, :, 0:8], tiled(A["w_router_group"][0])).then_inc(S("moe_in"), 16)
            pool.dma_start(w_rt[:, :, 8:40], tiled(A["w_router_expert"][0])).then_inc(S("moe_in"), 16)
            pool.dma_start(b_rt[:, 0:8], A["b_router_group"][0:1, :].broadcast_to([P, 8])).then_inc(S("moe_in"), 16)
            pool.dma_start(b_rt[:, 8:40], A["b_router_expert"][0:1, :].broadcast_to([P, 32])).then_inc(S("moe_in"), 16)
            pool.dma_start(fin_g, A["final_norm_g"].unsqueeze(0).broadcast_to([P, D])).then_inc(S("moe_in"), 16)
            load_memory(0)
            for t in range(NT):
                pool.wait_ge(S("xs_hi"), t + 1)
                pool.tensor_tensor(xs_lo[:, t, :], bigt[:, t, :], xs_hi[:, t, :].bitcast(F32), ALU.subtract
                                   ).then_inc(S("xs_lo"), 1)
            with pool.Fori(0, NGRP) as g:
                for j in range(PPG):
                    p = P_MOE + j
                    if p % 8 in POOL_OF_8:
                        pool.wait_ge(hi_done, g * PPG + (p + 1))
                        pool.tensor_tensor(wlo[:, p % SPL, :], wraw[:, p % RAW, :], whi[:, p % SPL, :].bitcast(F32),
                                           ALU.subtract).then_inc(lo_done[p % SPL], 1)
            pool.wait_ge(S("flag_in"), 1)
            pool.wait_ge(S("moe_end"), 1)
            with pool.If(pool.value_load(flag[0:1, 0:1], min_val=0, max_val=T) > 0):
                with pool.Fori(0, NGRP * EPG) as e:
                    one = bass.ds(e, 1)
                    pool.wait_ge(S("gen_y"), e * 8 + 8)
                    pool.dma_start(gen_gu[:, 0, :, :], w_g_e[one].rearrange("e p k f -> p (e k) f")).then_inc(S("gen_in"), 16)
                    pool.dma_start(gen_gu[:, 1, :, :], w_u_e[one].rearrange("e p k f -> p (e k) f")).then_inc(S("gen_in"), 16)
                    pool.dma_start(gen_d, w_d_e[one].rearrange("e p k f -> p (e k) f")).then_inc(S("gen_in"), 16)
            end_phase(pool, "POOL")

            for t in range(NT):
                pool.wait_ge(S("fin_x"), t + 1)
                pool.dma_start(x_mid[t * P:t * P + P, :], xn[t]).then_inc(S("mid_out"), 16)
            pool.wait_ge(S("mid_out"), 16 * NT)
            end_phase(pool, "POOL")

            pool.dma_start(c_dil, A["const"][:, C_MOE:C_DIL]).then_inc(S("dil_in"), 16)
            for i, w in enumerate(("q_gain_a_2", "k_gain_a_2")):
                pool.dma_start(qkg[:, :, i, :], A[w][0:1].broadcast_to([P, 3, P])).then_inc(S("dil_in"), 16)
            pool.dma_start(posi[:, :], A["positions_2"].rearrange("o (p r) -> (o p) r", r=4)).then_inc(S("dil_in"), 16)
            pool.wait_ge(S("rot2"), 1)
            heads = qk_t.rearrange("p t (g c) -> p t g c", g=3)
            for n in range(16):
                pool.wait_ge(S("qk_rs"), n + 1)
                if n % 2:
                    link(pool.tensor_tensor(heads, heads, k_rs.unsqueeze(3).broadcast_to([P, NT, 3, P]), ALU.mult))
                rope(heads[:, :, :, 0:16], heads[:, :, :, 16:32], cos2, sin2, rtmp, (NT, 3, 16)).then_inc(S("qk_rot"), 1)
            end_phase(pool, "POOL")
            load_memory(1)
            for r in range(NT):
                pool.dma_start(res2[:, r, :], x_mid.rearrange("(p r) d -> r p d", r=4)[r]).then_inc(S("res2"), 16)
            for r in range(NT):
                wait_read(pool, "fin01", r)
                pool.dma_start(x_mid2.rearrange("(p r) d -> r p d", r=4)[r], res2[:, r, :]).then_inc(S("mid_out2"), 16)
            pool.wait_ge(S("mid_out2"), 16 * NT)
            end_phase(pool, "POOL")

            pool.dma_start(c_gla, A["const"][:, C_DIL:C_ALL]).then_inc(S("gla_in"), 16)
            pool.dma_start(og, A["o_gain_b_2"][0:1, :].broadcast_to([P, P])).then_inc(S("gla_in"), 16)
            with nc.allow_non_contiguous_dma(reason="a column of lower bounds for each head"):
                for i in range(2):
                    pool.dma_start(lbl[:, i, :], A["lb_logits_2"][i].rearrange("(h c) -> c h", c=P)).then_inc(S("gla_in"), 16)
            for hh in range(2):
                wait_tp_read(pool, f"fl{hh}", 4)
                pool.memset(lA, 0.0).then_inc(S("lA_zero"), 1)
                for n in range(36 * hh, 36 * hh + 36):
                    h, half = n // 9 % 4, 1 << n % 9
                    pool.wait_ge(S("gl_x"), n + 1)
                    e1, k1 = halves(kq[n % 5], half)[0], halves(lk[:, h, :], half)[0]
                    pool.tensor_tensor(e1, k1, e1, ALU.mult).then_inc(S("gl_k"), 1)
            pool.wait_ge(S("gl_od"), 8)
            pool.dma_start(res3, x_mid2.rearrange("(t p) d -> p t d", p=P)).then_inc(S("res3"), 16)
            for t in range(NT):
                wait_read(pool, "fin11", t)
                pool.dma_start(out[0, t * P:t * P + P, :], res3[:, t, :]).then_inc(S("out_done"), 16)
            pool.wait_ge(S("out_done"), 16 * NT)

        @block.scalar
        def _(act):
            his = [0]

            def feed(p):
                if p >= NP:
                    return
                act.wait_ge(raw_in[p % RAW], 96 * (p // RAW + 1))
                if p >= SPL:
                    act.wait_ge(piece_used, p - SPL + 1)
                act.activation(w_slot(whi, p, p % SPL), w_slot(wraw, p, p % RAW), ACT.Copy).then_inc(hi_done, 1)

            def during(j, fed=0):
                for i in range(fed, chunks[j]["count"] - 1):
                    feed(chunks[j]["first"] + i + SPL)

            def after(j):
                feed(chunks[j]["first"] + chunks[j]["count"] - 1 + SPL)

            def evac(name, dst, func=ACT.Copy, scale=1.0):
                j = CH[name]
                during(j)
                for t in range(chunks[j]["nt"]):
                    wait_acc(act, j, t)
                    src = ACC[t][:, 0:chunks[j]["n"]]
                    d = dst(t)
                    if len(d.shape) == 3:
                        src = src.rearrange("p (h c) -> p h c", h=d.shape[1])
                    act.activation(d, src, func, scale=scale).then_inc(acc_free[t], 1)
                after(j)

            def hi(name, i, dst, src, gain=None):
                act.wait_ge(tp_ready, TPU[name] + i + 1)
                act.activation(dst, src, ACT.Copy, scale=1.0 if gain is None else gain).then_inc(act_hi, 1)

            def tcopy(name, i, dst, src, scale=1.0):
                u = TPU[name] + i
                act.wait_ge(tp_ready, u + 1)
                act.activation(dst, src, ACT.Copy, scale=scale).then_inc(tp_free[u % 2], 1)

            def tb(name, i):
                return TP[(TPU[name] + i) % 2]

            def sumsq(src, junk, ss, name, t):
                if t:
                    act.wait_ge(norm_ss, so_far(name, 1, t))
                act.activation(junk, src, ACT.Square, accum_out=ss).then_inc(norm_ss, 1)

            def root(name, c):
                act.wait_ge(norm_ms, ORDER.index(name) + 1)
                act.activation(c["rt"], c["ms"], ACT.Sqrt).then_inc(norm_rt, 1)

            def attention(name, unit, n):
                U0 = AU[name]

                def out_of_psum(i):
                    u = unit(i)
                    U = U0 + i
                    act.wait_ge(att_o, U + 1)
                    act.wait_ge(att_r, U + 1)
                    act.activation(u["o"], SC[U % 2][:, 0:u["dv"]], ACT.Copy, scale=att_rl[:, U % 4:U % 4 + 1]
                                   ).then_inc(att_done, 1)

                def exponentials(i):
                    u = unit(i)
                    U = U0 + i
                    act.wait_ge(att_m, U + 1)
                    s = u["sb"][U % len(u["sb"])][:, 0:u["kw"]]
                    masked = u["mask"] is not None
                    act.activation(s, s if masked else scores_out(U, u["kw"]), ACT.Exp, bias=att_nm[:, U % 4:U % 4 + 1],
                                   scale=1.0 if masked else u["scale"],
                                   accum_out=att_l[:, U % 4:U % 4 + 1]).then_inc(att_p, 1)

                for i in range(n + 2):
                    if i < n:
                        exponentials(i)
                    if i >= 2:
                        out_of_psum(i - 2)

            def head_norm(name, chunk, tok, nt, dst, sq):
                for t in range(nt):
                    if t:
                        act.wait_ge(head_red, so_far(name, 3, t))
                    wait_read(act, chunk, t)
                    act.activation(sq, tok[:, t, :], ACT.Square).then_inc(head_sq, 1)
                root(name, dst)

            def memory_squares(l, junk):
                act.wait_ge(S(f"memx{l}"), 48)
                for t in range(2):
                    sumsq(memx[l][:, t, :], junk, ns[f"mem{l}"]["ss"][:, t:t + 1], f"mem{l}", t)

            def memory_root(l):
                root(f"mem{l}", ns[f"mem{l}"])

            def memory_hi(l):
                for k in range(KD):
                    hi(f"mem{l}", k, AT_mem_hi[:, k, :], tb(f"mem{l}", k)[:, 0:MEM], g_mem[l][:, k:k + 1])

            def memory_stage(l, ready, rows, junk, place):
                name = f"n{l + 2}"
                for t in range(NT):
                    ready(t)
                    sumsq(rows(t), junk, ns[name]["ss"][:, t:t + 1], name, t)
                root(name, ns[name])
                if l:
                    act.wait_ge(S("mid_out2"), 16 * NT)
                    act.wait_ge(norm_xs, so_far(name, 2, NT))
                evac(f"mkv{l}0", lambda t: km_tok[:, t, :])
                for k in range(KD):
                    hi(name, k, *place(k), g_n2[l][:, k:k + 1])
                head_norm(f"km{l}", f"mkv{l}0", km_tok, 2, ns[f"km{l}"], msq)
                evac(f"qm{l}", lambda t: qm_tok[:, t, :])
                for h in range(MH):
                    tcopy(f"km{l}", h, kmT[:, h, :], tb(f"km{l}", h)[:, 0:MEM])
                head_norm(f"qm{l}", f"qm{l}", qm_tok, NT, ns[f"qm{l}"], msq)
                evac(f"mkv{l}1", lambda t: vm[:, t, :])
                for h in range(MH):
                    tcopy(f"qm{l}", h, qmT[:, h, :], tb(f"qm{l}", h))
                attention(f"mat{l}", mem_unit, 16)

            def gate_out(l, c, tmp):
                j = CH[f"gate{l}{THIRDS[l][c]}"]
                for t in range(NT):
                    n = NT * c + t
                    wait_acc(act, j, t)
                    if l == 1 and c < 2:
                        act.activation(ACC[t], ACC[t], ACT.Silu).then_inc(S("silu_in"), 1)
                        continue
                    if l == 0 and n >= 2:
                        act.wait_ge(S("gated0"), n - 1)
                    act.activation(tmp[n % len(tmp)], ACC[t][:, :], ACT.Silu).then_inc(acc_free[t], 1)

            def gated_hi(l, c):
                if c == 1:
                    wait_used(act, f"gate{l}{THIRDS[l][2]}")
                for k in range(4):
                    hi(f"y{l}{c}", k, AT_hi[:, (8 + 4 * c + k) % 12, :], tb(f"y{l}{c}", k))

            act.dma_start(base0, A["const"][:, 0:C_BASE]).then_inc(S("consts"), 16)
            with nc.allow_non_contiguous_dma(reason="gains as columns"):
                for dst, src in ((g_mix, A["norm_mix_g"][0]), (g_cq, A["mla_q_norm_g"][0]), (g_ckv, A["mla_kv_norm_g"][0]),
                                 (g_ffn, A["norm_ffn_g"][0]), (g_n2[0], A["norm_gain_2"][0]), (g_n2[1], A["norm_gain_2"][1]),
                                 (g_mem[0], A["mem_norm_gain_2"][0]), (g_mem[1], A["mem_norm_gain_2"][1])):
                    act.dma_start(dst, src.rearrange("(k p) -> p k", p=P)).then_inc(S("gains_in"), 16)
            for t in range(NT):
                act.wait_ge(S(f"x_in{t}"), 16)
                sumsq(xr[:, t, :], work[:, 0:1024], ns["n1"]["ss"][:, t:t + 1], "n1", t)
            root("n1", ns["n1"])
            for p in range(SPL):
                feed(p)
            act.wait_ge(S("gains_in"), 128)
            for k in range(KD):
                hi("n1", k, AT_hi[:, k, :], tb("n1", k), g_mix[:, k:k + 1])
            for i in range(2):
                evac(f"cqkv{i}", lambda t: cqkv[:, t, 336 * i:336 * i + 336])
            for name, c0, w in (("cq", 0, 384), ("ckv", 384, 256)):
                for t in range(NT):
                    act.wait_ge(acc_free[t], 2)
                    sumsq(cqkv[:, t, c0:c0 + w], work[:, 0:w], ns[name]["ss"][:, t:t + 1], name, t)
                root(name, ns[name])
            for k in range(3):
                hi("cq", k, AT_hi[:, 8 + k, :], tb("cq", k), g_cq[:, k:k + 1])
            for i in range(2):
                evac(f"uq{i}", lambda t: qk_tok[:, t, 4 * i:4 * i + 4, :])
            wait_used(act, "uq1")
            for k in range(2):
                hi("ckv", k, AT_hi[:, 8 + k, :], tb("ckv", k), g_ckv[:, k:k + 1])
            evac("uv", lambda t: v_a[:, t, :])
            for h in range(H8):
                tcopy("qa", h, qaT[0:96, h, :], tb("qa", h)[0:96, :])
            evac("uk", lambda t: qk_tok[:, t, :, 0:64])
            for h in range(H8):
                tcopy("ka", h, kaT[0:96, h, :], tb("ka", h)[0:96, :])
            attention("mla", mla_unit, 32)
            for k in range(4):
                hi("oa", k, AT_hi[:, 8 + k, :], tb("oa", k))
            end_phase(act, "ACT")

            for name, tok, c0 in (("idx0", idx, 0), ("idx1", idx, 292), ("qkvb0", qkvb, 0), ("qkvb1", qkvb, 512),
                                  ("qkvb2", qkvb, 1024)):
                evac(name, lambda t: tok[:, t, c0:c0 + chunks[CH[name]]["n"]])
            for i in range(4):
                tcopy("qi", i, qiT[:, i, :], tb("qi", i))
            tcopy("ki", 0, kiT, tb("ki", 0))
            for i in range(8):
                tcopy("qkb", i, qkbT[:, i, :], tb("qkb", i))
            for n in range(24):
                kw = P * (n // 8 + 2)
                act.wait_ge(S("idx_mm"), n + 1)
                if n >= 2:
                    act.wait_ge(S("idx_add"), n - 1)
                act.activation(rel[n % 2][:, 0:kw], SC[n % 2][:, 0:kw], ACT.Relu, scale=0.125).then_inc(S("idx_relu"), 1)
            for i in range(2):
                evac(f"ga{i}", lambda t: y1[:, t, 512 * i:512 * i + 512], ACT.Sigmoid)
            for i in range(2):
                during(CH[f"oa{i}"])
                after(CH[f"oa{i}"])
            evac("gb0", lambda t: gb[0][:, t, :], ACT.Sigmoid)
            attention("dsa", dsa_unit, 32)
            evac("gb1", lambda t: gb[1][:, t, :], ACT.Sigmoid)
            wait_used(act, "oa1")
            for k in range(4):
                hi("ob", k, AT_hi[:, 8 + k, :], tb("ob", k))
            for i in range(2):
                during(CH[f"ob{i}"])
                after(CH[f"ob{i}"])
            wait_used(act, "gb1")
            for k in range(KD):
                hi("y", k, AT_hi[:, k, :], tb("y", k))
            for i in range(2):
                during(CH[f"out{i}"])
                after(CH[f"out{i}"])

            for t in range(NT):
                wait_read(act, "out1", t)
                sumsq(x1[:, t, :], big[:, 0:1024], ns["ffn"]["ss"][:, t:t + 1], "ffn", t)
            root("ffn", ns["ffn"])
            for k in range(KD):
                tcopy("h2", k, h2T[:, k, :], tb("h2", k), g_ffn[:, k:k + 1])
            for t in range(NT):
                act.wait_ge(norm_xs, so_far("ffn", 2, t + 1))
                act.activation(xs_hi[:, t, :], bigt[:, t, :], ACT.Copy).then_inc(S("xs_hi"), 1)
            act.wait_ge(S("rt_exp"), 1)
            act.activation(r_e, r_d, ACT.Exp).then_inc(S("rt_exp_done"), 1)
            memory_squares(0, gen_sil.rearrange("p a b -> p (a b)"))
            act.wait_ge(S("rt_exp"), 2)
            act.activation(r_e2, r_d2, ACT.Exp).then_inc(S("rt_exp_done"), 1)
            act.wait_ge(S("key_mm"), 1)
            act.activation(keyrow, ACC[2], ACT.Copy).then_inc(S("key_row"), 1)
            act.wait_ge(S("rt_comb"), 1)
            act.activation(comb_s[:, :, 0:4], comb4, ACT.Copy).then_inc(S("comb_hi"), 1)
            memory_root(0)
            def feed_in(g, j):
                p = P_MOE + j + SPL
                if isinstance(g, int):
                    return feed(g * PPG + p)
                act.wait_ge(raw_in[p % RAW], g * (96 * PPG // RAW) + 96 * (p // RAW + 1))
                act.wait_ge(piece_used, g * PPG + (P_MOE + j + 1))
                act.activation(whi[:, p % SPL, :], wraw[:, p % RAW, :], ACT.Copy).then_inc(hi_done, 1)

            def feeds(g, kind, e, qs):
                for q in qs:
                    feed_in(g, piece_of[kind, e, q])

            def gathered(g, i):
                act.wait_ge(tp_ready, g * 2 + (TPU["moe"] + i + 1))
                for k in range(4):
                    r = act.activation(xg_hi[:, 4 * i + k, :], TP[i][:, k * P:k * P + P], ACT.Copy,
                                       scale=g_ffn[:, 4 * i + k:4 * i + k + 1])
                r.then_inc(act_hi, 1)

            def silu(g, e):
                act.wait_ge(piece_used, g * PPG + (P_MOE + piece_of["gu", e, 3] + 1))
                act.wait_ge(S("hid_done"), g * EPG + (e + 1))
                act.activation(sg_sb[e % 2], ACC[e % 2][:, 0:FF], ACT.Silu).then_inc(S("silu"), 1)

            def hidden_hi(g, e):
                act.wait_ge(S("hd_t"), g * EPG + (e + 1))
                act.activation(hd_hi[e % 2], SC[e % 2][:, 0:FF], ACT.Copy).then_inc(S("hd_hi"), 1)

            def first_expert(g):
                feeds(g, "gu", 0, (0, 1, 2))
                silu(g, 0)
                feeds(g, "gu", 0, (3,))

            def group(g, last):
                for e in (1, 2, 3):
                    feeds(g, "gu", e, (0, 1))
                    hidden_hi(g, e - 1)
                    feeds(g, "gu", e, (2,))
                    silu(g, e)
                    feeds(g, "gu", e, (3,))
                    if e < 3:
                        feeds(g, "dn", e - 1, (0, 1))
                if not last:
                    gathered(g + 1, 0)
                feeds(g, "dn", 2, (0, 1))
                hidden_hi(g, 3)
                if not last:
                    gathered(g + 1, 1)
                feeds(g, "dn", 3, (0,))
                act.wait_ge(piece_used, g * PPG + (P_MOE + PPG))
                act.wait_ge(S("sc_ready"), g * 8 + 1)
                for n in range(2):
                    act.activation(y_hi[:, 512 * n:512 * n + 512], ACC[2 + n], ACT.Copy).then_inc(S("y_hi"), 1)
                feeds(g, "dn", 3, (1,))
                if not last:
                    first_expert(g + 1)

            gathered(0, 0)
            gathered(0, 1)
            first_expert(0)
            with act.Fori(0, NGRP - 1) as g:
                group(g, False)
            group(NGRP - 1, True)
            act.wait_ge(S("flag_in"), 1)
            with act.If(act.value_load(flag[0:1, 0:1], min_val=0, max_val=T) > 0):
                with act.Fori(0, NGRP * EPG) as e:
                    act.wait_ge(S("gen_gu"), e + 1)
                    act.wait_ge(S("gen_hid"), e + 1)
                    act.activation(gen_sil[:, 0, :], ACC[0], ACT.Silu)
                    act.activation(gen_sil[:, 1, :], ACC[1], ACT.Silu).then_inc(S("gen_silu"), 1)
            end_phase(act, "ACT")

            memory_hi(0)
            for t in range(NT):
                sumsq(x1[:, t, :], junkD, ns["final"]["ss"][:, t:t + 1], "final", t)
            root("final", ns["final"])
            memory_stage(0, lambda t: act.wait_ge(S("fin_x"), t + 1),
                         lambda t: xn[t], junkD,
                         lambda k: (AT_perm(AT_hi, k), tb("n2", k).rearrange("p (t q r) -> p t q r", t=NT, r=4)))
            end_phase(act, "ACT")

            act.wait_ge(S("rot_ang"), 1)
            act.activation(sin2, rot_r, ACT.Sin)
            act.activation(cos2, rot_c, ACT.Sin).then_inc(S("rot2"), 1)
            for hd in range(9):
                for i in range(12):
                    step, r = attention_step(i)
                    if hd:
                        u = dil_unit(hd - 1, r)
                        U = u["U"]
                        if step == "scores":
                            act.wait_ge(att_m, U + 1)
                            act.activation(d_s, d_s, ACT.Exp, bias=att_nm[:, U % 4:U % 4 + 1],
                                           accum_out=att_l[:, U % 4:U % 4 + 1]).then_inc(att_p, 1)
                        elif step == "output":
                            act.wait_ge(att_o, U + 1)
                            act.wait_ge(att_r, U + 1)
                            act.activation(u["o"], D_OUT, ACT.Copy, scale=att_rl[:, U % 4:U % 4 + 1]).then_inc(att_done, 1)
                    nm, q = "qkv"[i // 4], i % 4
                    if hd == 8:
                        if q == 3:
                            gate_out(0, i // 4, silu_sb)
                        feed(chunks[CH[f"gate0{THIRDS[0][i // 4]}"]]["first"] + q + SPL)
                        if i == 6:
                            gated_hi(0, 0)
                        continue
                    j = CH[f"{nm}d{hd}"]
                    n = 2 * hd + i // 4
                    if q == 3:
                        for t in range(NT):
                            wait_acc(act, j, t)
                            if nm == "v":
                                act.activation(v2[:, hd % 2, t, :], ACC[t][:, 0:384], ACT.Copy).then_inc(acc_free[t], 1)
                            else:
                                if t or n:
                                    act.wait_ge(S("qk_red"), NT * n + t)
                                act.activation(sqb, ACC[t][:, 0:384], ACT.Square).then_inc(S("qk_sq"), 1)
                    feed(chunks[j]["first"] + q + SPL)
                    if q == 3 and nm != "v":
                        act.wait_ge(S("qk_ms"), n + 1)
                        act.activation(qk_n["rt"], qk_n["ms"], ACT.Sqrt).then_inc(S("qk_rt"), 1)
                    if i in (6, 10):
                        name, dst = (f"dq_{hd}", qT) if i == 6 else (f"dk_{hd}", kT)
                        for g in range(3):
                            tcopy(name, g, dst[:, hd % 2, g, :], tb(name, g))
            end_phase(act, "ACT")
            gated_hi(0, 1)
            gated_hi(0, 2)
            memory_squares(1, mjunk)
            memory_root(1)
            during(CH["fin00"])
            after(CH["fin00"])
            for i in range(6):
                if i == 4:
                    memory_hi(1)
                feed(chunks[CH["fin01"]]["first"] + i + SPL)
            memory_stage(1, lambda t: wait_read(act, "fin01", t),
                         lambda t: res2[:, t, :], junkE,
                         lambda k: (AT_hi[:, k, :].rearrange("p (q r) -> p r q", r=4), tb("n3", k).rearrange("p (r q) -> p r q", r=4)))
            end_phase(act, "ACT")

            act.wait_ge(S("lb_in"), 1)
            act.activation(lb, lbl[:, 1, :], ACT.Sigmoid)
            act.activation(lb1, lbl[:, 1, :], ACT.Sigmoid, scale=-1.0).then_inc(S("lb_ready"), 1)
            def squares(hh):
                act.wait_ge(S("gl_od"), 4 * hh + 4)
                for t in range(NT):
                    act.activation(lsq[hh][t], mix[:, t, 512 * hh:512 * hh + 512], ACT.Square).then_inc(S("gla_sq"), 1)
                act.wait_ge(S("gla_ms"), hh + 1)
                cols = slice(16 * hh, 16 * hh + 16)
                act.activation(gl_n["rt"][:, cols], gl_n["ms"][:, cols], ACT.Sqrt).then_inc(S("gla_rt"), 1)

            for hh in range(2):
                if hh:
                    act.wait_ge(S("gl_o"), 4)
                evac(f"ql{hh}", lambda t: l_tok[:, t, :])
                for i in range(4):
                    tcopy(f"ql{hh}", i, lq[:, i, :], tb(f"ql{hh}", i))
                evac(f"fl{hh}", lambda t: l_tok[:, t, :])
                for i in range(4):
                    u = TPU[f"fl{hh}"] + i
                    act.wait_ge(tp_ready, u + 1)
                    act.activation(lf[:, i, :], TP[u % 2], ACT.Sigmoid)
                    act.activation(lk[:, i, :], TP[u % 2], ACT.Sigmoid, scale=-1.0).then_inc(tp_free[u % 2], 1)
                act.wait_ge(S("lf_in"), hh + 1)
                act.activation(lf, lf, ACT.Ln).then_inc(S("lf_done"), 1)

                def decay(n):
                    act.wait_ge(S("gl_e"), n + 1)
                    act.activation(kq[n % 5], kq[n % 5], ACT.Exp).then_inc(S("gl_x"), 1)

                for n in range(36 * hh, 36 * hh + AHEAD):
                    decay(n)
                if hh:
                    gated_hi(1, 0)
                    squares(0)
                    act.wait_ge(S("gla_red"), NT)
                evac(f"vl{hh}", lambda t: lv[:, t, :])

                def head_out(H):
                    act.wait_ge(S("gl_o"), H + 1)
                    act.activation(mix[:, :, P * H:P * H + P], TP[H % 2].rearrange("p (t c) -> p t c", t=NT),
                                   ACT.Copy).then_inc(S("gl_od"), 1)

                steps = gate_steps(hh)
                for n in range(36 * hh, 36 * hh + 36):
                    if n % 36 >= AHEAD:
                        decay(n)
                    if n % 9 == AHEAD + 1 and n % 36 > 9:
                        head_out(n // 9 - 1)
                    if hh and n % 36 == halving(steps[15][0]) + 3:
                        gate_out(1, 1, None)
                    for m, name, q, t in steps:
                        if t == NT - 1 and n % 36 == min(halving(m) + 4, 35):
                            feed(chunks[CH[name]]["first"] + q + SPL)
                if hh == 0:
                    gate_out(1, 0, None)
                else:
                    act.wait_ge(S("gl_o"), 7)
                    gate_out(1, 2, silu_b)
                head_out(4 * hh + 3)
            squares(1)
            j = CH["fin10"]
            for c in (1, 2):
                for q in (0, 1):
                    feed(chunks[j]["first"] + 2 * (c - 1) + q + SPL)
                gated_hi(1, c)
            during(j, 4)
            after(j)
            during(CH["fin11"])
            after(CH["fin11"])

        @block.vector
        def _(dve):
            chain, los = [0], [0]

            def link(ins):
                chain[0] += 1
                ins.then_inc(S("dve_step"), 1)
                dve.wait_ge(S("dve_step"), chain[0])

            def feed(p):
                if p >= NP or lo_by_pool(p):
                    return
                dve.wait_ge(hi_done, p + 1)
                dve.tensor_tensor(w_slot(wlo, p, p % SPL), w_slot(wraw, p, p % RAW), w_slot(whi, p, p % SPL).bitcast(F32),
                                  ALU.subtract).then_inc(lo_done[p % SPL], 1)

            def during(j, fed=0):
                for i in range(fed, chunks[j]["count"] - 1):
                    feed(chunks[j]["first"] + i + SPL)

            def after(j):
                feed(chunks[j]["first"] + chunks[j]["count"] - 1 + SPL)

            def flow(name):
                during(CH[name])
                after(CH[name])

            def lo(name, i, dst, src, hi, gain=None):
                u = TPU[name] + i
                los[0] += 1
                dve.wait_ge(act_hi, los[0])
                if gain is None:
                    r = dve.tensor_tensor(dst, src, hi.bitcast(F32), ALU.subtract)
                else:
                    r = dve.scalar_tensor_tensor(dst, src, gain, hi.bitcast(F32), ALU.mult, ALU.subtract)
                r.then_inc(tp_free[u % 2], 1)

            def tb(name, i):
                return TP[(TPU[name] + i) % 2]

            def mean(name, c, width):
                dve.tensor_scalar(c["ms"], c["ss"], 1.0 / width, EPS, ALU.mult, ALU.add).then_inc(norm_ms, 1)
                dve.wait_ge(norm_rt, ORDER.index(name) + 1)
                link(dve.reciprocal(c["rs"], c["rt"]))

            def row_norm(name, nt, width, rows, dst=None):
                dve.wait_ge(norm_ss, so_far(name, 1, nt))
                mean(name, ns[name], width)
                for t in range(nt):
                    dve.tensor_scalar((dst or rows)(t), rows(t), ns[name]["rs"][:, t:t + 1], None, ALU.mult
                                      ).then_inc(norm_xs, 1)

            def head_norm(name, tok, nt, gain, sq):
                c = ns[name]
                for t in range(nt):
                    dve.wait_ge(head_sq, so_far(name, 3, t + 1))
                    dve.tensor_reduce(c["ss"][:, MH * t:MH * t + MH], sq.rearrange("p (h c) -> p h c", h=MH),
                                      AX.X, ALU.add).then_inc(head_red, 1)
                dve.wait_ge(head_red, so_far(name, 3, nt))
                mean(name, c, HD)
                for t in range(nt):
                    for h in range(MH):
                        x = tok[:, t, P * h:P * h + P]
                        dve.scalar_tensor_tensor(x, x, c["rs"][:, MH * t + h:MH * t + h + 1], gain, ALU.mult, ALU.mult
                                                 ).then_inc(norm_xs, 1)

            def attention(name, unit, n):
                U0 = AU[name]

                def maxima(i):
                    u, U = unit(i), U0 + i
                    r, kw = U % 4, u["kw"]
                    nm, mx = att_nm[:, r:r + 1], att_mx[:, 3 * r:3 * r + 1]
                    dve.wait_ge(att_s, U + 1)
                    if u["mask"] is None:
                        link(dve.tensor_reduce(mx, scores_out(U, kw), AX.X, ALU.max))
                        dve.tensor_scalar(nm, mx, -u["scale"], None, ALU.mult).then_inc(att_m, 1)
                    else:
                        link(dve.tensor_tensor_reduce(u["sb"][U % len(u["sb"])][:, 0:kw], scores_out(U, kw), u["mask"], u["scale"],
                                                      LOW, ALU.add, ALU.max, mx))
                        dve.tensor_scalar(nm, mx, -1.0, None, ALU.mult).then_inc(att_m, 1)

                for i in range(LOOK):
                    maxima(i)
                for i in range(n):
                    u, U = unit(i), U0 + i
                    if i + LOOK < n:
                        maxima(i + LOOK)
                    pt = u["pt"][i % len(u["pt"])]
                    if i >= len(u["pt"]):
                        dve.wait_ge(att_o, U - len(u["pt"]) + 1)
                    tu = TPU[name] + i
                    dve.wait_ge(tp_ready, tu + 1)
                    dve.tensor_copy(pt[:, 0:u["kw"]], TP[tu % 2][:, 0:u["kw"]]).then_inc(tp_free[tu % 2], 1)
                    dve.wait_ge(att_p, U + 1)
                    dve.reciprocal(att_rl[:, U % 4:U % 4 + 1], att_l[:, U % 4:U % 4 + 1]).then_inc(att_r, 1)

            def accumulate(name, dst, fed=0):
                j = CH[name]
                during(j, fed)
                for t in range(NT):
                    wait_acc(dve, j, t)
                    d = dst(t)
                    dve.tensor_tensor(d, ACC[t][:, :], d, ALU.add).then_inc(acc_free[t], 1)
                after(j)

            def memory_norm(l):
                row_norm(f"mem{l}", 2, D, lambda t: memx[l][:, t, :])

            def memory_lo(l):
                for k in range(KD):
                    lo(f"mem{l}", k, AT_mem_lo[:, k, :], tb(f"mem{l}", k)[:, 0:MEM], AT_mem_hi[:, k, :], g_mem[l][:, k:k + 1])

            def memory_stage(l, rows, scaled, place):
                name = f"n{l + 2}"
                row_norm(name, NT, D, rows, dst=scaled)
                flow(f"mkv{l}0")
                for k in range(KD):
                    dst, src, hi = place(k)
                    lo(name, k, dst, src, hi, g_n2[l][:, k:k + 1])
                head_norm(f"km{l}", km_tok, 2, mg[l][:, P:2 * P], msq)
                flow(f"qm{l}")
                head_norm(f"qm{l}", qm_tok, NT, mg[l][:, 0:P], msq)
                flow(f"mkv{l}1")
                attention(f"mat{l}", mem_unit, 16)

            def gate(l, c, tmp):
                i = THIRDS[l][c]
                if l == 0 and i == 1:
                    dve.wait_ge(att_done, AU["dil"] + 32)
                for t in range(NT):
                    m = mix[:, t, 512 * i:512 * i + 512]
                    if l == 1 and c < 2:
                        dve.wait_ge(S("silu_in"), NT * c + t + 1)
                        dve.tensor_tensor(m, m, ACC[t], ALU.mult).then_inc(acc_free[t], 1)
                        continue
                    wait_read(dve, f"gate{l}{i}", t)
                    dve.tensor_tensor(m, m, tmp[(NT * c + t) % len(tmp)], ALU.mult).then_inc(S(f"gated{l}"), 1)

            def gated_lo(l, c):
                for k in range(4):
                    r = (8 + 4 * c + k) % 12
                    lo(f"y{l}{c}", k, AT_lo[:, r, :], tb(f"y{l}{c}", k), AT_hi[:, r, :])

            dve.sem_inc(S("hid_done"), 2)
            dve.sem_inc(S("y_done"), 2)
            dve.sem_inc(S("sc_ready"), 1)
            dve.sem_inc(S("sc_free"), 2)
            dve.sem_inc(S("gen_y"), 8)
            dve.sem_inc(S("gen_hid"), 1)
            dve.sem_inc(S("gen_add"), 2)
            row_norm("n1", NT, D, lambda t: xr[:, t, :])
            for p in range(SPL):
                feed(p)
            dve.wait_ge(S("gains_in"), 128)
            dve.wait_ge(S("consts"), 16)
            for k in range(KD):
                lo("n1", k, AT_lo[:, k, :], tb("n1", k), AT_hi[:, k, :], g_mix[:, k:k + 1])
            flow("cqkv0")
            flow("cqkv1")
            row_norm("cq", NT, 384, lambda t: cqkv[:, t, 0:384])
            row_norm("ckv", NT, 256, lambda t: cqkv[:, t, 384:640])
            for k in range(3):
                lo("cq", k, AT_lo[:, 8 + k, :], tb("cq", k), AT_hi[:, 8 + k, :], g_cq[:, k:k + 1])
            flow("uq0")
            flow("uq1")
            for k in range(2):
                lo("ckv", k, AT_lo[:, 8 + k, :], tb("ckv", k), AT_hi[:, 8 + k, :], g_ckv[:, k:k + 1])
            flow("uv")
            dve.wait_ge(S("kr_rot"), 1)
            wait_tp_read(dve, "qa", 8)
            for t in range(NT):
                dve.tensor_copy(qk_tok[:, t, :, 64:96], cqkv[:, t, 640:672].unsqueeze(1).broadcast_to([P, H8, 32])
                                ).then_inc(S("ka_rot"), 1)
            flow("uk")
            attention("mla", mla_unit, 32)
            for k in range(4):
                lo("oa", k, AT_lo[:, 8 + k, :], tb("oa", k), AT_hi[:, 8 + k, :])
            end_phase(dve, "DVE")

            for name in ("idx0", "idx1", "qkvb0", "qkvb1", "qkvb2"):
                flow(name)
            dve.wait_ge(S("b_rot"), 2)
            dve.wait_ge(tp_ready, TPU["ki"] + 1)
            for n in range(24):
                qt, h = 1 + n // 8, n % 8
                kw = P * (qt + 1)
                sc, w = score[:, qt - 1, 0:kw], wi_s[:, qt, h:h + 1]
                dve.wait_ge(S("idx_relu"), n + 1)
                if h == 0:
                    dve.tensor_scalar(sc, rel[n % 2][:, 0:kw], w, None, ALU.mult).then_inc(S("idx_add"), 1)
                else:
                    dve.wait_ge(S("idx_add"), n)
                    dve.scalar_tensor_tensor(sc, rel[n % 2][:, 0:kw], w, sc, ALU.mult, ALU.add).then_inc(S("idx_add"), 1)
                if h == 7:
                    dve.wait_ge(S("idx_add"), n + 1)
                    link(dve.tensor_tensor(sc[:, kw - P:kw], sc[:, kw - P:kw], cmask[:, 384:512], ALU.add))
            ROUNDS = TOPK // 8

            def top_rounds(first, count):
                for n in range(first, first + count):
                    qt, r = 1 + n // ROUNDS, n % ROUNDS
                    kw = P * (qt + 1)
                    sc, left = score[:, qt - 1, 0:kw], tk[:, 0:kw]
                    src = left if r else sc
                    link(dve.max(max8, src))
                    link(dve.match_replace(left, max8, src, GONE))
                    if r == ROUNDS - 1:
                        link(dve.tensor_tensor(sc, left, sc, ALU.is_equal))
                        link(dve.tensor_scalar(sc, sc, NEG, None, ALU.mult))

            done = 0
            some = -(-(NT - 1) * ROUNDS // sum(chunks[CH[name]]["count"] for name in ("ga0", "ga1", "oa0", "oa1", "gb0")))
            for name in ("ga0", "ga1", "oa0", "oa1", "gb0"):
                j = CH[name]
                for q in range(chunks[j]["count"]):
                    if name[0] == "o" and q == chunks[j]["count"] - 1:
                        for t in range(NT):
                            wait_acc(dve, j, t)
                            wait_read(dve, "g" + name[1:], t)
                            y = y1[:, t, 512 * int(name[2]):512 * int(name[2]) + 512]
                            dve.tensor_tensor(y, ACC[t][:, :], y, ALU.mult).then_inc(acc_free[t], 1)
                    feed(chunks[j]["first"] + q + SPL)
                    more = min(some, (NT - 1) * ROUNDS - done)
                    top_rounds(done, more)
                    done += more
            attention("dsa", dsa_unit, 32)
            flow("gb1")
            for k in range(4):
                lo("ob", k, AT_lo[:, 8 + k, :], tb("ob", k), AT_hi[:, 8 + k, :])
            for i in range(2):
                j = CH[f"ob{i}"]
                during(j)
                for t in range(NT):
                    wait_acc(dve, j, t)
                    wait_read(dve, f"gb{i}", t)
                    b = gb[i][:, t, :]
                    dve.tensor_tensor(b, ACC[t][:, :], b, ALU.mult).then_inc(acc_free[t], 1)
                for t in range(NT):
                    y = y1[:, t, 512 * i:512 * i + 512]
                    wait_read(dve, f"ob{i}", t)
                    dve.tensor_tensor(y, y, gb[i][:, t, :], ALU.add).then_inc(S("y_sum"), 1)
                after(j)
            for k in range(KD):
                lo("y", k, AT_lo[:, k, :], tb("y", k), AT_hi[:, k, :])
            dve.wait_ge(S("res1"), 16)
            for i in range(2):
                accumulate(f"out{i}", lambda t: x1[:, t, 512 * i:512 * i + 512])

            row_norm("ffn", NT, D, lambda t: x1[:, t, :], dst=lambda t: bigt[:, t, :])
            spread = lambda a, n: a.unsqueeze(2).broadcast_to([P, NT, n])
            rows = lambda a, n: a.unsqueeze(1).broadcast_to([P, NT, n])
            dve.wait_ge(S("moe_in"), 96)
            dve.wait_ge(S("rt_mm"), 1)
            link(dve.tensor_tensor(lg, ACC[0][:, 0:NT * 40].rearrange("p (t c) -> p t c", t=NT), rows(b_rt, 40), ALU.add))
            glg = lg[:, :, 0:8]
            link(dve.tensor_reduce(r_gmax, glg, AX.X, ALU.max))
            dve.tensor_tensor(r_d, glg, spread(r_gmax, 8), ALU.subtract).then_inc(S("rt_exp"), 1)
            link(dve.tensor_tensor(r_eq, glg, spread(r_gmax, 8), ALU.is_equal))
            link(dve.scalar_tensor_tensor(r_cand, r_eq, -8.0, rows(iota_g, 8), ALU.mult, ALU.add))
            link(dve.tensor_reduce(r_gi, r_cand, AX.X, ALU.min))
            dve.tensor_tensor(oneh, r_cand, spread(r_gi, 8), ALU.is_equal).then_inc(S("rt_oneh"), 1)
            dve.wait_ge(S("rt_oneh"), 1)
            link(dve.tensor_tensor(r_el, lg[:, :, 8:40].rearrange("p t (g e) -> p t g e", g=8),
                                   oneh.unsqueeze(3).broadcast_to([P, NT, 8, EPG]), ALU.mult))
            link(dve.tensor_reduce(r_in4, r_el.rearrange("p t g e -> p t e g"), AX.X, ALU.add))
            src = r_in4
            for m, oh in ((r_m1, r_oh1), (r_m2, r_oh2)):
                link(dve.tensor_reduce(m, src, AX.X, ALU.max))
                link(dve.tensor_tensor(r_eq4, src, spread(m, EPG), ALU.is_equal))
                link(dve.scalar_tensor_tensor(r_cand4, r_eq4, -8.0, rows(iota_g[:, 0:EPG], EPG), ALU.mult, ALU.add))
                link(dve.tensor_reduce(r_min4, r_cand4, AX.X, ALU.min))
                link(dve.tensor_tensor(oh, r_cand4, spread(r_min4, EPG), ALU.is_equal))
                if m is r_m1:
                    link(dve.scalar_tensor_tensor(r_in4b, r_oh1, LOW, r_in4, ALU.mult, ALU.add))
                    src = r_in4b
            dve.tensor_tensor(r_d2, r_m2, r_m1, ALU.subtract).then_inc(S("rt_exp"), 1)
            dve.wait_ge(S("rank_mm"), 1)
            link(dve.tensor_tensor(r_eq, ACC[1][:, 0:NT * 8].rearrange("p (t c) -> p t c", t=NT), oneh, ALU.mult))
            link(dve.tensor_reduce(r_rank, r_eq, AX.X, ALU.add))
            dve.tensor_scalar(r_over, r_rank, float(CAP), None, ALU.is_ge).then_inc(S("rt_over"), 1)
            link(dve.scalar_tensor_tensor(key, r_gi, float(P), r_rank, ALU.mult, ALU.add))
            link(dve.tensor_scalar(key, key, float(8 * P), None, ALU.add))
            link(dve.scalar_tensor_tensor(key, r_over, 1e6, key, ALU.mult, ALU.add))
            dve.tensor_copy(keyb, spread(key, P)).then_inc(S("key_b"), 1)
            dve.wait_ge(S("rt_exp_done"), 2)
            link(dve.tensor_reduce(r_sum, r_e, AX.X, ALU.add))
            link(dve.tensor_scalar(r_w1, r_e2, 1.0, None, ALU.add))
            link(dve.tensor_tensor(r_w1, r_w1, r_sum, ALU.mult))
            link(dve.reciprocal(r_w1, r_w1))
            link(dve.tensor_tensor(r_w2, r_w1, r_e2, ALU.mult))
            dve.tensor_tensor(r_oh1, r_oh1, spread(r_w1, EPG), ALU.mult)
            link(dve.tensor_tensor(r_oh2, r_oh2, spread(r_w2, EPG), ALU.mult))
            dve.tensor_tensor(comb4, r_oh1, r_oh2, ALU.add).then_inc(S("rt_comb"), 1)
            dve.wait_ge(S("comb_hi"), 1)
            dve.tensor_tensor(comb_s[:, :, 4:8], comb4, comb_s[:, :, 0:4].bitcast(F32), ALU.subtract).then_inc(S("comb_lo"), 1)
            dve.wait_ge(S("rt_over"), 1)
            link(dve.tensor_tensor(r_eq4, comb4, spread(r_over, EPG), ALU.mult))
            link(dve.tensor_tensor(comb32.rearrange("p t (g e) -> p t g e", g=NGRP), oneh.unsqueeze(3).broadcast_to([P, NT, 8, EPG]),
                                   r_eq4.unsqueeze(2).broadcast_to([P, NT, 8, EPG]), ALU.mult))
            dve.wait_ge(S("over_mm"), 1)
            link(dve.tensor_reduce(r_sum[0:1, 0:1], ACC[1][0:1, 64:64 + NT], AX.X, ALU.add))
            dve.tensor_copy(flag[0:1, 0:1], r_sum[0:1, 0:1]).then_inc(S("flag_in"), 1)
            dve.wait_ge(S("flag_in"), 1)
            dve.wait_ge(S("key_row"), 1)
            def feed_in(g, j):
                p = P_MOE + j + SPL
                if isinstance(g, int):
                    return feed(g * PPG + p)
                if p % 8 in POOL_OF_8:
                    return
                dve.wait_ge(hi_done, g * PPG + (p + 1))
                dve.tensor_tensor(wlo[:, p % SPL, :], wraw[:, p % RAW, :], whi[:, p % SPL, :].bitcast(F32),
                                  ALU.subtract).then_inc(lo_done[p % SPL], 1)

            def feeds(g, kind, e, qs):
                for q in qs:
                    feed_in(g, piece_of[kind, e, q])

            def picks():
                for t in range(NT):
                    r = dve.tensor_scalar(pick[:, t, :], iota_s, key[:, t:t + 1], None, ALU.is_equal)
                r.then_inc(S("pick"), 1)

            def puts():
                dve.tensor_scalar(put, keyrow, iota_p[:, 0:1], None, ALU.is_equal).then_inc(S("put"), 1)

            def gathered(g, i):
                dve.wait_ge(act_hi, g * 2 + (los[0] + i + 1))
                for k in range(4):
                    r = dve.scalar_tensor_tensor(xg_lo[:, 4 * i + k, :], TP[i][:, k * P:k * P + P], g_ffn[:, 4 * i + k:4 * i + k + 1],
                                                 xg_hi[:, 4 * i + k, :].bitcast(F32), ALU.mult, ALU.subtract)
                r.then_inc(tp_free[i], 1)

            def slot_weights(g):
                dve.wait_ge(S("ws_mm"), g + 1)
                dve.tensor_reduce(wslot, ACC[1][:, 0:2 * EPG].rearrange("p (h e) -> p e h", h=2), AX.X, ALU.add
                                  ).then_inc(S("ws_read"), 1)

            def hidden(g, e):
                dve.wait_ge(S("ws_read"), g + 1)
                dve.wait_ge(S("silu"), g * EPG + (e + 1))
                dve.scalar_tensor_tensor(hid_sb[e % 2], ACC[e % 2][:, FF:2 * FF], wslot[:, e:e + 1], sg_sb[e % 2],
                                         ALU.mult, ALU.mult).then_inc(S("hid_done"), 1)

            def hidden_lo(g, e):
                dve.wait_ge(S("hd_hi"), g * EPG + (e + 1))
                dve.tensor_tensor(hd_lo[e % 2], SC[e % 2][:, 0:FF], hd_hi[e % 2].bitcast(F32), ALU.subtract
                                  ).then_inc(S("hd_split"), 1)

            def spread_sums(g, tiles):
                for i in tiles:
                    x = x1[:, i // 2, 512 * (i % 2):512 * (i % 2) + 512]
                    dve.wait_ge(S("sc_ready"), g * 8 + (i + 2))
                    dve.tensor_tensor(x, SC[i % 2], x, ALU.add).then_inc(S("sc_free"), 1)

            def group(g, last):
                if not last:
                    dve.wait_ge(S("pick"), g + 1)
                    dve.tensor_scalar(key, key, float(-P), None, ALU.add).then_inc(S("key_next"), 1)
                    dve.wait_ge(S("ws_mm"), g + 1)
                    dve.wait_ge(S("key_next"), g + 1)
                    picks()
                for e in (1, 2, 3):
                    feeds(g, "gu", e, (0, 1))
                    hidden_lo(g, e - 1)
                    feeds(g, "gu", e, (2,))
                    hidden(g, e)
                    feeds(g, "gu", e, (3,))
                    if e < 3:
                        feeds(g, "dn", e - 1, (0, 1))
                if not last:
                    gathered(g + 1, 0)
                feeds(g, "dn", 2, (0, 1))
                hidden_lo(g, 3)
                if not last:
                    gathered(g + 1, 1)
                    slot_weights(g + 1)
                feeds(g, "dn", 3, (0,))
                for n in range(2):
                    dve.wait_ge(S("y_hi"), g * 2 + (n + 1))
                    dve.tensor_tensor(y_lo[:, 512 * n:512 * n + 512], ACC[2 + n], y_hi[:, 512 * n:512 * n + 512].bitcast(F32),
                                      ALU.subtract).then_inc(S("y_done"), 1)
                feeds(g, "dn", 3, (1,))
                if last:
                    spread_sums(g, range(8))
                    return
                feeds(g + 1, "gu", 0, (0, 1))
                spread_sums(g, (0, 1))
                feeds(g + 1, "gu", 0, (2,))
                spread_sums(g, (2, 3))
                hidden(g + 1, 0)
                feeds(g + 1, "gu", 0, (3,))
                spread_sums(g, (4, 5, 6, 7))
                dve.wait_ge(S("put"), g + 1)
                dve.tensor_scalar(keyrow, keyrow, float(-P), None, ALU.add).then_inc(S("row_next"), 1)
                dve.wait_ge(S("row_next"), g + 1)
                puts()
                dve.wait_ge(S("sc_free"), g * 8 + (8 + 2))

            picks()
            puts()
            memory_norm(0)
            gathered(0, 0)
            gathered(0, 1)
            slot_weights(0)
            feeds(0, "gu", 0, (0, 1, 2))
            hidden(0, 0)
            feeds(0, "gu", 0, (3,))
            with dve.Fori(0, NGRP - 1) as g:
                group(g, False)
            group(NGRP - 1, True)
            dve.wait_ge(S("sc_free"), 8 * NGRP + 2)
            los[0] += 2 * NGRP
            with dve.If(dve.value_load(flag[0:1, 0:1], min_val=0, max_val=T) > 0):
                with dve.Fori(0, NGRP * EPG) as e:
                    dve.wait_ge(S("gen_silu"), e + 1)
                    dve.tensor_tensor(gen_hid[:, 0, :], ACC[2], gen_sil[:, 0, :], ALU.mult)
                    dve.tensor_tensor(gen_hid[:, 1, :], ACC[3], gen_sil[:, 1, :], ALU.mult).then_inc(S("gen_hid"), 1)
                    for i in range(2 * NT):
                        t, n = i // 2, i % 2
                        x = x1[:, t, 512 * n:512 * n + 512]
                        dve.wait_ge(S("gen_y"), e * 8 + (8 + i + 1))
                        dve.scalar_tensor_tensor(x, SC[i % 2], comb32[:, t, bass.ds(e, 1)], x, ALU.mult, ALU.add
                                                 ).then_inc(S("gen_add"), 1)
                    dve.wait_ge(S("gen_add"), e * 8 + (8 + 2))
            end_phase(dve, "DVE")

            memory_lo(0)
            c = ns["final"]
            dve.wait_ge(norm_ss, so_far("final", 1, NT))
            mean("final", c, D)
            for t in range(NT):
                dve.scalar_tensor_tensor(xn[t], x1[:, t, :], c["rs"][:, t:t + 1], fin_g, ALU.mult, ALU.mult
                                         ).then_inc(S("fin_x"), 1)
            memory_stage(0, lambda t: xn[t], lambda t: x1[:, t, :],
                         lambda k: (AT_perm(AT_lo, k), tb("n2", k).rearrange("p (t q r) -> p t q r", t=NT, r=4), AT_perm(AT_hi, k)))
            end_phase(dve, "DVE")

            dve.wait_ge(S("dil_in"), 64)
            ROUND, C1, C2 = 1.5 * 2 ** 23, 6.28125, 0.0019350051879882812
            C3 = 2 * np.pi - C1 - C2
            link(dve.tensor_copy(rot_p, posi[:, :]))
            link(dve.tensor_tensor(rot_a, rot_p.unsqueeze(2).broadcast_to([P, NT, 16]), inv2.unsqueeze(1).broadcast_to([P, NT, 16]),
                                   ALU.mult))
            link(dve.tensor_scalar(rot_k, rot_a, 1 / (2 * np.pi), ROUND, ALU.mult, ALU.add))
            link(dve.tensor_scalar(rot_k, rot_k, ROUND, None, ALU.subtract))
            for cc in (C1, C2, C3):
                link(dve.scalar_tensor_tensor(rot_a, rot_k, -float(cc), rot_a, ALU.mult, ALU.add))
            link(dve.tensor_scalar(rot_r, rot_a, 3.1415925, -3.1415925, ALU.min, ALU.max))
            link(dve.scalar_tensor_tensor(rot_c, rot_r, -1.0, rot_r, ALU.mult, ALU.min))
            dve.tensor_scalar(rot_c, rot_c, float(np.pi / 2), None, ALU.add).then_inc(S("rot_ang"), 1)
            for hd in range(9):
                for i in range(12):
                    step, r = attention_step(i)
                    if hd:
                        u = dil_unit(hd - 1, r)
                        U = u["U"]
                        c = U % 4
                        nm, mx = att_nm[:, c:c + 1], att_mx[:, 3 * c:3 * c + 3]
                        if step == "scores":
                            dve.wait_ge(att_s, U + 1)
                            at = 0
                            for g, (src, _, keys, mask, scale) in enumerate(u["s"]):
                                w = keys.shape[1]
                                ins = dve.tensor_tensor_reduce(d_s[:, at:at + w], src[:, 0:w], mask, scale, LOW,
                                                               ALU.add, ALU.max, mx[:, g:g + 1])
                                at += w
                            link(ins)
                            link(dve.tensor_reduce(nm, mx, AX.X, ALU.max))
                            dve.tensor_scalar(nm, nm, -1.0, None, ALU.mult).then_inc(att_m, 1)
                        elif step == "probs":
                            if U > AU["dil"]:
                                dve.wait_ge(att_o, U)
                            for k, w in ((0, 4 * P), (1, 2 * P)):
                                tu = TPU[f"da{r}_{hd - 1}"] + k
                                dve.wait_ge(tp_ready, tu + 1)
                                dve.tensor_copy(d_pt[:, 512 * k:512 * k + w], TP[tu % 2][:, 0:w]).then_inc(tp_free[tu % 2], 1)
                            dve.wait_ge(att_p, U + 1)
                            dve.reciprocal(att_rl[:, c:c + 1], att_l[:, c:c + 1]).then_inc(att_r, 1)
                    nm, q = "qkv"[i // 4], i % 4
                    if hd == 8:
                        if q == 3:
                            gate(0, i // 4, silu_sb)
                        feed(chunks[CH[f"gate0{THIRDS[0][i // 4]}"]]["first"] + q + SPL)
                        if i == 6:
                            gated_lo(0, 0)
                        continue
                    j = CH[f"{nm}d{hd}"]
                    n = 2 * hd + i // 4
                    if q == 3 and nm != "v":
                        if n:
                            dve.wait_ge(tp_ready, TPU[f"dq_{hd}" if nm == "k" else f"dk_{hd - 1}"] + 3)
                        for t in range(NT):
                            dve.wait_ge(S("qk_sq"), NT * n + t + 1)
                            dve.tensor_reduce(qk_n["ss"][:, 3 * t:3 * t + 3], sqb.rearrange("p (g c) -> p g c", g=3), AX.X, ALU.add
                                              ).then_inc(S("qk_red"), 1)
                            dve.tensor_tensor(qk_t[:, t, :].rearrange("p (g c) -> p g c", g=3),
                                              ACC[t][:, 0:384].rearrange("p (g c) -> p g c", g=3), qkg[:, :, i // 4, :], ALU.mult
                                              ).then_inc(acc_free[t], 1)
                    feed(chunks[j]["first"] + q + SPL)
                    if q == 3 and nm != "v":
                        dve.wait_ge(S("qk_red"), NT * n + NT)
                        dve.tensor_scalar(qk_n["ms"], qk_n["ss"], 1.0 / HD, EPS, ALU.mult, ALU.add).then_inc(S("qk_ms"), 1)
                        dve.wait_ge(S("qk_rt"), n + 1)
                        rt_ = qk_n["rt"].rearrange("p (t g) -> p t g", t=NT)
                        if nm == "q":
                            rs = q_rs[hd % 2]
                            link(dve.reciprocal(rs, rt_))
                            dve.tensor_scalar(rs, rs, HD ** -0.5, None, ALU.mult).then_inc(S("qk_rs"), 1)
                        else:
                            dve.reciprocal(k_rs, rt_).then_inc(S("qk_rs"), 1)
            end_phase(dve, "DVE")
            gated_lo(0, 1)
            gated_lo(0, 2)
            memory_norm(1)
            dve.wait_ge(S("res2"), 64)
            accumulate("fin00", lambda t: res2[:, t, 0:512])
            for i in range(4):
                feed(chunks[CH["fin01"]]["first"] + i + SPL)
            memory_lo(1)
            accumulate("fin01", lambda t: res2[:, t, 512:1024], 4)
            by_token = lambda a, k: a[:, k, :].rearrange("p (q r) -> p r q", r=4)
            memory_stage(1, lambda t: res2[:, t, :], lambda t: n3x[:, t, :],
                         lambda k: (by_token(AT_lo, k), tb("n3", k).rearrange("p (r q) -> p r q", r=4), by_token(AT_hi, k)))
            end_phase(dve, "DVE")

            dve.wait_ge(S("gla_in"), 64)
            dve.tensor_tensor(lbl[:, 1, :], lbl[:, 1, :], lbl[:, 0, :], ALU.subtract).then_inc(S("lb_in"), 1)
            dve.wait_ge(S("lb_ready"), 1)
            diag = view(at_ltok, 2560, NT, 640)[:, :, 0:P]
            four = lambda a: a.rearrange("p (t c) -> p t c", t=NT)
            def heads_norm(hh):
                cols = slice(16 * hh, 16 * hh + 16)
                ss, rs = gl_n["ss"][:, cols], gl_n["rs"][:, cols]
                for t in range(NT):
                    dve.wait_ge(S("gla_sq"), NT * hh + t + 1)
                    dve.tensor_reduce(ss[:, 4 * t:4 * t + 4], lsq[hh][t].rearrange("p (h c) -> p h c", h=4), AX.X, ALU.add
                                      ).then_inc(S("gla_red"), 1)
                dve.wait_ge(S("gla_red"), NT * hh + NT)
                dve.tensor_scalar(gl_n["ms"][:, cols], ss, 1.0 / HD, EPS, ALU.mult, ALU.add).then_inc(S("gla_ms"), 1)
                dve.wait_ge(S("gla_rt"), hh + 1)
                link(dve.reciprocal(rs, gl_n["rt"][:, cols]))
                for t in range(NT):
                    for h in range(4):
                        m = mix[:, t, 512 * hh + P * h:512 * hh + P * h + P]
                        r = dve.scalar_tensor_tensor(m, m, rs[:, 4 * t + h:4 * t + h + 1], og, ALU.mult, ALU.mult)
                link(r)

            for hh in range(2):
                if hh:
                    gate(1, 0, None)
                flow(f"ql{hh}")
                flow(f"fl{hh}")
                wait_tp_read(dve, f"fl{hh}", 4)
                for i in range(4):
                    H = 4 * hh + i
                    dve.tensor_scalar(lf[:, i, :], lf[:, i, :], lb1[:, H:H + 1], lb[:, H:H + 1], ALU.mult, ALU.add)
                    r = dve.tensor_scalar(lk[:, i, :], lk[:, i, :], lb1[:, H:H + 1], None, ALU.mult)
                r.then_inc(S("lf_in"), 1)
                dve.wait_ge(S("lf_done"), hh + 1)
                dve.wait_ge(S("lf_in"), hh + 1)
                dve.wait_ge(S("lA_zero"), hh + 1)

                def decays(H):
                    if H >= 2:
                        dve.wait_ge(S("gl_e"), 9 * (H - 1))
                    dve.tensor_tensor_scan(G64[H % 2], seg, lf[:, H % 4, :], 0.0, ALU.mult, ALU.add)
                    link(dve.tensor_tensor_scan(G512[H % 2], ones[:, 0:1].broadcast_to([P, T]), lf[:, H % 4, :], 0.0,
                                                ALU.mult, ALU.add))

                def exponents(n):
                    H, half = n // 9, 1 << n % 9
                    if n % 9 == 0:
                        decays(H)
                    if n >= 5:
                        dve.wait_ge(S("gl_mm"), n - 5 + (n - 5) // 9 + 2)
                    first, second = halves((G64 if half <= 64 else G512)[H % 2], half)
                    d1, d2 = halves(kq[n % 5], half)
                    ref = first[:, :, half - 1:half].broadcast_to([P, T // (2 * half), half])
                    dve.tensor_tensor(d1, ref, first, ALU.subtract)
                    if half == 64:
                        r = dve.tensor_copy(d2, second)
                    else:
                        r = dve.tensor_tensor(d2, second, ref, ALU.subtract)
                    r.then_inc(S("gl_e"), 1)

                def queries(n):
                    half = 1 << n % 9
                    e2, q2 = halves(kq[n % 5], half)[1], halves(lq[:, n // 9 % 4, :], half)[1]
                    dve.wait_ge(S("gl_x"), n + 1)
                    dve.tensor_tensor(e2, q2, e2, ALU.mult).then_inc(S("gl_q"), 1)

                def collect(m):
                    i = m % 10
                    dve.wait_ge(S("gl_mm"), m + 1)
                    src = four(SC[m % 2])
                    if m:
                        dve.wait_ge(S("gl_c"), m)
                    if i == 0:
                        mask = lmask[:, 7, :].bitcast(I32).unsqueeze(1).broadcast_to([P, NT, P])
                        dve.copy_predicated(diag, mask, src).then_inc(S("gl_c"), 1)
                    elif i <= 7:
                        half = 1 << i - 1
                        mask = halves(lmask[:, i - 1, :], half)[1].bitcast(I32).unsqueeze(1).broadcast_to([P, NT, 64 // half, half])
                        dve.copy_predicated(diag.rearrange("p t (n s c) -> p t n s c", s=2, c=half)[:, :, :, 1, :], mask,
                                            SC[m % 2][:, 0:256].rearrange("p (t n c) -> p t n c", t=NT, c=half)
                                            ).then_inc(S("gl_c"), 1)
                    elif i == 8:
                        dve.tensor_copy(lA[:, 0, P:2 * P], src[:, 1, :])
                        dve.tensor_copy(lA[:, 2, 3 * P:4 * P], src[:, 3, :]).then_inc(S("gl_c"), 1)
                    else:
                        dve.tensor_copy(lA[:, 0:2, 2 * P:4 * P], SC[m % 2].rearrange("p (s t) -> p s t", s=2)
                                        ).then_inc(S("gl_c"), 1)

                first, end = 36 * hh, 36 * hh + 36
                for n in range(first, first + AHEAD):
                    exponents(n)
                queries(first)
                if hh:
                    gated_lo(1, 0)
                    heads_norm(0)
                flow(f"vl{hh}")
                for n in range(first, end):
                    if n + AHEAD < end:
                        exponents(n + AHEAD)
                    if n + 1 < end:
                        queries(n + 1)
                    H = n // 9
                    if n % 9 == 0:
                        if H:
                            dve.wait_ge(S("gl_o"), H)
                        collect(10 * H)
                    collect(10 * H + n % 9 + 1)
                    steps = gate_steps(hh)
                    if hh and n % 36 == halving(steps[15][0]) + 3:
                        gate(1, 1, None)
                    for m, name, q, t in steps:
                        if t == NT - 1 and n % 36 == min(halving(m) + 4, 35):
                            feed(chunks[CH[name]]["first"] + q + SPL)
            heads_norm(1)
            gate(1, 2, silu_b)
            j = CH["fin10"]
            for c in (1, 2):
                for q in (0, 1):
                    feed(chunks[j]["first"] + 2 * (c - 1) + q + SPL)
                gated_lo(1, c)
            dve.wait_ge(S("res3"), 16)
            accumulate("fin10", lambda t: res3[:, t, 0:512], 4)
            accumulate("fin11", lambda t: res3[:, t, 512:1024])

        @block.tensor
        def _(pe):
            PASSES = lambda ah, al, bh, bl: ((ah, bh), (ah, bl), (al, bh))

            def project_piece(name, i):
                for t in range(chunks[CH[name]]["nt"]):
                    project_tile(name, i, t)

            def project_tile(name, i, t):
                j = CH[name]
                c = chunks[j]
                n, per, nt = c["n"], c["per"], c["nt"]
                p = c["first"] + i
                if t == 0:
                    pe.wait_ge(lo_done[p % SPL], p // SPL + 1)
                if i == 0 and bank_uses[j][t]:
                    pe.wait_ge(acc_free[t], bank_uses[j][t])
                for kk in range(per):
                    kc = i * per + kk
                    cols = slice(t * P, t * P + P)
                    ah, al = ((AT_mem_hi[:, kc, cols], AT_mem_lo[:, kc, cols]) if c["mem"] else
                              (AT_hi[:, (c["at"] + kc) % 12, cols], AT_lo[:, (c["at"] + kc) % 12, cols]))
                    bh, bl = (w[:, p % SPL, kk * n:kk * n + n] for w in (whi, wlo))
                    for q, (a, b) in enumerate(PASSES(ah, al, bh, bl)):
                        mm = pe.matmul(ACC[t][:, 0:n], a, b, start=kc == 0 and q == 0,
                                       stop=i == c["count"] - 1 and kk == per - 1 and q == 2)
                if t == nt - 1:
                    mm.then_inc(piece_used, 1)
                elif i == c["count"] - 1:
                    mm.then_inc(acc_ready, 1)

            def project(name, operand=None):
                c = chunks[CH[name]]
                if isinstance(operand, str):
                    operand = range(TPU[operand], TPU[operand] + c["count"] * c["per"])
                for i in range(c["count"]):
                    if operand is not None:
                        for u in operand[i * c["per"]:(i + 1) * c["per"]]:
                            pe.wait_ge(tp_free[u % 2], u // 2 + 1)
                    project_piece(name, i)

            def transposes(name, i, blocks):
                u = TPU[name] + i
                if u >= 2:
                    pe.wait_ge(tp_free[u % 2], u // 2)
                at = 0
                for b in blocks:
                    tr = pe.transpose(TP[u % 2][0:b.shape[1], at:at + P], b, ident)
                    at += P
                tr.then_inc(tp_ready, 1)

            def rows_t(name, n, rows, nt=NT):
                for k in range(n):
                    if k == 0:
                        pe.wait_ge(norm_xs, so_far(name, 2, nt))
                    transposes(name, k, [rows(t)[:, P * k:P * k + P] for t in range(nt)])

            def attention(name, unit, n):
                U0 = AU[name]

                def scores(i):
                    u, U = unit(i), U0 + i
                    pe.matmul(scores_out(U, u["kw"]), u["q"], u["k"], start=True, stop=True).then_inc(att_s, 1)

                def probs_t(i):
                    u, U = unit(i), U0 + i
                    pe.wait_ge(att_p, U + 1)
                    s = u["sb"][U % len(u["sb"])]
                    transposes(name, i, [s[:, P * b:P * b + P] for b in range(u["kw"] // P)])

                def output(i):
                    u, U = unit(i), U0 + i
                    tu = TPU[name] + i
                    pe.wait_ge(tp_free[tu % 2], tu // 2 + 1)
                    if U >= 2:
                        pe.wait_ge(att_done, U - 1)
                    pt, nb = u["pt"][i % len(u["pt"])], u["kw"] // P
                    for b in range(nb):
                        mm = pe.matmul(SC[U % 2][:, 0:u["dv"]], pt[:, P * b:P * b + P], u["v"][b], start=b == 0, stop=b == nb - 1)
                    mm.then_inc(att_o, 1)

                for i in range(LOOK):
                    scores(i)
                for i in range(n + 1):
                    if i + LOOK < n:
                        scores(i + LOOK)
                    if i < n:
                        probs_t(i)
                    if i:
                        output(i - 1)

            def read_all(name):
                for t in range(chunks[CH[name]]["nt"]):
                    wait_read(pe, name, t)

            def memory_t(l):
                rows_t(f"mem{l}", KD, lambda t: memx[l][:, t, :], nt=2)

            def memory_stage(l, rows):
                project(f"mkv{l}0", f"mem{l}")
                rows_t(f"n{l + 2}", KD, rows)
                project(f"qm{l}", f"n{l + 2}")
                for name, tok, nt in ((f"km{l}", km_tok, 2), (f"qm{l}", qm_tok, NT)):
                    if tok is qm_tok:
                        project(f"mkv{l}1")
                    pe.wait_ge(norm_xs, so_far(name, 2, MH * nt))
                    for h in range(MH):
                        transposes(name, h, [tok[:, t, P * h:P * h + P] for t in range(nt)])
                wait_tp_read(pe, f"km{l}", MH)
                wait_tp_read(pe, f"qm{l}", MH)
                read_all(f"mkv{l}1")
                read_all(f"qm{l}")
                attention(f"mat{l}", mem_unit, 16)

            def gated_t(l, c):
                if l == 1 and c < 2:
                    read_all(f"gate1{THIRDS[1][c]}")
                else:
                    pe.wait_ge(S(f"gated{l}"), NT * (c if l == 0 else 0) + NT)
                for k in range(4):
                    cols = slice(512 * THIRDS[l][c] + P * k, 512 * THIRDS[l][c] + P * k + P)
                    transposes(f"y{l}{c}", k, [mix[:, t, cols] for t in range(NT)])

            pe.wait_ge(S("consts"), 16)
            rows_t("n1", KD, lambda t: xr[:, t, :])
            project("cqkv0", "n1")
            project("cqkv1")
            rows_t("cq", 3, lambda t: cqkv[:, t, 0:384])
            project("uq0", "cq")
            project("uq1")
            rows_t("ckv", 2, lambda t: cqkv[:, t, 384:640])
            project("uv", "ckv")
            project("uk")
            for h in range(H8):
                pe.wait_ge(S("qa_rot"), h // 4 + 1)
                transposes("qa", h, [qk_tok[:, t, h, :] for t in range(NT)])
            read_all("uk")
            pe.wait_ge(S("ka_rot"), NT)
            for h in range(H8):
                transposes("ka", h, [qk_tok[:, t, h, :] for t in range(NT)])
            wait_tp_read(pe, "ka", H8)
            read_all("uv")
            attention("mla", mla_unit, 32)
            for i in (0, 1):
                project_piece("idx0", i)
            pe.wait_ge(att_done, AU["mla"] + 32)
            for k in range(4):
                transposes("oa", k, [o_tok[:, t, P * k:P * k + P] for t in range(NT)])
            project_piece("idx0", 2)
            end_phase(pe, "PE")

            project_piece("idx0", 3)
            for name in ("idx1", "qkvb0", "qkvb1", "qkvb2"):
                project(name)
            pe.wait_ge(S("b_rot"), 1)
            for i in range(4):
                transposes("qi", i, [idx[:, t, P * i:P * i + P] for t in range(NT)])
            transposes("ki", 0, [kidup[:, t, :] for t in range(NT)])
            pe.wait_ge(S("b_rot"), 2)
            for i in range(8):
                transposes("qkb", i, [qkvb[:, t, P * i:P * i + P] for t in range(NT)])
            wait_tp_read(pe, "qkb", 8)
            wait_tp_read(pe, "qi", 4)
            wait_tp_read(pe, "ki", 1)
            for n in range(24):
                qt, h = 1 + n // 8, n % 8
                r0 = 64 * (h % 2)
                kw = P * (qt + 1)
                if n >= 2:
                    pe.wait_ge(S("idx_relu"), n - 1)
                pe.matmul(SC[n % 2][:, 0:kw], qiT[r0:r0 + 64, h // 2, qt * P:qt * P + P], kiT[r0:r0 + 64, 0:kw],
                          start=True, stop=True).then_inc(S("idx_mm"), 1)
            for name in ("ga0", "ga1", "oa0", "oa1", "gb0"):
                project(name)
            pe.wait_ge(S("idx_relu"), 24)
            read_all("gb0")
            attention("dsa", dsa_unit, 32)
            project("gb1")
            pe.wait_ge(att_done, AU["dsa"] + 32)
            for k in range(4):
                transposes("ob", k, [o_tokb[:, t, P * k:P * k + P] for t in range(NT)])
            project("ob0", "ob")
            project("ob1")
            pe.wait_ge(S("y_sum"), 2 * NT)
            for k in range(KD):
                transposes("y", k, [y1[:, t, P * k:P * k + P] for t in range(NT)])
            project("out0", "y")
            project("out1")

            pe.wait_ge(norm_xs, so_far("ffn", 2, NT))
            for k in range(KD):
                transposes("h2", k, [bigt[:, t, P * k:P * k + P] for t in range(NT)])
            wait_tp_read(pe, "h2", KD)
            pe.wait_ge(S("moe_in"), 96)
            read_all("out1")
            for t in range(NT):
                for k in range(KD):
                    mm = pe.matmul(ACC[0][:, 40 * t:40 * t + 40], h2T[:, k, t * P:t * P + P], w_rt[:, k, :],
                                   start=k == 0, stop=k == KD - 1)
            mm.then_inc(S("rt_mm"), 1)
            pe.wait_ge(S("rt_oneh"), 1)
            for t in range(NT):
                for b in range(t + 1):
                    mm = pe.matmul(ACC[1][:, 8 * t:8 * t + 8], before if b == t else ones, oneh[:, b, :],
                                   start=b == 0, stop=b == t)
            mm.then_inc(S("rank_mm"), 1)
            pe.wait_ge(S("rt_over"), 1)
            pe.matmul(ACC[1][:, 64:64 + NT], ones, r_over, start=True, stop=True).then_inc(S("over_mm"), 1)
            pe.wait_ge(S("key_b"), 1)
            for t in range(NT):
                mm = pe.matmul(ACC[2][:, t * P:t * P + P], keyb[:, t, :], ident, start=True, stop=True)
            mm.then_inc(S("key_mm"), 1)
            pe.wait_ge(S("xs_lo"), NT)
            pe.wait_ge(S("key_row"), 1)
            def piece(g, what):
                p = P_MOE + piece_of[what]
                pe.wait_ge(lo_done[p % SPL], g * (PPG // SPL) + (p // SPL + 1))
                return p % SPL

            def gather(g, i):
                pe.wait_ge(tp_free[i], g + (TPU["moe"] // 2))
                for k in range(4):
                    n = 0
                    cols = slice((4 * i + k) * P, (4 * i + k) * P + P)
                    for part in (xs_hi, xs_lo):
                        for t in range(NT):
                            mm = pe.matmul(TP[i][:, k * P:k * P + P], part[:, t, cols], pick[:, t, :], start=n == 0, stop=n == 7)
                            n += 1
                mm.then_inc(tp_ready, 1)

            def slot_weights(g):
                for t in range(NT):
                    mm = pe.matmul(ACC[1][:, 0:2 * EPG], pick[:, t, :], comb_s[:, t, :], start=t == 0, stop=t == NT - 1)
                mm.then_inc(S("ws_mm"), 1)

            def gate_up(g, e, qs):
                for q in qs:
                    s = piece(g, ("gu", e, q))
                    if q == 0:
                        pe.wait_ge(S("hid_done"), g * EPG + (e + 1))
                    if e == 1 and q == 0:
                        pe.wait_ge(S("ws_read"), g + 1)
                    if e == 0 and q % 2 == 0:
                        pe.wait_ge(tp_free[q // 2], g + (TPU["moe"] // 2 + 1))
                    for kk in range(2):
                        k = 2 * q + kk
                        bh, bl = (w[:, s, kk * 512:kk * 512 + 512] for w in (whi, wlo))
                        for n, (a, b) in enumerate(PASSES(xg_hi[:, k, :], xg_lo[:, k, :], bh, bl)):
                            mm = pe.matmul(ACC[e % 2], a, b, start=k == 0 and n == 0, stop=k == 7 and n == 2)
                    mm.then_inc(piece_used, 1)

            def hidden_t(g, e):
                if e == 0:
                    pe.wait_ge(S("sc_free"), g * 8 + 2)
                pe.wait_ge(S("hid_done"), g * EPG + (e + 3))
                for b in range(2):
                    tr = pe.transpose(SC[e % 2][:, b * P:b * P + P], hid_sb[e % 2][:, b * P:b * P + P], ident)
                tr.then_inc(S("hd_t"), 1)

            def down(g, e):
                for b in range(2):
                    s = piece(g, ("dn", e, b))
                    if b == 0:
                        pe.wait_ge(S("hd_split"), g * EPG + (e + 1))
                    for n in range(2):
                        if e == 0 and b == 0:
                            pe.wait_ge(S("y_done"), g * 2 + (n + 1))
                        bh, bl = (w[:, s, 512 * n:512 * n + 512] for w in (whi, wlo))
                        for q, (x, y) in enumerate(PASSES(hd_hi[e % 2][:, b * P:b * P + P], hd_lo[e % 2][:, b * P:b * P + P], bh, bl)):
                            mm = pe.matmul(ACC[2 + n], x, y, start=e == 0 and b == 0 and q == 0, stop=e == 3 and b == 1 and q == 2)
                    mm.then_inc(piece_used, 1)

            def scatter(g, tiles):
                for i in tiles:
                    t, n = i // 2, i % 2
                    if i == 0:
                        pe.wait_ge(S("put"), g + 1)
                    if i < 2:
                        pe.wait_ge(S("y_done"), g * 2 + (i + 3))
                    pe.wait_ge(S("sc_free"), g * 8 + (i + 1))
                    for q, y in enumerate((y_hi, y_lo)):
                        mm = pe.matmul(SC[i % 2], put[:, t * P:t * P + P], y[:, 512 * n:512 * n + 512], start=q == 0, stop=q == 1)
                    mm.then_inc(S("sc_ready"), 1)

            def group(g, last):
                for e in (1, 2, 3):
                    gate_up(g, e, (0, 1))
                    hidden_t(g, e - 1)
                    gate_up(g, e, (2, 3))
                    if e < 3:
                        down(g, e - 1)
                if not last:
                    pe.wait_ge(S("pick"), g + 2)
                    gather(g + 1, 0)
                down(g, 2)
                hidden_t(g, 3)
                if not last:
                    gather(g + 1, 1)
                    slot_weights(g + 1)
                down(g, 3)
                if last:
                    scatter(g, range(8))
                    return
                gate_up(g + 1, 0, (0, 1))
                scatter(g, (0, 1))
                gate_up(g + 1, 0, (2,))
                scatter(g, (2, 3))
                gate_up(g + 1, 0, (3,))
                scatter(g, (4, 5, 6, 7))

            pe.wait_ge(S("pick"), 1)
            gather(0, 0)
            gather(0, 1)
            pe.wait_ge(S("comb_lo"), 1)
            slot_weights(0)
            gate_up(0, 0, range(4))
            with pe.Fori(0, NGRP - 1) as g:
                group(g, False)
            group(NGRP - 1, True)
            pe.wait_ge(S("sc_free"), 8 * NGRP + 2)
            pe.sem_inc(S("moe_end"), 1)
            pe.wait_ge(S("flag_in"), 1)
            with pe.If(pe.value_load(flag[0:1, 0:1], min_val=0, max_val=T) > 0):
                with pe.Fori(0, NGRP * EPG) as e:
                    pe.wait_ge(S("gen_in"), e * 48 + 48)
                    for f in range(2):
                        for w in range(2):
                            for k in range(KD):
                                mm = pe.matmul(ACC[2 * w + f], gen_gu[:, w, k, f * P:f * P + P], h2T[:, k, :],
                                               start=k == 0, stop=k == KD - 1)
                    mm.then_inc(S("gen_gu"), 1)
                    pe.wait_ge(S("gen_hid"), e + 2)
                    for i in range(2 * NT):
                        t, n = i // 2, i % 2
                        pe.wait_ge(S("gen_add"), e * 8 + (i + 1))
                        for f in range(2):
                            mm = pe.matmul(SC[i % 2], gen_hid[:, f, t * P:t * P + P], gen_d[:, f, 512 * n:512 * n + 512],
                                           start=f == 0, stop=f == 1)
                        mm.then_inc(S("gen_y"), 1)
            end_phase(pe, "PE")

            memory_t(0)
            memory_stage(0, lambda t: x1[:, t, :])
            end_phase(pe, "PE")
            for hd in range(9):
                for i in range(12):
                    step, r = attention_step(i)
                    if hd:
                        u = dil_unit(hd - 1, r)
                        U, name = u["U"], f"da{r}_{hd - 1}"
                        if step == "scores":
                            if r == 0:
                                wait_tp_read(pe, f"dk_{hd - 1}", 3)
                                read_all(f"vd{hd - 1}")
                            if U > AU["dil"]:
                                pe.wait_ge(att_done, U)
                            for dst, q, k, _, _ in u["s"]:
                                mm = pe.matmul(dst[:, 0:k.shape[1]], q, k, start=True, stop=True)
                            mm.then_inc(att_s, 1)
                        elif step == "probs":
                            pe.wait_ge(att_p, U + 1)
                            transposes(name, 0, [d_s[:, P * b:P * b + P] for b in range(4)])
                            transposes(name, 1, [d_s[:, P * b:P * b + P] for b in (4, 5)])
                        else:
                            wait_tp_read(pe, name, 2)
                            for b, v in enumerate(u["v"]):
                                mm = pe.matmul(D_OUT, d_pt[:, P * b:P * b + P], v, start=b == 0, stop=b == 5)
                            mm.then_inc(att_o, 1)
                    if hd == 8:
                        project_piece(f"gate0{THIRDS[0][i // 4]}", i % 4)
                        if i == 6:
                            gated_t(0, 0)
                        continue
                    project_piece(f"{'qkv'[i // 4]}d{hd}", i % 4)
                    if i in (6, 10):
                        pe.wait_ge(S("qk_rot"), 2 * hd + (i == 10) + 1)
                        for g in range(3):
                            transposes(f"dq_{hd}" if i == 6 else f"dk_{hd}", g, [qk_t[:, t, P * g:P * g + P] for t in range(NT)])
            end_phase(pe, "PE")
            gated_t(0, 1)
            gated_t(0, 2)
            project("fin00", [TPU[f"y0{c}"] + k for c in range(3) for k in range(4)])
            for i in range(6):
                if i == 4:
                    memory_t(1)
                project_piece("fin01", i)
            memory_stage(1, lambda t: n3x[:, t, :])
            end_phase(pe, "PE")

            for hh in range(2):
                if hh:
                    pe.wait_ge(S("gl_od"), 4)
                project(f"ql{hh}")
                for nm, following in (("q", "f"), ("f", "v")):
                    project_piece(f"{following}l{hh}", 0)
                    read_all(f"{nm}l{hh}")
                    for i in range(4):
                        transposes(f"{nm}l{hh}", i, [l_tok[:, t, P * i:P * i + P] for t in range(NT)])
                    for i in (1, 2, 3):
                        if hh and nm == "f" and i == 3:
                            gated_t(1, 0)
                        project_piece(f"{following}l{hh}", i)
                read_all(f"vl{hh}")
                pe.wait_ge(S("lf_in"), hh + 1)
                wait_tp_read(pe, "y10" if hh else "fl0", 4)
                gates = {m: step for m, *step in gate_steps(hh)}
                for h in range(4):
                    H = 4 * hh + h
                    for i in range(10):
                        m = 10 * H + i
                        if m >= 2:
                            pe.wait_ge(S("gl_c"), m - 1)
                        if i == 0:
                            k, q = lk[:, h, :], lq[:, h, :]
                        else:
                            n = 9 * H + i - 1
                            pe.wait_ge(S("gl_k"), n + 1)
                            pe.wait_ge(S("gl_q"), n + 1)
                            k = q = kq[n % 5]
                        tile = lambda a, t: a[:, t * P:t * P + P]
                        if i == 0:
                            blocks = [(t * P, t, q[:, t * P:t * P + P]) for t in range(NT)]
                        elif i <= 7:
                            blocks = [(t * 64, t, halves(q[:, t * P:t * P + P], 1 << i - 1)[1]) for t in range(NT)]
                        elif i == 8:
                            blocks = [(t * P, t - 1, q[:, t * P:t * P + P]) for t in (1, 3)]
                        else:
                            blocks = [(2 * P * s, s, q[:, 2 * P:4 * P]) for s in range(2)]
                        for c0, s, rhs in blocks:
                            dst = SC[m % 2][:, c0:c0 + int(np.prod(rhs.shape[1:]))]
                            if len(rhs.shape) == 3:
                                dst = dst.rearrange("p (n c) -> p n c", c=rhs.shape[2])
                            mm = pe.matmul(dst, tile(k, s), rhs, start=True, stop=True)
                        mm.then_inc(S("gl_mm"), 1)
                        if 10 * h + i in gates:
                            project_tile(*gates[10 * h + i])
                    pe.wait_ge(S("gl_c"), 10 * H + 10)
                    if H >= 2:
                        pe.wait_ge(S("gl_od"), H - 1)
                    for t in range(NT):
                        for s in range(t + 1):
                            mm = pe.matmul(TP[H % 2][:, t * P:t * P + P], lA[:, s, t * P:t * P + P], lv[:, s, P * h:P * h + P],
                                           start=s == 0, stop=s == t)
                    mm.then_inc(S("gl_o"), 1)
            for i in range(6):
                c = i // 2
                if i == 2:
                    pe.wait_ge(S("gl_od"), 8)
                if i in (2, 4):
                    gated_t(1, c)
                    wait_tp_read(pe, f"y1{c}", 4)
                project_piece("fin10", i)
            project("fin11")


def kernel(x, norm_mix_g, w_in, mla_q_norm_g, w_uq, mla_kv_norm_g, w_uk, w_uv, w_o_a, w_o_b, w_out,
           norm_ffn_g, w_router_group, b_router_group, w_router_expert, b_router_expert, w_gate, w_up,
           w_down, final_norm_g, mem_2, positions_2, norm_gain_2, w_in_a_2, q_gain_a_2, k_gain_a_2,
           w_out_a_2, w_in_b_2, lb_logits_2, o_gain_b_2, w_out_b_2, mem_norm_gain_2, w_mem_kv_2,
           mem_q_gain_2, mem_k_gain_2):
    import concourse.bacc as bacc
    from concourse.bass_utils import run_bass_kernel_spmd

    arrays = dict(
        x=x, norm_mix_g=norm_mix_g, w_in=w_in, mla_q_norm_g=mla_q_norm_g, w_uq=w_uq, mla_kv_norm_g=mla_kv_norm_g,
        w_uk=w_uk, w_uv=w_uv, w_o_a=w_o_a, w_o_b=w_o_b, w_out=w_out, norm_ffn_g=norm_ffn_g,
        w_router_group=w_router_group, b_router_group=b_router_group, w_router_expert=w_router_expert,
        b_router_expert=b_router_expert, w_gate=w_gate, w_up=w_up, w_down=w_down, final_norm_g=final_norm_g,
        mem_2=mem_2, positions_2=positions_2, norm_gain_2=norm_gain_2, w_in_a_2=w_in_a_2, q_gain_a_2=q_gain_a_2,
        k_gain_a_2=k_gain_a_2, w_out_a_2=w_out_a_2, w_in_b_2=w_in_b_2, lb_logits_2=lb_logits_2, o_gain_b_2=o_gain_b_2,
        w_out_b_2=w_out_b_2, mem_norm_gain_2=mem_norm_gain_2, w_mem_kv_2=w_mem_kv_2, mem_q_gain_2=mem_q_gain_2,
        mem_k_gain_2=mem_k_gain_2)
    arrays = {name: np.ascontiguousarray(a) for name, a in arrays.items()}
    arrays["const"] = CONST
    nc = bacc.Bacc("TRN2", target_bir_lowering=False, num_devices=1)
    aps = {name: nc.dram_tensor(name, a.shape, mybir.dt.from_np(a.dtype), kind="ExternalInput").ap()
           for name, a in arrays.items()}
    out = nc.dram_tensor("out", (1, T, D), F32, kind="ExternalOutput").ap()
    build(nc, aps, out)
    return run_bass_kernel_spmd(nc, [arrays], core_ids=[0]).results[0]["out"]
```
